# Optimizing a Trainium2 kernel written in Bass

```python
import math
import jax
import jax.numpy as jnp
from jax import lax
import numpy as np

D_MODEL = 1024
BATCH = 1
SEQ = 512
DEPTH = 2

HEAD_DIM = 64
GROUP_HEADS = 4
GROUP_W = GROUP_HEADS * HEAD_DIM
N_GROUPS = 4
D_MIX = N_GROUPS * GROUP_W
NORM_EPS = 1e-6
NEG = -1e30
Q_BLOCK = 128

CMP_LEN = 32
CMP_STRIDE = 16
SEL_LEN = 64
SEL_TOPN = 16
WINDOW = 512
N_CMP_IN_SEL = (SEL_LEN - CMP_LEN) // CMP_STRIDE + 1
SEL_FORCE = 1e3
N_BUCKETS = 32
MAX_DISTANCE = 128

MLSTM_CHUNK = 64
GDN_CHUNK = 64
CONV_W = 4

Q_LORA = 256
KV_LORA = 128
QK_NOPE = 64
QK_ROPE = 32
V_HEAD = 64
ROPE_THETA = 10000.0

PEER_HEADS = 8
PEER_DK = 256
N_KEYS = 128
N_EXPERTS = N_KEYS * N_KEYS
PEER_TOPK = 16
PEER_CHUNK = 128

NSA_IN = GROUP_W + 6 * HEAD_DIM + 3 * GROUP_HEADS
MLSTM_IN = 4 * GROUP_W + 2 * GROUP_HEADS
GDN_IN = 4 * GROUP_W + 2 * GROUP_HEADS
MLA_IN = Q_LORA + KV_LORA + QK_ROPE
D_IN = NSA_IN + MLSTM_IN + GDN_IN + MLA_IN

kernel_name = 'hybrid_nsa_mlstm_gdn_mla_peer'

def _split(t, widths):
    outs = []
    start = 0
    for w in widths:
        outs.append(t[..., start:start + w])
        start += w
    return outs

def rms_norm(x, g):
    xf = x.astype(jnp.float32)
    y = xf * lax.rsqrt(jnp.mean(xf * xf, axis=-1, keepdims=True) + NORM_EPS)
    return (y * g.astype(jnp.float32)).astype(x.dtype)

def _heads(t):
    b, s, _ = t.shape
    return t.reshape(b, s, -1, HEAD_DIM).transpose(0, 2, 1, 3)

def _unheads(t):
    b, h, s, d = t.shape
    return t.transpose(0, 2, 1, 3).reshape(b, s, h * d)

def _chunk(t, size):
    sh = t.shape
    return t.reshape(sh[0], sh[1], sh[2] // size, size, *sh[3:])

def masked_softmax(s, mask):
    s = jnp.where(mask, s.astype(jnp.float32), NEG)
    p = jax.nn.softmax(s, axis=-1)
    return jnp.where(mask, p, 0.0)

def t5_bucket(dist):
    dist = jnp.maximum(dist, 0)
    max_exact = N_BUCKETS // 2
    d = jnp.maximum(dist, 1).astype(jnp.float32)
    large = max_exact + (jnp.log(d / max_exact) / math.log(MAX_DISTANCE / max_exact)
                         * (N_BUCKETS - max_exact)).astype(jnp.int32)
    large = jnp.minimum(large, N_BUCKETS - 1)
    return jnp.where(dist < max_exact, dist, large)

def t5_bias(dist, table, head_axis):
    return jnp.moveaxis(table[t5_bucket(dist)].astype(jnp.float32), -1, head_axis)

def apply_rope(t, cos, sin):
    t1, t2 = t[..., :QK_ROPE // 2], t[..., QK_ROPE // 2:]
    return jnp.concatenate([t1 * cos - t2 * sin, t2 * cos + t1 * sin], axis=-1)

def causal_conv(t, w):
    c = t.shape[-1]
    return lax.conv_general_dilated(t, w[:, None, :].astype(t.dtype), window_strides=(1,),
                                    padding=[(CONV_W - 1, 0)],
                                    dimension_numbers=('NWC', 'WIO', 'NWC'),
                                    feature_group_count=c)

def nsa_group(h, w_cmp_k, w_cmp_v, cmp_pos, t5_table):
    f32 = jnp.float32
    b, s, _ = h.shape
    q, kc, vc, ks, vs, kw, vw, gates = _split(h, (GROUP_W,) + (HEAD_DIM,) * 6 + (3 * GROUP_HEADS,))
    qh = _heads(q).astype(f32) * HEAD_DIM ** -0.5

    n_cmp = (s - CMP_LEN) // CMP_STRIDE + 1

    def compress(t, w):
        tr = t.reshape(b, s // CMP_STRIDE, CMP_STRIDE, HEAD_DIM)
        blocks = jnp.concatenate([tr[:, :-1], tr[:, 1:]], axis=2) + cmp_pos
        return (blocks.reshape(b, n_cmp, CMP_LEN * HEAD_DIM) @ w).astype(f32)

    k_cmp = compress(kc, w_cmp_k)
    v_cmp = compress(vc, w_cmp_v)
    cmp_end = jnp.arange(n_cmp) * CMP_STRIDE + CMP_LEN - 1

    n_sel = s // SEL_LEN
    top_n = min(SEL_TOPN, n_sel)
    ks_blk = ks.astype(f32).reshape(b, n_sel, SEL_LEN, HEAD_DIM)
    vs_blk = vs.astype(f32).reshape(b, n_sel, SEL_LEN, HEAD_DIM)
    sel_blk = jnp.arange(n_sel)
    n_pad = n_sel * (SEL_LEN // CMP_STRIDE) - n_cmp

    kw_pad = jnp.pad(kw.astype(f32), ((0, 0), (WINDOW, 0), (0, 0)))
    vw_pad = jnp.pad(vw.astype(f32), ((0, 0), (WINDOW, 0), (0, 0)))

    nb = s // Q_BLOCK
    q_blocks = jnp.moveaxis(qh.reshape(b, GROUP_HEADS, nb, Q_BLOCK, HEAD_DIM), 2, 0)

    def block(args):
        qb, bi = args
        t = bi * Q_BLOCK + jnp.arange(Q_BLOCK)
        dist_c = t[:, None] - cmp_end[None, :]
        s_c = jnp.einsum('bhqd,bnd->bhqn', qb, k_cmp) + t5_bias(dist_c, t5_table, 0)
        p_c = masked_softmax(s_c, dist_c >= 0)
        o_c = jnp.einsum('bhqn,bnd->bhqd', p_c, v_cmp)
        imp = jnp.pad(p_c.sum(axis=1), ((0, 0), (0, 0), (0, n_pad)))
        imp = imp.reshape(b, Q_BLOCK, n_sel, SEL_LEN // CMP_STRIDE)[..., :N_CMP_IN_SEL].sum(-1)
        cur = t // SEL_LEN
        forced = ((sel_blk[None, :] == 0) | (sel_blk[None, :] == cur[:, None])
                  | (sel_blk[None, :] == cur[:, None] - 1))
        score = jnp.where(sel_blk[None, :] <= cur[:, None],
                          imp + jnp.where(forced, SEL_FORCE, 0.0), NEG)
        top_s, idx = lax.top_k(score, top_n)
        kg = jax.vmap(lambda kb_, ib_: kb_[ib_])(ks_blk, idx)
        vg = jax.vmap(lambda vb_, ib_: vb_[ib_])(vs_blk, idx)
        tok = idx[..., None] * SEL_LEN + jnp.arange(SEL_LEN)
        dist_s = t[None, :, None, None] - tok
        m_s = (top_s > 0.5 * NEG)[..., None] & (dist_s >= 0)
        s_s = jnp.einsum('bhqd,bqnld->bhqnl', qb, kg) + t5_bias(dist_s, t5_table, 1)
        p_s = masked_softmax(s_s.reshape(b, GROUP_HEADS, Q_BLOCK, top_n * SEL_LEN),
                             m_s.reshape(b, 1, Q_BLOCK, top_n * SEL_LEN))
        o_s = jnp.einsum('bhqnl,bqnld->bhqd', p_s.reshape(s_s.shape), vg)
        kwb = lax.dynamic_slice_in_dim(kw_pad, bi * Q_BLOCK, Q_BLOCK + WINDOW, axis=1)
        vwb = lax.dynamic_slice_in_dim(vw_pad, bi * Q_BLOCK, Q_BLOCK + WINDOW, axis=1)
        src = bi * Q_BLOCK - WINDOW + jnp.arange(Q_BLOCK + WINDOW)
        dist_w = t[:, None] - src[None, :]
        m_w = (dist_w >= 0) & (dist_w < WINDOW) & (src[None, :] >= 0)
        s_w = jnp.einsum('bhqd,bkd->bhqk', qb, kwb) + t5_bias(dist_w, t5_table, 0)
        o_w = jnp.einsum('bhqk,bkd->bhqd', masked_softmax(s_w, m_w), vwb)
        return jnp.stack([o_c, o_s, o_w], axis=0)

    outs = lax.map(block, (q_blocks, jnp.arange(nb)))
    outs = outs.transpose(1, 2, 3, 0, 4, 5).reshape(3, b, GROUP_HEADS, s, HEAD_DIM)
    g = jax.nn.sigmoid(gates.astype(f32)).reshape(b, s, 3, GROUP_HEADS).transpose(2, 0, 3, 1)
    return _unheads((g[..., None] * outs).sum(0))

def mlstm_group(h, i_bias, f_bias, norm_g):
    f32 = jnp.float32
    b, s, _ = h.shape
    q, k, v, ig, fg, og = _split(h, (GROUP_W,) * 3 + (GROUP_HEADS, GROUP_HEADS, GROUP_W))
    qh = _heads(q).astype(f32)
    kh = _heads(k).astype(f32) * HEAD_DIM ** -0.5
    vh = _heads(v).astype(f32)
    i_pre = (ig + i_bias).astype(f32).transpose(0, 2, 1)
    log_f = jax.nn.log_sigmoid((fg + f_bias).astype(f32)).transpose(0, 2, 1)
    L = MLSTM_CHUNK
    tri = jnp.tril(jnp.ones((L, L), dtype=bool))

    def step(carry, xs):
        c_st, n_st, m_st = carry
        qc, kc, vc, ic, lf = xs
        bcum = jnp.cumsum(lf, axis=-1)
        log_d = jnp.where(tri, bcum[..., :, None] - bcum[..., None, :] + ic[..., None, :], -jnp.inf)
        m_inter = bcum + m_st[..., None]
        m_t = jnp.maximum(log_d.max(-1), m_inter)
        dmat = jnp.exp(log_d - m_t[..., None])
        inter = jnp.exp(m_inter - m_t)
        sqk = jnp.einsum('bhtd,bhsd->bhts', qc, kc) * dmat
        num = (jnp.einsum('bhts,bhse->bhte', sqk, vc)
               + inter[..., None] * jnp.einsum('bhek,bhtk->bhte', c_st, qc))
        den = sqk.sum(-1) + inter * jnp.einsum('bhk,bhtk->bht', n_st, qc)
        h_t = num / jnp.maximum(jnp.abs(den), jnp.exp(-m_t))[..., None]
        b_end = bcum[..., -1]
        log_w = b_end[..., None] - bcum + ic
        m_new = jnp.maximum(b_end + m_st, log_w.max(-1))
        w = jnp.exp(log_w - m_new[..., None])
        decay = jnp.exp(b_end + m_st - m_new)
        c_st = decay[..., None, None] * c_st + jnp.einsum('bhs,bhse,bhsk->bhek', w, vc, kc)
        n_st = decay[..., None] * n_st + jnp.einsum('bhs,bhsk->bhk', w, kc)
        return (c_st, n_st, m_new), h_t

    xs = (jnp.moveaxis(_chunk(qh, L), 2, 0), jnp.moveaxis(_chunk(kh, L), 2, 0),
          jnp.moveaxis(_chunk(vh, L), 2, 0), jnp.moveaxis(_chunk(i_pre, L), 2, 0),
          jnp.moveaxis(_chunk(log_f, L), 2, 0))
    init = (jnp.zeros((b, GROUP_HEADS, HEAD_DIM, HEAD_DIM), f32),
            jnp.zeros((b, GROUP_HEADS, HEAD_DIM), f32),
            jnp.zeros((b, GROUP_HEADS), f32))
    _, hs = lax.scan(step, init, xs)
    hs = jnp.moveaxis(hs, 0, 2).reshape(b, GROUP_HEADS, s, HEAD_DIM).transpose(0, 2, 1, 3)
    o = jax.nn.sigmoid(og.astype(f32)).reshape(b, s, GROUP_HEADS, HEAD_DIM)
    y = rms_norm(o * hs, norm_g.reshape(GROUP_HEADS, HEAD_DIM))
    return y.reshape(b, s, GROUP_W)

def gdn_group(h, conv_w, a_log, dt_bias, norm_g):
    f32 = jnp.float32
    b, s, _ = h.shape
    qkv, beta_pre, a_pre, z = _split(h, (3 * GROUP_W, GROUP_HEADS, GROUP_HEADS, GROUP_W))
    qkv = jax.nn.silu(causal_conv(qkv, conv_w))
    q, k, v = _split(qkv, (GROUP_W,) * 3)

    def l2n(t):
        return t * lax.rsqrt(jnp.sum(t * t, axis=-1, keepdims=True) + NORM_EPS)

    qh = l2n(_heads(q).astype(f32)) * HEAD_DIM ** -0.5
    kh = l2n(_heads(k).astype(f32))
    vh = _heads(v).astype(f32)
    beta = jax.nn.sigmoid(beta_pre.astype(f32)).transpose(0, 2, 1)
    g = (-jnp.exp(a_log.astype(f32)) * jax.nn.softplus((a_pre + dt_bias).astype(f32))).transpose(0, 2, 1)
    L = GDN_CHUNK
    qc, kc, vc = _chunk(qh, L), _chunk(kh, L), _chunk(vh, L)
    gc = jnp.cumsum(_chunk(g, L), axis=-1)
    bc = _chunk(beta, L)
    tri = jnp.tril(jnp.ones((L, L), dtype=bool))
    strict = jnp.tril(jnp.ones((L, L), dtype=bool), k=-1)
    decay = jnp.exp(jnp.where(tri, gc[..., :, None] - gc[..., None, :], -jnp.inf))
    kb = kc * bc[..., None]
    vb = vc * bc[..., None]
    a_mat = jnp.where(strict, jnp.einsum('bhnid,bhnjd->bhnij', kb, kc) * decay, 0.0)
    m_mat = a_mat + jnp.eye(L, dtype=f32)
    u = lax.linalg.triangular_solve(m_mat, vb, left_side=True, lower=True)
    w = lax.linalg.triangular_solve(m_mat, kb * jnp.exp(gc)[..., None], left_side=True, lower=True)
    attn_qk = jnp.einsum('bhnid,bhnjd->bhnij', qc, kc) * decay
    q_dec = qc * jnp.exp(gc)[..., None]
    k_dec = kc * jnp.exp(gc[..., -1:] - gc)[..., None]
    g_end = jnp.exp(gc[..., -1])

    def step(state, xs):
        qd, aqk, uc, wc, kd, ge = xs
        v_new = uc - jnp.einsum('bhlk,bhkv->bhlv', wc, state)
        o = jnp.einsum('bhlk,bhkv->bhlv', qd, state) + jnp.einsum('bhij,bhjv->bhiv', aqk, v_new)
        state = state * ge[..., None, None] + jnp.einsum('bhlk,bhlv->bhkv', kd, v_new)
        return state, o

    xs = (jnp.moveaxis(q_dec, 2, 0), jnp.moveaxis(attn_qk, 2, 0), jnp.moveaxis(u, 2, 0),
          jnp.moveaxis(w, 2, 0), jnp.moveaxis(k_dec, 2, 0), jnp.moveaxis(g_end, 2, 0))
    init = jnp.zeros((b, GROUP_HEADS, HEAD_DIM, HEAD_DIM), f32)
    _, os_ = lax.scan(step, init, xs)
    os_ = jnp.moveaxis(os_, 0, 2).reshape(b, GROUP_HEADS, s, HEAD_DIM).transpose(0, 2, 1, 3)
    zg = jax.nn.silu(z.astype(f32)).reshape(b, s, GROUP_HEADS, HEAD_DIM)
    return (rms_norm(os_, norm_g) * zg).reshape(b, s, GROUP_W)

def mla_group(h, positions, q_norm_g, kv_norm_g, w_uq, w_ukv):
    f32 = jnp.float32
    b, s, _ = h.shape
    c_q, c_kv, k_r = _split(h, (Q_LORA, KV_LORA, QK_ROPE))
    qf = (rms_norm(c_q, q_norm_g) @ w_uq).astype(f32).reshape(b, s, GROUP_HEADS, QK_NOPE + QK_ROPE)
    kvf = (rms_norm(c_kv, kv_norm_g) @ w_ukv).astype(f32).reshape(b, s, GROUP_HEADS, QK_NOPE + V_HEAD)
    inv_freq = ROPE_THETA ** (-jnp.arange(0, QK_ROPE, 2, dtype=f32) / QK_ROPE)
    ang = positions.astype(f32)[..., None] * inv_freq
    cos, sin = jnp.cos(ang), jnp.sin(ang)
    scale = (QK_NOPE + QK_ROPE) ** -0.5
    q_nope = qf[..., :QK_NOPE].transpose(0, 2, 1, 3) * scale
    q_rope = apply_rope(qf[..., QK_NOPE:], cos[:, :, None], sin[:, :, None]).transpose(0, 2, 1, 3) * scale
    k_nope = kvf[..., :QK_NOPE].transpose(0, 2, 1, 3)
    v = kvf[..., QK_NOPE:].transpose(0, 2, 1, 3)
    k_rope = apply_rope(k_r.astype(f32), cos, sin)
    nb = s // Q_BLOCK
    qn_b = jnp.moveaxis(q_nope.reshape(b, GROUP_HEADS, nb, Q_BLOCK, QK_NOPE), 2, 0)
    qr_b = jnp.moveaxis(q_rope.reshape(b, GROUP_HEADS, nb, Q_BLOCK, QK_ROPE), 2, 0)
    key_pos = jnp.arange(s)

    def block(args):
        qn, qr, bi = args
        t = bi * Q_BLOCK + jnp.arange(Q_BLOCK)
        sc = jnp.einsum('bhqd,bhkd->bhqk', qn, k_nope) + jnp.einsum('bhqr,bkr->bhqk', qr, k_rope)
        p = masked_softmax(sc, key_pos[None, :] <= t[:, None])
        return jnp.einsum('bhqk,bhkd->bhqd', p, v)

    o = lax.map(block, (qn_b, qr_b, jnp.arange(nb)))
    o = jnp.moveaxis(o, 0, 2).reshape(b, GROUP_HEADS, s, V_HEAD)
    return _unheads(o)

def hybrid_mixer(xn, positions, t5_table, w_in, w_out, nsa_w_cmp_k, nsa_w_cmp_v, nsa_cmp_pos,
                 mlstm_i_bias, mlstm_f_bias, mlstm_norm_g, gdn_conv_w, gdn_a_log, gdn_dt_bias,
                 gdn_norm_g, mla_q_norm_g, mla_kv_norm_g, mla_w_uq, mla_w_ukv):
    h = xn @ w_in
    h_nsa, h_ml, h_gdn, h_mla = _split(h, (NSA_IN, MLSTM_IN, GDN_IN, MLA_IN))
    o = jnp.concatenate([
        nsa_group(h_nsa, nsa_w_cmp_k, nsa_w_cmp_v, nsa_cmp_pos, t5_table).astype(xn.dtype),
        mlstm_group(h_ml, mlstm_i_bias, mlstm_f_bias, mlstm_norm_g).astype(xn.dtype),
        gdn_group(h_gdn, gdn_conv_w, gdn_a_log, gdn_dt_bias, gdn_norm_g).astype(xn.dtype),
        mla_group(h_mla, positions, mla_q_norm_g, mla_kv_norm_g, mla_w_uq, mla_w_ukv).astype(xn.dtype),
    ], axis=-1)
    return o @ w_out

def peer_ffn(xn, w_q, sub_keys, u_tab, v_tab):
    b, s, d = xn.shape
    half = PEER_DK // 2
    xt = xn.reshape(b * s // PEER_CHUNK, PEER_CHUNK, d)

    def chunk(xc):
        qh = (xc @ w_q).reshape(PEER_CHUNK, PEER_HEADS, 2, half)
        sc = jnp.einsum('tpcd,pcnd->tpcn', qh, sub_keys).astype(jnp.float32)
        s1, i1 = lax.top_k(sc[:, :, 0], PEER_TOPK)
        s2, i2 = lax.top_k(sc[:, :, 1], PEER_TOPK)
        cand = (s1[..., :, None] + s2[..., None, :]).reshape(PEER_CHUNK, PEER_HEADS, PEER_TOPK * PEER_TOPK)
        cidx = (i1[..., :, None] * N_KEYS + i2[..., None, :]).reshape(PEER_CHUNK, PEER_HEADS, PEER_TOPK * PEER_TOPK)
        top, pos = lax.top_k(cand, PEER_TOPK)
        eidx = jnp.take_along_axis(cidx, pos, axis=-1)
        gate = jax.nn.softmax(top, axis=-1)
        u = u_tab[eidx]
        v = v_tab[eidx]
        act = jax.nn.gelu(jnp.einsum('td,tpkd->tpk', xc, u).astype(jnp.float32), approximate=False)
        return jnp.einsum('tpk,tpkd->td', (gate * act).astype(xc.dtype), v)

    return lax.map(chunk, xt).reshape(b, s, d)

def setup_inputs(seed: int = 0) -> dict:
    key = jax.random.key(seed)
    ks = jax.random.split(key, 32)
    f32 = jnp.float32

    def nrm(k, shape, scale):
        return jax.random.normal(k, shape, f32) * scale

    dt = jnp.exp(jax.random.uniform(ks[16], (DEPTH, GROUP_HEADS), f32)
                 * (math.log(0.1) - math.log(0.001)) + math.log(0.001))
    return {
        'x': nrm(ks[0], (BATCH, SEQ, D_MODEL), 1.0),
        'positions': jnp.tile(jnp.arange(SEQ, dtype=jnp.int32)[None, :], (BATCH, 1)),
        't5_table': nrm(ks[1], (N_BUCKETS, GROUP_HEADS), 0.5),
        'norm1_g': 1.0 + nrm(ks[2], (DEPTH, D_MODEL), 0.02),
        'norm2_g': 1.0 + nrm(ks[3], (DEPTH, D_MODEL), 0.02),
        'final_norm_g': 1.0 + nrm(ks[4], (D_MODEL,), 0.02),
        'w_in': nrm(ks[5], (DEPTH, D_MODEL, D_IN), D_MODEL ** -0.5),
        'w_out': nrm(ks[6], (DEPTH, D_MIX, D_MODEL), D_MIX ** -0.5),
        'nsa_w_cmp_k': nrm(ks[7], (DEPTH, CMP_LEN * HEAD_DIM, HEAD_DIM), (CMP_LEN * HEAD_DIM) ** -0.5),
        'nsa_w_cmp_v': nrm(ks[8], (DEPTH, CMP_LEN * HEAD_DIM, HEAD_DIM), (CMP_LEN * HEAD_DIM) ** -0.5),
        'nsa_cmp_pos': nrm(ks[9], (DEPTH, CMP_LEN, HEAD_DIM), 0.1),
        'mlstm_i_bias': nrm(ks[10], (DEPTH, GROUP_HEADS), 0.1),
        'mlstm_f_bias': jnp.linspace(3.0, 6.0, GROUP_HEADS, dtype=f32)[None, :] + nrm(ks[11], (DEPTH, GROUP_HEADS), 0.1),
        'mlstm_norm_g': 1.0 + nrm(ks[12], (DEPTH, GROUP_W), 0.02),
        'gdn_conv_w': nrm(ks[13], (DEPTH, CONV_W, 3 * GROUP_W), CONV_W ** -0.5),
        'gdn_a_log': jnp.log(jax.random.uniform(ks[14], (DEPTH, GROUP_HEADS), f32, 1.0, 16.0)),
        'gdn_dt_bias': dt + jnp.log(-jnp.expm1(-dt)),
        'gdn_norm_g': 1.0 + nrm(ks[15], (DEPTH, HEAD_DIM), 0.02),
        'mla_q_norm_g': 1.0 + nrm(ks[17], (DEPTH, Q_LORA), 0.02),
        'mla_kv_norm_g': 1.0 + nrm(ks[18], (DEPTH, KV_LORA), 0.02),
        'mla_w_uq': nrm(ks[19], (DEPTH, Q_LORA, GROUP_HEADS * (QK_NOPE + QK_ROPE)), Q_LORA ** -0.5),
        'mla_w_ukv': nrm(ks[20], (DEPTH, KV_LORA, GROUP_HEADS * (QK_NOPE + V_HEAD)), KV_LORA ** -0.5),
        'peer_w_q': nrm(ks[21], (DEPTH, D_MODEL, PEER_HEADS * PEER_DK), D_MODEL ** -0.5),
        'peer_sub_keys': nrm(ks[22], (DEPTH, PEER_HEADS, 2, N_KEYS, PEER_DK // 2), (PEER_DK // 2) ** -0.5),
        'peer_u': nrm(ks[23], (DEPTH, N_EXPERTS, D_MODEL), D_MODEL ** -0.5),
        'peer_v': nrm(ks[24], (DEPTH, N_EXPERTS, D_MODEL), 0.2),
    }

def reference(x, positions, t5_table, norm1_g, norm2_g, final_norm_g, w_in, w_out,
              nsa_w_cmp_k, nsa_w_cmp_v, nsa_cmp_pos, mlstm_i_bias, mlstm_f_bias, mlstm_norm_g,
              gdn_conv_w, gdn_a_log, gdn_dt_bias, gdn_norm_g, mla_q_norm_g, mla_kv_norm_g,
              mla_w_uq, mla_w_ukv, peer_w_q, peer_sub_keys, peer_u, peer_v):
    h = x
    for l in range(DEPTH):
        xn = rms_norm(h, norm1_g[l])
        h = h + hybrid_mixer(xn, positions, t5_table, w_in[l], w_out[l], nsa_w_cmp_k[l],
                             nsa_w_cmp_v[l], nsa_cmp_pos[l], mlstm_i_bias[l], mlstm_f_bias[l],
                             mlstm_norm_g[l], gdn_conv_w[l], gdn_a_log[l], gdn_dt_bias[l],
                             gdn_norm_g[l], mla_q_norm_g[l], mla_kv_norm_g[l], mla_w_uq[l],
                             mla_w_ukv[l])
        h = h + peer_ffn(rms_norm(h, norm2_g[l]), peer_w_q[l], peer_sub_keys[l], peer_u[l], peer_v[l])
    return rms_norm(h, final_norm_g)


_drawn_inputs = setup_inputs


def setup_inputs(seed=0):
    import zlib

    import numpy as np

    out = dict(_drawn_inputs(seed))
    spreads = {}
    factors = {'norm2_g': 2.73,
     'final_norm_g': 2.869,
     'mlstm_i_bias': 8.0,
     'gdn_norm_g': 3.896,
     'mla_q_norm_g': 7.526,
     'mla_kv_norm_g': 6.036}
    for name, (base, spread) in spreads.items():
        noise = np.random.default_rng([zlib.crc32(name.encode()), seed]).standard_normal(out[name].shape)
        drawn = base * np.exp(spread * noise) if base else spread * noise
        out[name] = jnp.asarray(drawn.astype(out[name].dtype))
    for name, factor in factors.items():
        out[name] = (out[name] * factor).astype(out[name].dtype)
    return out
```

```python
import math
from contextlib import ExitStack

import concourse.bass as bass
import numpy as np
from concourse import mybir

F32 = mybir.dt.float32
I32 = mybir.dt.int32
U32 = mybir.dt.uint32
ALU = mybir.AluOpType
ACT = mybir.ActivationFunctionType
AX = mybir.AxisListType

P = 128
D_MODEL, SEQ, DEPTH = 1024, 512, 2
NT = SEQ // P
KD = D_MODEL // P
HD, NH, GW = 64, 4, 256
EPS = 1e-6
NEG = -1e30
CMP_LEN, CMP_STRIDE = 32, 16
N_CMP = (SEQ - CMP_LEN) // CMP_STRIDE + 1
N_BUCKETS, MAX_DISTANCE = 32, 128
Q_LORA, KV_LORA, NOPE, ROPE = 256, 128, 64, 32
QD = NOPE + ROPE
CONV_W = 4
PH, PDK, NK, TOPK = 8, 256, 128, 16
N_EXPERTS = NK * NK

NSA_IN = GW + 6 * HD + 3 * NH
ML_IN = 4 * GW + 2 * NH
MLA_IN = Q_LORA + KV_LORA + ROPE
ML_BASE = NSA_IN
GDN_BASE = ML_BASE + ML_IN
MLA_BASE = GDN_BASE + ML_IN
BANK = 512

CONST_COLS = {}


def shape_constants():
    p = np.arange(P)[:, None]
    c = np.arange(P)[None, :]
    y = np.arange(SEQ)[None, :]
    parts = [
        ("ident", p == c),
        ("iota", np.broadcast_to(c, (P, P))),
        ("headones", p // HD == c // HD),
        ("maskq", np.where(p + SEQ - P - y >= 0, 0.0, NEG)),
        ("mask_strict", np.where(p > c, 0.0, NEG)),
        ("mask_t", np.where(c >= p, 0.0, NEG)),
        ("mask_strict_t", np.where(c > p, 0.0, NEG)),
        ("diag16", p // 16 == c // 16),
    ]
    for n in (16, 32, 64):
        below = (p // n == c // n + 1) & (p // (2 * n) == c // (2 * n))
        parts += [(f"below{n}", below), (f"below{n}_t", below.T)]
    freq = (10000.0 ** (-np.arange(0, ROPE, 2, dtype=np.float32) / ROPE)).astype(np.float32)
    parts.append(("freq", np.broadcast_to(freq[None, :], (P, ROPE // 2))))
    parts.append(("past_first_block", p >= CMP_LEN - 1))
    parts.append(("ones", np.ones((P, SEQ))))
    sel = np.zeros((P, NH, P))
    for h in range(NH):
        sel[h, h, :] = 1.0
    parts.append(("headrow", sel.reshape(P, NH * P)))
    d = np.maximum(np.arange(SEQ), 1).astype(np.float32)
    exact = N_BUCKETS // 2
    large = exact + (np.log(d / exact) / math.log(MAX_DISTANCE / exact) * (N_BUCKETS - exact)).astype(np.int32)
    bucket = np.where(np.arange(SEQ) < exact, np.arange(SEQ), np.minimum(large, N_BUCKETS - 1))
    parts.append(("bucket", p == bucket[None, :]))
    at = 0
    for name, a in parts:
        CONST_COLS[name] = (at, a.shape[1])
        at += a.shape[1]
    return np.ascontiguousarray(np.concatenate([np.asarray(a, np.float32) for _, a in parts], axis=1))


CONSTS_SHAPE = shape_constants().shape


class Tensors:
    pass


def linker(engine, sem):
    count = [0]

    def link(ins):
        count[0] += 1
        ins.then_inc(sem, 1)
        engine.wait_ge(sem, count[0])
    return link


def tok(ti):
    return slice(ti * P, (ti + 1) * P)


def setup_phase(nc, T, sem, x, positions, t5_table, consts, bias_dram):
    with ExitStack() as ctx:
        W = 896
        BL = 640 + SEQ
        hank = ctx.enter_context(nc.sbuf_tensor("hank", [P, NH, W], F32))
        table = ctx.enter_context(nc.sbuf_tensor("table", [N_BUCKETS, NH], F32))
        bucket = ctx.enter_context(nc.sbuf_tensor("bucket", [N_BUCKETS, SEQ], F32))
        brow = ctx.enter_context(nc.sbuf_tensor("brow", [NH, BL], F32))
        pos_i = ctx.enter_context(nc.sbuf_tensor("pos_i", [P, NT], I32))
        pos_f = ctx.enter_context(nc.sbuf_tensor("pos_f", [P, NT], F32))
        ang = ctx.enter_context(nc.sbuf_tensor("ang", [P, NT, 2, 16], F32))
        turns = ctx.enter_context(nc.sbuf_tensor("turns", [P, NT, 2, 16], F32))
        turns_i = ctx.enter_context(nc.sbuf_tensor("turns_i", [P, NT, 2, 16], I32))
        ps = ctx.enter_context(nc.psum_tensor("ps_setup", [P, 1, BANK], F32))
        consts_in, small_in, resid_in = sem("consts_in"), sem("small_in"), sem("resid_in")
        row_mm, row_ready, row_out, hank_in = sem("row_mm"), sem("row_ready"), sem("row_out"), sem("hank_in")
        chain, angle_ready, rope_done = sem("setup_chain"), sem("angle_ready"), sem("rope_done")
        block = ctx.enter_context(nc.Block())

        @block.sync
        def _(sp):
            sp.dma_start(T.consts[:, :], consts[:, 0:CONSTS_SHAPE[1] - SEQ]).then_inc(consts_in, 16)
            sp.dma_start(bucket[:, :], consts[0:N_BUCKETS, CONSTS_SHAPE[1] - SEQ:]).then_inc(small_in, 16)
            sp.dma_start(table[:, :], t5_table).then_inc(small_in, 16)
            sp.dma_start(pos_i[:, :], positions[0, :].rearrange("(t p) -> p t", p=P)).then_inc(small_in, 16)
            sp.dma_start(T.resid[:, :, :], x[0, :, :].rearrange("(t p) d -> p t d", p=P)).then_inc(resid_in, 16)
            sp.wait_ge(row_ready, 1)
            sp.dma_start(bias_dram[:, :], brow[:, :]).then_inc(row_out, 16)
            sp.wait_ge(row_out, 16)
            sp.dma_start(hank[:, :, :], bass.AP(tensor=bias_dram.tensor, offset=129,
                                                ap=[[1, P], [BL, NH], [1, W]])).then_inc(hank_in, 16)
            sp.wait_ge(resid_in, 16)

        @block.tensor
        def _(pe):
            pe.wait_ge(consts_in, 16)
            pe.wait_ge(small_in, 48)
            nc.tensor.matmul(ps[0:NH, 0, :], table[:, :], bucket[:, :],
                             start=True, stop=True).then_inc(row_mm, 1)

        @block.vector
        def _(dve):
            link = linker(dve, chain)
            link(nc.vector.memset(brow[:, 0:640], NEG))
            dve.wait_ge(row_mm, 1)
            nc.vector.tensor_copy(brow[:, 640:BL], ps[0:NH, 0, :]).then_inc(row_ready, 1)
            dve.wait_ge(small_in, 48)
            link(nc.vector.tensor_copy(pos_f[:, :], pos_i[:, :]))
            for half in range(2):
                link(nc.vector.tensor_tensor(ang[:, :, half, :],
                                             pos_f[:, :].unsqueeze(2).to_broadcast([P, NT, 16]),
                                             T.const("freq").unsqueeze(1).to_broadcast([P, NT, 16]), ALU.mult))
            for half, ahead in ((0, 0.25), (1, 0.0)):
                link(nc.vector.tensor_scalar(turns[:, :, half, :], ang[:, :, half, :], 1.0 / (2 * math.pi),
                                             ahead, ALU.mult, ALU.add))
            link(nc.vector.tensor_copy(turns_i[:, :, :, :], turns[:, :, :, :]))
            link(nc.vector.tensor_copy(turns[:, :, :, :], turns_i[:, :, :, :]))
            c1 = 6.28125
            c2 = float(np.float32(np.round((2 * math.pi - c1) * 2 ** 20) / 2 ** 20))
            c3 = 2 * math.pi - c1 - c2
            for part in (c1, c2, c3):
                link(nc.vector.scalar_tensor_tensor(ang[:, :, :, :].rearrange("p t c f -> p (t c f)"),
                                                    turns[:, :, :, :].rearrange("p t c f -> p (t c f)"), -part,
                                                    ang[:, :, :, :].rearrange("p t c f -> p (t c f)"),
                                                    ALU.mult, ALU.add))
            link(nc.vector.tensor_scalar_add(ang[:, :, 0, :], ang[:, :, 0, :], math.pi / 2))
            flat = ang[:, :, :, :].rearrange("p t c f -> p (t c f)")
            nc.vector.tensor_scalar(flat, flat, 3.1415925, -3.1415925, ALU.min, ALU.max).then_inc(angle_ready, 1)
            dve.wait_ge(hank_in, 16)
            nc.vector.tensor_copy(T.biasq[:, :, :], hank[:, :, W - 1:W - 1 - SEQ:-1])
            for h in range(NH):
                for ti in range(NT):
                    first = 480 + P * ti
                    nc.vector.tensor_copy(T.biasc[:, h, ti, :],
                                          hank[:, h, first - 16 * (N_CMP - 1):first + 1][:, ::-CMP_STRIDE])

        @block.scalar
        def _(act):
            act.wait_ge(angle_ready, 1)
            nc.scalar.activation(T.cossin[:, :, :, :].rearrange("p t c f -> p (t c f)"),
                                 ang[:, :, :, :].rearrange("p t c f -> p (t c f)"), ACT.Sin)


def norm_phase(nc, T, sem, name, gain_src):
    with ExitStack() as ctx:
        gain = ctx.enter_context(nc.sbuf_tensor(f"{name}_gain", [P, KD], F32))
        xn = ctx.enter_context(nc.sbuf_tensor(f"{name}_xn", [P, NT, D_MODEL], F32))
        stat = ctx.enter_context(nc.sbuf_tensor(f"{name}_stat", [P, 4, NT], F32))
        ps = ctx.enter_context(nc.psum_tensor(f"{name}_ps", [P, KD, BANK], F32))
        gain_in, squares, mean_ready, root_ready = (sem(f"{name}_{s}") for s in ("gain_in", "squares", "mean", "root"))
        normed, turned, chain = (sem(f"{name}_{s}") for s in ("normed", "turned", "chain"))
        block = ctx.enter_context(nc.Block())

        @block.sync
        def _(sp):
            sp.dma_start(gain[:, :], gain_src).then_inc(gain_in, 16)

        def evacuate(k, engine):
            engine.wait_ge(turned, k + 1)

        @block.scalar
        def _(act):
            for ti in range(NT):
                nc.scalar.activation(xn[:, ti, :], T.resid[:, ti, :], ACT.Square,
                                     accum_out=stat[:, 0, ti:ti + 1]).then_inc(squares, 1)
            act.wait_ge(mean_ready, 1)
            nc.scalar.activation(stat[:, 2, :], stat[:, 1, :], ACT.Sqrt).then_inc(root_ready, 1)
            act.wait_ge(gain_in, 16)
            for k in range(0, KD, 2):
                evacuate(k, act)
                nc.scalar.activation(T.xnT[:, k, :], ps[:, k, :], ACT.Copy, scale=gain[:, k:k + 1])

        @block.vector
        def _(dve):
            link = linker(dve, chain)
            dve.wait_ge(squares, NT)
            nc.vector.tensor_scalar(stat[:, 1, :], stat[:, 0, :], 1.0 / D_MODEL, EPS,
                                    ALU.mult, ALU.add).then_inc(mean_ready, 1)
            dve.wait_ge(root_ready, 1)
            link(nc.vector.reciprocal(stat[:, 3, :], stat[:, 2, :]))
            for ti in range(NT):
                nc.vector.tensor_scalar(xn[:, ti, :], T.resid[:, ti, :], stat[:, 3, ti:ti + 1], None,
                                        ALU.mult).then_inc(normed, 1)
            dve.wait_ge(gain_in, 16)
            for k in range(1, KD, 2):
                evacuate(k, dve)
                nc.vector.tensor_scalar(T.xnT[:, k, :], ps[:, k, :], gain[:, k:k + 1], None, ALU.mult)

        @block.tensor
        def _(pe):
            pe.wait_ge(normed, NT)
            for k in range(KD):
                for ti in range(NT):
                    last = nc.tensor.transpose(ps[:, k, tok(ti)], xn[:, ti, k * P:(k + 1) * P], T.const("ident"))
                last.then_inc(turned, 1)


GROUPS = [(0, 384), (384, NSA_IN - 384),
          (ML_BASE, 384), (ML_BASE + 384, 384), (ML_BASE + 768, GW + 2 * NH),
          (GDN_BASE, 384), (GDN_BASE + 384, 384), (GDN_BASE + 768, GW + 2 * NH),
          (MLA_BASE, MLA_IN)]
MAX_GROUP = max(width for _, width in GROUPS)


def projection_tiles():
    tiles = []

    def fm(g, col, width, copies):
        tiles.append((g, True, col, width, 0, copies))

    def tm(g, col, width, name):
        for ti in range(NT):
            tiles.append((g, False, col, width, ti, [(name, ti, 0, 1.0)]))
    scale = HD ** -0.5
    for i in range(2):
        fm(0, i * P, P, [("nsa_q", 2 * i + j, 64 * j, scale) for j in range(2)])
    fm(0, 256, P, [("cmp_kv", j, 64 * j, 1.0) for j in range(2)])
    fm(1, 0, HD, [("nsa_k", 0, 0, 1.0)])
    fm(1, 128, HD, [("nsa_k", 1, 0, 1.0)])
    tm(1, 64, NSA_IN - 448, "nsa_tm")
    for i in range(2):
        fm(2, i * P, P, [("ml_q", 2 * i + j, 64 * j, 1.0) for j in range(2)])
    fm(2, 256, P, [("ml_k", j, 64 * j, scale) for j in range(2)])
    fm(3, 0, P, [("ml_k", 2 + j, 64 * j, scale) for j in range(2)])
    tm(3, P, GW, "ml_v")
    tm(4, 0, GW + 2 * NH, "ml_gates")
    for i in range(6):
        fm(5 + i // 3, i % 3 * P, P, [("gdn_in", i, 0, 1.0)])
    tm(7, 0, GW + 2 * NH, "gdn_gates")
    tm(8, 0, MLA_IN, "mla_tm")
    return tiles


def projection_phase(nc, T, sem, layer, w_in):
    tiles = projection_tiles()
    with ExitStack() as ctx:
        wbuf = ctx.enter_context(nc.sbuf_tensor("w_in_buf", [P, 2, KD, MAX_GROUP], F32))
        ps = ctx.enter_context(nc.psum_tensor("ps_proj", [P, 8, BANK], F32))
        group_in = [sem(f"w_in_{g}") for g in range(len(GROUPS))]
        product, out_act, out_dve = sem("proj_product"), sem("proj_act"), sem("proj_dve")
        block = ctx.enter_context(nc.Block())

        def target(copy, width, is_fm):
            name, at, row, _ = copy
            if name == "gdn_in":
                return T.gdn_in[:, at, CONV_W - 1:CONV_W - 1 + SEQ]
            if is_fm:
                return {"nsa_q": T.nsa_q, "cmp_kv": T.cmp_kv, "nsa_k": T.nsa_k,
                        "ml_q": T.ml_q, "ml_k": T.ml_k}[name][:, at, :]
            return {"nsa_tm": T.nsa_tm, "ml_v": T.ml_v, "ml_gates": T.ml_gates,
                    "gdn_gates": T.gdn_gates, "mla_tm": T.mla_tm}[name][:, at, :]

        def source(n, copy):
            _, is_fm, _, width, _, copies = tiles[n]
            if not is_fm:
                return ps[:, n % 8, 0:width]
            rows = HD if copy[0] != "gdn_in" else P
            return ps[copy[2]:copy[2] + rows, n % 8, :]

        @block.sync
        def _(sp):
            for g, (base, width) in enumerate(GROUPS):
                if g >= 2:
                    sp.wait_ge(product, [t[0] for t in tiles].index(g - 1))
                sp.dma_start(wbuf[:, g % 2, :, 0:width],
                             w_in[bass.ds(layer, 1), :, base:base + width]
                             .rearrange("a (k p) c -> p (a k) c", p=P)).then_inc(group_in[g], 16)

        @block.tensor
        def _(pe):
            for n, (g, is_fm, col, width, ti, _) in enumerate(tiles):
                if n == 0 or tiles[n - 1][0] != g:
                    pe.wait_ge(group_in[g], 16)
                if n >= 8:
                    pe.wait_ge(out_act if n % 2 == 0 else out_dve, (n - 8) // 2 + 1)
                for k in range(KD):
                    w = wbuf[:, g % 2, k, col:col + width]
                    if is_fm:
                        last = nc.tensor.matmul(ps[0:width, n % 8, :], w, T.xnT[:, k, :],
                                                start=(k == 0), stop=(k == KD - 1))
                    else:
                        last = nc.tensor.matmul(ps[:, n % 8, 0:width], T.xnT[:, k, tok(ti)], w,
                                                start=(k == 0), stop=(k == KD - 1))
                last.then_inc(product, 1)

        @block.scalar
        def _(act):
            for n in range(0, len(tiles), 2):
                act.wait_ge(product, n + 1)
                for copy in tiles[n][5]:
                    last = nc.scalar.activation(target(copy, tiles[n][3], tiles[n][1]), source(n, copy),
                                                ACT.Copy, scale=copy[3])
                last.then_inc(out_act, 1)

        @block.vector
        def _(dve):
            nc.vector.memset(T.gdn_in[:, :, 0:CONV_W - 1], 0.0)
            for n in range(1, len(tiles), 2):
                dve.wait_ge(product, n + 1)
                for copy in tiles[n][5]:
                    last = nc.vector.tensor_scalar(target(copy, tiles[n][3], tiles[n][1]), source(n, copy),
                                                   copy[3], None, ALU.mult)
                last.then_inc(out_dve, 1)


C_NEGM, C_NEGMT, C_GC, C_R, C_KD, C_LB = range(6)


def gate_phase(nc, T, sem, layer, ml_i_bias, ml_f_bias, gdn_dt_bias, gdn_a_log):
    with ExitStack() as ctx:
        def sb(name, shape):
            return ctx.enter_context(nc.sbuf_tensor(name, shape, F32))
        bias = sb("gate_bias", [P, 4, NH])
        lx = sb("gate_lx", [P, NT, 3, NH])
        tmp = sb("gate_tmp", [P, 3, NT, 3, NH])
        ea = sb("gate_ea", [P, NH])
        tokg = sb("gate_tok", [P, 4, NT, NH])
        rows = sb("gate_rows", [NH, 4, SEQ])
        work = sb("gate_work", [NH, 6, SEQ])
        cum = sb("gate_cum", [NH, 2, SEQ])
        ps = ctx.enter_context(nc.psum_tensor("ps_gate", [P, 8, BANK], F32))
        bias_in, chain, shrunk, exp_done = sem("gate_bias_in"), sem("gate_chain"), sem("gate_shrunk"), sem("gate_exp")
        shifted, ln_done, tok_ready, row_mm = sem("gate_shifted"), sem("gate_ln"), sem("gate_tok_ready"), sem("gate_row_mm")
        rows_ready, col_mm, cols_ready = sem("gate_rows_ready"), sem("gate_col_mm"), sem("gate_cols_ready")
        block = ctx.enter_context(nc.Block())

        @block.sync
        def _(sp):
            for n, src in enumerate((ml_i_bias, ml_f_bias, gdn_dt_bias, gdn_a_log)):
                sp.dma_start(bias[:, n, :], src[bass.ds(layer, 1), :].to_broadcast([P, NH])).then_inc(bias_in, 16)

        @block.scalar
        def _(act):
            act.wait_ge(shrunk, 1)
            nc.scalar.activation(tmp[:, 1, :, :, :].rearrange("p t c h -> p (t c h)"),
                                 tmp[:, 0, :, :, :].rearrange("p t c h -> p (t c h)"), ACT.Exp).then_inc(exp_done, 1)
            nc.scalar.activation(ea[:, :], bias[:, 3, :], ACT.Exp).then_inc(exp_done, 1)
            act.wait_ge(shifted, 1)
            nc.scalar.activation(tmp[:, 2, :, :, :].rearrange("p t c h -> p (t c h)"),
                                 tmp[:, 1, :, :, :].rearrange("p t c h -> p (t c h)"), ACT.Ln).then_inc(ln_done, 1)
            act.wait_ge(cols_ready, 1)
            nc.scalar.activation(T.exp_cols[:, :, :, :].rearrange("p c t h -> p (c t h)"),
                                 T.cols[:, :, :, :].rearrange("p c t h -> p (c t h)"), ACT.Exp)

        @block.vector
        def _(dve):
            link = linker(dve, chain)
            dve.wait_ge(bias_in, 64)

            def over_tiles(n):
                return bias[:, n, :].unsqueeze(1).to_broadcast([P, NT, NH])
            nc.vector.tensor_tensor(tokg[:, 0, :, :], T.ml_gates[:, :, 0:NH], over_tiles(0), ALU.add)
            link(nc.vector.tensor_tensor(lx[:, :, 0, :], T.ml_gates[:, :, NH:2 * NH], over_tiles(1), ALU.add))
            link(nc.vector.tensor_copy(lx[:, :, 1, :], T.gdn_gates[:, :, 0:NH]))
            link(nc.vector.tensor_tensor(lx[:, :, 2, :], T.gdn_gates[:, :, NH:2 * NH], over_tiles(2), ALU.add))
            link(nc.vector.tensor_scalar_mul(lx[:, :, 2, :], lx[:, :, 2, :], -1.0))
            flat = lx[:, :, :, :].rearrange("p t c h -> p (t c h)")

            def part(n):
                return tmp[:, n, :, :, :].rearrange("p t c h -> p (t c h)")
            link(nc.vector.tensor_scalar_mul(part(0), flat, -1.0))
            nc.vector.tensor_tensor(part(0), part(0), flat, ALU.min).then_inc(shrunk, 1)
            dve.wait_ge(exp_done, 2)
            nc.vector.tensor_scalar_add(part(1), part(1), 1.0).then_inc(shifted, 1)
            link(nc.vector.tensor_scalar_min(part(0), flat, 0.0))
            dve.wait_ge(ln_done, 1)
            for c in range(3):
                link(nc.vector.tensor_tensor(tokg[:, 1 + c, :, :], tmp[:, 0, :, c, :], tmp[:, 2, :, c, :],
                                             ALU.subtract))
            nc.vector.tensor_tensor(tokg[:, 3, :, :], tokg[:, 3, :, :],
                                    ea[:, :].unsqueeze(1).to_broadcast([P, NT, NH]), ALU.mult).then_inc(tok_ready, 1)
            dve.wait_ge(row_mm, 1)
            link(nc.vector.tensor_copy(rows[:, :, :], ps[0:NH, 0:4, :]))
            ones = T.const("ones", 0, NH)
            link(nc.vector.tensor_tensor_scan(cum[:, 0, :], ones, rows[:, 1, :], 0.0, ALU.mult, ALU.add))
            link(nc.vector.tensor_tensor(T.rows[:, 0, :], rows[:, 0, :], cum[:, 0, :], ALU.subtract))
            link(nc.vector.tensor_tensor_scan(cum[:, 1, :], T.rows[:, 0, :], T.rows[:, 0, :], 0.0, ALU.max, ALU.max))
            link(nc.vector.tensor_scalar_mul(work[:, C_NEGM, :], cum[:, 1, :], -1.0))
            link(nc.vector.tensor_tensor(work[:, C_NEGMT, :], work[:, C_NEGM, :], cum[:, 0, :], ALU.subtract))
            for ti in range(NT):
                link(nc.vector.tensor_tensor_scan(work[:, C_GC, tok(ti)], ones[:, tok(0)], rows[:, 3, tok(ti)],
                                                  0.0, ALU.mult, ALU.add))
                end = (ti + 1) * P
                link(nc.vector.tensor_scalar(work[:, C_KD, tok(ti)], work[:, C_GC, tok(ti)], -1.0,
                                             work[:, C_GC, end - 1:end], ALU.mult, ALU.add))
            link(nc.vector.tensor_copy(T.rows[:, 1, :], work[:, C_GC, :]))
            link(nc.vector.tensor_tensor(work[:, C_R, :], work[:, C_GC, :], rows[:, 2, :], ALU.add))
            link(nc.vector.tensor_copy(T.rows[:, 2, :], work[:, C_R, :]))
            nc.vector.tensor_copy(work[:, C_LB, :], rows[:, 2, :]).then_inc(rows_ready, 1)
            dve.wait_ge(col_mm, 1)
            nc.vector.tensor_copy(T.cols[:, :, :, :].rearrange("p c t h -> p (c t h)"),
                                  ps[:, 4, 0:6 * NT * NH]).then_inc(cols_ready, 1)
            dve.wait_ge(cols_ready, 1)
            nc.vector.tensor_scalar_mul(T.neg_gc[:, :, :].rearrange("p t h -> p (t h)"),
                                        T.cols[:, C_GC, :, :].rearrange("p t h -> p (t h)"), -1.0)

        @block.tensor
        def _(pe):
            pe.wait_ge(tok_ready, 1)
            for c in range(4):
                for ti in range(NT):
                    last = nc.tensor.transpose(ps[0:NH, c, tok(ti)], tokg[:, c, ti, :], T.const("ident"))
            last.then_inc(row_mm, 1)
            pe.wait_ge(rows_ready, 1)
            for c in range(6):
                for ti in range(NT):
                    at = (c * NT + ti) * NH
                    last = nc.tensor.transpose(ps[:, 4, at:at + NH], work[:, c, tok(ti)],
                                               T.const("ident", 0, NH, NH))
            last.then_inc(col_mm, 1)


def compress_phase(nc, T, sem, layer, w_cmp_k, w_cmp_v, cmp_pos):
    with ExitStack() as ctx:
        wk = ctx.enter_context(nc.sbuf_tensor("cmp_wk", [HD, CMP_LEN, HD], F32))
        wv = ctx.enter_context(nc.sbuf_tensor("cmp_wv", [HD, CMP_LEN, HD], F32))
        pos = ctx.enter_context(nc.sbuf_tensor("cmp_pos", [CMP_LEN, HD], F32))
        posT = ctx.enter_context(nc.sbuf_tensor("cmp_posT", [HD, CMP_LEN], F32))
        blocks = ctx.enter_context(nc.sbuf_tensor("cmp_blocks", [HD, 2, N_CMP, CMP_LEN], F32))
        ps = ctx.enter_context(nc.psum_tensor("ps_cmp", [P, 3, BANK], F32))
        loaded, pos_mm, pos_ready = sem("cmp_loaded"), sem("cmp_pos_mm"), sem("cmp_pos_ready")
        blocks_ready, product = sem("cmp_blocks_ready"), sem("cmp_product")
        block = ctx.enter_context(nc.Block())

        @block.sync
        def _(sp):
            sp.dma_start(pos[:, :], cmp_pos[bass.ds(layer, 1), :, :].rearrange("a l d -> (a l) d")).then_inc(loaded, 16)
            for w, src in ((wk, w_cmp_k), (wv, w_cmp_v)):
                sp.dma_start(w[:, :, :], src[bass.ds(layer, 1), :, :]
                             .rearrange("a (l d) e -> d (a l) e", d=HD)).then_inc(loaded, 16)

        @block.tensor
        def _(pe):
            pe.wait_ge(loaded, 48)
            nc.tensor.transpose(ps[0:HD, 2, 0:CMP_LEN], pos[:, :], T.const("ident", 0, CMP_LEN, CMP_LEN)).then_inc(pos_mm, 1)
            pe.wait_ge(blocks_ready, 2)
            for i in range(CMP_LEN):
                last = nc.tensor.matmul(ps[0:HD, 0, 0:N_CMP], wk[:, i, :], blocks[:, 0, :, i],
                                        start=(i == 0), stop=(i == CMP_LEN - 1))
            last.then_inc(product, 1)
            for i in range(CMP_LEN):
                last = nc.tensor.matmul(ps[0:N_CMP, 1, 0:HD], blocks[:, 1, :, i], wv[:, i, :],
                                        start=(i == 0), stop=(i == CMP_LEN - 1))
            last.then_inc(product, 1)

        @block.vector
        def _(dve):
            dve.wait_ge(pos_mm, 1)
            nc.vector.tensor_copy(posT[:, :], ps[0:HD, 2, 0:CMP_LEN]).then_inc(pos_ready, 1)
            dve.wait_ge(pos_ready, 1)
            for c in range(2):
                src = T.cmp_kv[:, c, :]
                src = bass.AP(tensor=src.tensor, offset=src.offset,
                              ap=[list(src.ap[0]), [CMP_STRIDE, N_CMP], [1, CMP_LEN]])
                nc.vector.tensor_tensor(blocks[:, c, :, :], src,
                                        posT[:, :].unsqueeze(1).to_broadcast([HD, N_CMP, CMP_LEN]),
                                        ALU.add).then_inc(blocks_ready, 1)
            dve.wait_ge(product, 1)
            nc.vector.tensor_copy(T.k_cmp[:, :], ps[0:HD, 0, 0:N_CMP])
            dve.wait_ge(product, 2)
            nc.vector.tensor_copy(T.v_cmp[:, :], ps[0:N_CMP, 1, 0:HD])

        @block.scalar
        def _(act):
            nc.scalar.activation(T.nsa_gate[:, :, :], T.nsa_tm[:, :, 192:192 + 3 * NH], ACT.Sigmoid)


def mla_phase(nc, T, sem, layer, q_norm_g, kv_norm_g, w_uq, w_ukv):
    with ExitStack() as ctx:
        def sb(name, shape):
            return ctx.enter_context(nc.sbuf_tensor(name, shape, F32))
        wq = sb("mla_wq", [P, 2, NH * QD])
        wkv = sb("mla_wkv", [P, NH * 2 * HD])
        gain = sb("mla_gain", [P, 3])
        stat = sb("mla_stat", [P, 4, NT, 2])
        cn = sb("mla_cn", [P, NT, Q_LORA + KV_LORA])
        cT = sb("mla_cT", [P, 3, SEQ])
        qcat = sb("mla_qcat", [P, NT, NH, QD])
        kcat = sb("mla_kcat", [P, NT, NH, QD])
        kr = sb("mla_kr", [P, NT, ROPE])
        ra = sb("mla_ra", [P, 4, NT, NH, 16])
        rk = sb("mla_rk", [P, 4, NT, 16])
        ps = ctx.enter_context(nc.psum_tensor("ps_mla", [P, 8, BANK], F32))
        loaded, squares, mean_ready, root = sem("mla_loaded"), sem("mla_squares"), sem("mla_mean"), sem("mla_root")
        normed, turned, turned_out, product = sem("mla_normed"), sem("mla_turned"), sem("mla_turned_out"), sem("mla_product")
        raw_out, chain, cats_ready, cat_turned, chain_act = (sem("mla_raw_out"), sem("mla_chain"), sem("mla_cats"),
                                                             sem("mla_cat_turned"), sem("mla_cat_out"))
        block = ctx.enter_context(nc.Block())
        widths = ((0, Q_LORA), (Q_LORA, Q_LORA + KV_LORA))

        @block.sync
        def _(sp):
            sp.dma_start(wq[:, :, :], w_uq[bass.ds(layer, 1), :, :]
                         .rearrange("a (k p) c -> p (a k) c", p=P)).then_inc(loaded, 16)
            sp.dma_start(wkv[:, :], w_ukv[bass.ds(layer, 1), :, :].rearrange("a p c -> (a p) c")).then_inc(loaded, 16)
            sp.dma_start(gain[:, 0:2], q_norm_g[bass.ds(layer, 1), :].rearrange("a (k p) -> p (a k)", p=P),
                         ).then_inc(loaded, 16)
            sp.dma_start(gain[:, 2:3], kv_norm_g[bass.ds(layer, 1), :].rearrange("a p -> p a")).then_inc(loaded, 16)

        @block.scalar
        def _(act):
            for ti in range(NT):
                for c, (a, b) in enumerate(widths):
                    nc.scalar.activation(cn[:, ti, a:b], T.mla_tm[:, ti, a:b], ACT.Square,
                                         accum_out=stat[:, 0, ti, c:c + 1]).then_inc(squares, 1)
            act.wait_ge(mean_ready, 2)
            nc.scalar.activation(stat[:, 2, :, :], stat[:, 1, :, :], ACT.Sqrt).then_inc(root, 1)
            act.wait_ge(loaded, 64)
            for c in range(3):
                act.wait_ge(turned, c + 1)
                nc.scalar.activation(cT[:, c, :], ps[:, c, :], ACT.Copy, scale=gain[:, c:c + 1]).then_inc(turned_out, 1)
            for ti in range(NT):
                act.wait_ge(product, NT + ti + 1)
                bank = ps[:, 4 + ti, :].rearrange("p (h c) -> p h c", h=NH)
                nc.scalar.activation(T.mla_v[:, ti, :, :], bank[:, :, HD:2 * HD], ACT.Copy)
                nc.scalar.activation(kcat[:, ti, :, 0:HD], bank[:, :, 0:HD], ACT.Copy).then_inc(raw_out, 1)
            for n in range(0, 8, 2):
                act.wait_ge(cat_turned, n + 1)
                nc.scalar.activation(T.mla_qk[:, n, :], ps[0:QD, n, :], ACT.Copy)

        @block.vector
        def _(dve):
            link = linker(dve, chain)
            dve.wait_ge(squares, 2 * NT)
            for c, (a, b) in enumerate(widths):
                nc.vector.tensor_scalar(stat[:, 1, :, c], stat[:, 0, :, c], 1.0 / (b - a), EPS,
                                        ALU.mult, ALU.add).then_inc(mean_ready, 1)
            dve.wait_ge(root, 1)
            link(nc.vector.reciprocal(stat[:, 3, :, :], stat[:, 2, :, :]))
            for ti in range(NT):
                for c, (a, b) in enumerate(widths):
                    nc.vector.tensor_scalar(cn[:, ti, a:b], T.mla_tm[:, ti, a:b], stat[:, 3, ti, c:c + 1], None,
                                            ALU.mult).then_inc(normed, 1)
            for ti in range(NT):
                dve.wait_ge(product, ti + 1)
                bank = ps[:, ti, 0:NH * QD].rearrange("p (h c) -> p h c", h=NH)
                link(nc.vector.tensor_scalar(qcat[:, ti, :, :], bank, QD ** -0.5, None, ALU.mult))
            cos, sin = T.cossin[:, :, 0, :], T.cossin[:, :, 1, :]
            cosq, sinq = (v.unsqueeze(2).to_broadcast([P, NT, NH, 16]) for v in (cos, sin))
            t1, t2 = qcat[:, :, :, HD:HD + 16], qcat[:, :, :, HD + 16:QD]
            k1, k2 = (T.mla_tm[:, :, Q_LORA + KV_LORA + 16 * i:Q_LORA + KV_LORA + 16 * i + 16] for i in range(2))
            for ti in range(NT):
                cq = cos[:, ti, :].unsqueeze(1).to_broadcast([P, NH, 16])
                sq = sin[:, ti, :].unsqueeze(1).to_broadcast([P, NH, 16])
                nc.vector.tensor_tensor(ra[:, 0, ti, :, :], t1[:, ti], cq, ALU.mult)
                nc.vector.tensor_tensor(ra[:, 1, ti, :, :], t2[:, ti], sq, ALU.mult)
                nc.vector.tensor_tensor(ra[:, 2, ti, :, :], t2[:, ti], cq, ALU.mult)
                link(nc.vector.tensor_tensor(ra[:, 3, ti, :, :], t1[:, ti], sq, ALU.mult))
            nc.vector.tensor_tensor(t1, ra[:, 0, :, :, :], ra[:, 1, :, :, :], ALU.subtract).then_inc(cats_ready, 1)
            nc.vector.tensor_tensor(t2, ra[:, 2, :, :, :], ra[:, 3, :, :, :], ALU.add).then_inc(cats_ready, 1)
            nc.vector.tensor_tensor(rk[:, 0, :, :], k1, cos, ALU.mult)
            nc.vector.tensor_tensor(rk[:, 1, :, :], k2, sin, ALU.mult)
            nc.vector.tensor_tensor(rk[:, 2, :, :], k2, cos, ALU.mult)
            link(nc.vector.tensor_tensor(rk[:, 3, :, :], k1, sin, ALU.mult))
            nc.vector.tensor_tensor(kr[:, :, 0:16], rk[:, 0, :, :], rk[:, 1, :, :], ALU.subtract)
            link(nc.vector.tensor_tensor(kr[:, :, 16:32], rk[:, 2, :, :], rk[:, 3, :, :], ALU.add))
            nc.vector.tensor_copy(kcat[:, :, :, HD:QD],
                                  kr[:, :, :].unsqueeze(2).to_broadcast([P, NT, NH, ROPE])).then_inc(cats_ready, 1)
            for n in range(1, 8, 2):
                dve.wait_ge(cat_turned, n + 1)
                nc.vector.tensor_copy(T.mla_qk[:, n, :], ps[0:QD, n, :])

        @block.tensor
        def _(pe):
            pe.wait_ge(normed, 2 * NT)
            for c in range(3):
                for ti in range(NT):
                    last = nc.tensor.transpose(ps[:, c, tok(ti)], cn[:, ti, c * P:(c + 1) * P], T.const("ident"))
                last.then_inc(turned, 1)
            pe.wait_ge(turned_out, 3)
            for ti in range(NT):
                for c in range(2):
                    last = nc.tensor.matmul(ps[:, ti, 0:NH * QD], cT[:, c, tok(ti)], wq[:, c, :],
                                            start=(c == 0), stop=(c == 1))
                last.then_inc(product, 1)
            for ti in range(NT):
                nc.tensor.matmul(ps[:, 4 + ti, :], cT[:, 2, tok(ti)], wkv[:, :], start=True, stop=True).then_inc(product, 1)
            pe.wait_ge(cats_ready, 3)
            pe.wait_ge(raw_out, NT)
            for n in range(8):
                cat = (qcat, kcat)[n // NH]
                for ti in range(NT):
                    last = nc.tensor.transpose(ps[0:QD, n, tok(ti)], cat[:, ti, n % NH, :], T.const("ident"))
                last.then_inc(cat_turned, 1)


def attention_phase(nc, T, sem):
    assert min(16, SEQ // 64) == SEQ // 64
    jobs = [(kind, qi, h) for qi in range(NT) for h in range(NH) for kind in ("cmp", "sel", "win", "mla")]
    n_jobs = len(jobs)
    with ExitStack() as ctx:
        def sb(name, shape):
            return ctx.enter_context(nc.sbuf_tensor(name, shape, F32))
        scores = sb("att_scores", [P, 2, SEQ])
        probs = sb("att_probs", [P, 2, SEQ])
        probsT = sb("att_probsT", [P, 2, SEQ])
        top = sb("att_top", [P, n_jobs])
        negtop = sb("att_negtop", [P, n_jobs])
        total = sb("att_total", [P, n_jobs])
        inv = sb("att_inv", [P, n_jobs])
        fac = sb("att_fac", [P, n_jobs])
        ps_s = ctx.enter_context(nc.psum_tensor("ps_scores", [P, 2, BANK], F32))
        ps_t = ctx.enter_context(nc.psum_tensor("ps_probsT", [P, 2, BANK], F32))
        ps_o = ctx.enter_context(nc.psum_tensor("ps_out", [P, 2, BANK], F32))
        scored, masked, top_ready, exp_done = sem("att_scored"), sem("att_masked"), sem("att_top_ready"), sem("att_exp")
        turned, turned_out, product, chain = sem("att_turned"), sem("att_turned_out"), sem("att_product"), sem("att_chain")
        finished = sem("att_finished")
        block = ctx.enter_context(nc.Block())

        def keys(job):
            kind, qi, h = job
            return N_CMP if kind == "cmp" else P * (qi + 1)

        def parts(job):
            n = keys(job)
            return [(b, min(P, n - P * b)) for b in range((n + P - 1) // P)]

        @block.tensor
        def _(pe):
            for j in range(n_jobs + 2):
                if j < n_jobs:
                    kind, qi, h = jobs[j]
                    if j >= 2:
                        pe.wait_ge(masked, j - 1)
                    if kind == "mla":
                        q, k = T.mla_qk[:, h, tok(qi)], T.mla_qk[:, NH + h, 0:keys(jobs[j])]
                    else:
                        q = T.nsa_q[:, h, tok(qi)]
                        k = {"cmp": T.k_cmp[:, :], "sel": T.nsa_k[:, 0, 0:keys(jobs[j])],
                             "win": T.nsa_k[:, 1, 0:keys(jobs[j])]}[kind]
                    nc.tensor.matmul(ps_s[:, j % 2, 0:keys(jobs[j])], q, k, start=True, stop=True).then_inc(scored, 1)
                if 1 <= j <= n_jobs:
                    i = j - 1
                    pe.wait_ge(exp_done, i + 1)
                    if i >= 2:
                        pe.wait_ge(turned_out, i - 1)
                    for b, n in parts(jobs[i]):
                        last = nc.tensor.transpose(ps_t[0:n, i % 2, tok(b)], probs[:, i % 2, P * b:P * b + n],
                                                   T.const("ident"))
                    last.then_inc(turned, 1)
                if j >= 2:
                    i = j - 2
                    kind, qi, h = jobs[i]
                    pe.wait_ge(turned_out, i + 1)
                    if i >= 2:
                        pe.wait_ge(finished, i - 1)
                    for b, n in parts(jobs[i]):
                        v = {"cmp": T.v_cmp[:, :], "sel": T.nsa_tm[:, b, 0:HD], "win": T.nsa_tm[:, b, 2 * HD:3 * HD],
                             "mla": T.mla_v[:, b, h, :]}[kind]
                        last = nc.tensor.matmul(ps_o[:, i % 2, 0:HD], probsT[0:n, i % 2, tok(b)], v,
                                                start=(b == 0), stop=(b == len(parts(jobs[i])) - 1))
                    last.then_inc(product, 1)

        @block.vector
        def _(dve):
            link = linker(dve, chain)
            for j in range(n_jobs + 2):
                if j < n_jobs:
                    kind, qi, h = jobs[j]
                    n = keys(jobs[j])
                    dve.wait_ge(scored, j + 1)
                    if j >= 2:
                        dve.wait_ge(exp_done, j - 1)
                    bias = {"cmp": T.biasc[:, h, qi, :], "mla": T.const("maskq")[:, SEQ - n:SEQ]}.get(
                        kind, T.biasq[:, h, SEQ - n:SEQ])
                    nc.vector.tensor_tensor_reduce(out=scores[:, j % 2, 0:n], in0=ps_s[:, j % 2, 0:n], in1=bias,
                                                   scale=1.0, scalar=-3e38, op0=ALU.add, op1=ALU.max,
                                                   accum_out=top[:, j:j + 1]).then_inc(masked, 1)
                    dve.wait_ge(masked, j + 1)
                    nc.vector.tensor_scalar_mul(negtop[:, j:j + 1], top[:, j:j + 1], -1.0).then_inc(top_ready, 1)
                if j >= 2:
                    i = j - 2
                    kind, qi, h = jobs[i]
                    dve.wait_ge(exp_done, i + 1)
                    link(nc.vector.reciprocal(inv[:, i:i + 1], total[:, i:i + 1]))
                    f = inv[:, i:i + 1]
                    if kind != "mla":
                        branch = {"cmp": 0, "sel": 1, "win": 2}[kind]
                        gate = T.nsa_gate[:, qi, branch * NH + h:branch * NH + h + 1]
                        link(nc.vector.tensor_tensor(fac[:, i:i + 1], f, gate, ALU.mult))
                        f = fac[:, i:i + 1]
                        if kind == "cmp" and qi == 0:
                            link(nc.vector.tensor_tensor(f, f, T.const("past_first_block"), ALU.mult))
                    dve.wait_ge(product, i + 1)
                    o = ps_o[:, i % 2, 0:HD]
                    if kind in ("cmp", "mla"):
                        at = h * HD + (3 * GW if kind == "mla" else 0)
                        nc.vector.tensor_scalar(T.mix[:, qi, at:at + HD], o, f, None, ALU.mult).then_inc(finished, 1)
                    else:
                        dve.wait_ge(finished, i)
                        nc.vector.scalar_tensor_tensor(T.mix[:, qi, h * HD:h * HD + HD], o, f,
                                                       T.mix[:, qi, h * HD:h * HD + HD], ALU.mult,
                                                       ALU.add).then_inc(finished, 1)

        @block.scalar
        def _(act):
            for j in range(n_jobs + 1):
                if j < n_jobs:
                    n = keys(jobs[j])
                    act.wait_ge(top_ready, j + 1)
                    if j >= 2:
                        act.wait_ge(turned, j - 1)
                    nc.scalar.activation(probs[:, j % 2, 0:n], scores[:, j % 2, 0:n], ACT.Exp,
                                         bias=negtop[:, j:j + 1], accum_out=total[:, j:j + 1]).then_inc(exp_done, 1)
                if j >= 1:
                    i = j - 1
                    act.wait_ge(turned, i + 1)
                    if i >= 2:
                        act.wait_ge(product, i - 1)
                    rows = min(P, keys(jobs[i]))
                    nc.scalar.activation(probsT[0:rows, i % 2, 0:P * len(parts(jobs[i]))],
                                         ps_t[0:rows, i % 2, 0:P * len(parts(jobs[i]))],
                                         ACT.Copy).then_inc(turned_out, 1)


def head_norm(nc, dve, act_sems, link, values, square, stat, gain, out):
    mean_ready, root_ready = act_sems
    link(nc.vector.tensor_tensor(square, values, values, ALU.mult))
    link(nc.vector.tensor_reduce(stat[:, 0, :, :], square, AX.X, ALU.add))
    nc.vector.tensor_scalar(stat[:, 1, :, :], stat[:, 0, :, :], 1.0 / HD, EPS, ALU.mult, ALU.add).then_inc(mean_ready, 1)
    dve.wait_ge(root_ready, 1)
    link(nc.vector.reciprocal(stat[:, 3, :, :], stat[:, 2, :, :]))
    link(nc.vector.tensor_tensor(square, values, stat[:, 3, :, :].unsqueeze(3).to_broadcast([P, NT, NH, HD]), ALU.mult))
    if out.shape[1] == NT:
        square = square.rearrange("p t h d -> p t (h d)")
    else:
        square = square.rearrange("p t h d -> p (t h) d")
    link(nc.vector.tensor_tensor(out, square, gain, ALU.mult))


def mlstm_phase(nc, T, sem, layer, norm_g):
    jobs = [(qi, h) for qi in range(NT) for h in range(NH)]
    n_jobs = len(jobs)
    with ExitStack() as ctx:
        def sb(name, shape):
            return ctx.enter_context(nc.sbuf_tensor(name, shape, F32))
        arow = sb("ml_arow", [P, NH, SEQ])
        ktok = sb("ml_masked", [P, 2, SEQ])
        decay = sb("ml_decay", [P, 2, SEQ])
        probs = sb("ml_probs", [P, 2, SEQ])
        probsT = sb("ml_probsT", [P, 2, SEQ])
        den = sb("ml_den", [P, 4, n_jobs])
        hs = sb("ml_hs", [P, NT, NH, HD])
        sq = sb("ml_square", [P, NT, NH, HD])
        og = sb("ml_og", [P, NT, NH, HD])
        gain = sb("ml_gain", [P, GW])
        stat = sb("ml_stat", [P, 4, NT, NH])
        ps_s = ctx.enter_context(nc.psum_tensor("ps_ml_scores", [P, 2, BANK], F32))
        ps_t = ctx.enter_context(nc.psum_tensor("ps_ml_probsT", [P, 2, BANK], F32))
        ps_o = ctx.enter_context(nc.psum_tensor("ps_ml_out", [P, 2, BANK], F32))
        ps_a = ctx.enter_context(nc.psum_tensor("ps_ml_arow", [P, 2, BANK], F32))
        gain_in, bcast, bcast_out, masked = sem("ml_gain_in"), sem("ml_bcast"), sem("ml_bcast_out"), sem("ml_masked")
        decayed, scored, weighed, turned = sem("ml_decayed"), sem("ml_scored"), sem("ml_weighed"), sem("ml_turned")
        turned_out, product, finished, chain = (sem("ml_turned_out"), sem("ml_product"), sem("ml_finished"),
                                                sem("ml_chain"))
        og_done, mean_ready, root_ready = sem("ml_og_done"), sem("ml_mean"), sem("ml_root")
        block = ctx.enter_context(nc.Block())

        @block.sync
        def _(sp):
            sp.dma_start(gain[:, :], norm_g[bass.ds(layer, 1), :].to_broadcast([P, GW])).then_inc(gain_in, 16)

        @block.tensor
        def _(pe):
            for h in range(NH):
                if h >= 2:
                    pe.wait_ge(bcast_out, h - 1)
                nc.tensor.matmul(ps_a[:, h % 2, :], T.head_row(h), T.rows[:, 0, :],
                                 start=True, stop=True).then_inc(bcast, 1)
            for j in range(n_jobs + 2):
                if j < n_jobs:
                    qi, h = jobs[j]
                    if j >= 2:
                        pe.wait_ge(weighed, j - 1)
                    nc.tensor.matmul(ps_s[:, j % 2, 0:P * (qi + 1)], T.ml_q[:, h, tok(qi)],
                                     T.ml_k[:, h, 0:P * (qi + 1)], start=True, stop=True).then_inc(scored, 1)
                if 1 <= j <= n_jobs:
                    i = j - 1
                    pe.wait_ge(weighed, i + 1)
                    if i >= 2:
                        pe.wait_ge(turned_out, i - 1)
                    for b in range(jobs[i][0] + 1):
                        last = nc.tensor.transpose(ps_t[:, i % 2, tok(b)], probs[:, i % 2, tok(b)], T.const("ident"))
                    last.then_inc(turned, 1)
                if j >= 2:
                    i = j - 2
                    qi, h = jobs[i]
                    pe.wait_ge(turned_out, i + 1)
                    if i >= 2:
                        pe.wait_ge(finished, i - 1)
                    for b in range(qi + 1):
                        last = nc.tensor.matmul(ps_o[:, i % 2, 0:HD], probsT[:, i % 2, tok(b)],
                                                T.ml_v[:, b, h * HD:(h + 1) * HD], start=(b == 0), stop=(b == qi))
                    last.then_inc(product, 1)

        @block.vector
        def _(dve):
            link = linker(dve, chain)
            for j in range(n_jobs + 3):
                if j < n_jobs:
                    qi, h = jobs[j]
                    n = P * (qi + 1)
                    if j < NH:
                        dve.wait_ge(bcast_out, j + 1)
                    if j >= 2:
                        dve.wait_ge(decayed, j - 1)
                    nc.vector.tensor_tensor(ktok[:, j % 2, 0:n], arow[:, h, 0:n], T.const("maskq")[:, SEQ - n:SEQ],
                                            ALU.add).then_inc(masked, 1)
                if 1 <= j <= n_jobs:
                    i = j - 1
                    qi, h = jobs[i]
                    n = P * (qi + 1)
                    dve.wait_ge(scored, i + 1)
                    dve.wait_ge(decayed, i + 1)
                    if i >= 2:
                        dve.wait_ge(turned, i - 1)
                    nc.vector.tensor_tensor_reduce(out=probs[:, i % 2, 0:n], in0=ps_s[:, i % 2, 0:n],
                                                   in1=decay[:, i % 2, 0:n], scale=1.0, scalar=0.0, op0=ALU.mult,
                                                   op1=ALU.add, accum_out=den[:, 0, i:i + 1]).then_inc(weighed, 1)
                if j >= 3:
                    i = j - 3
                    qi, h = jobs[i]
                    dve.wait_ge(weighed, i + 1)
                    link(nc.vector.scalar_tensor_tensor(den[:, 1, i:i + 1], den[:, 0, i:i + 1], -1.0,
                                                        den[:, 0, i:i + 1], ALU.mult, ALU.max))
                    link(nc.vector.tensor_tensor(den[:, 2, i:i + 1], den[:, 1, i:i + 1],
                                                 T.exp_cols[:, C_NEGMT, qi, h:h + 1], ALU.max))
                    link(nc.vector.reciprocal(den[:, 3, i:i + 1], den[:, 2, i:i + 1]))
                    dve.wait_ge(product, i + 1)
                    nc.vector.tensor_scalar(hs[:, qi, h, :], ps_o[:, i % 2, 0:HD], den[:, 3, i:i + 1], None,
                                            ALU.mult).then_inc(finished, 1)
            dve.wait_ge(finished, n_jobs)
            dve.wait_ge(og_done, 1)
            link(nc.vector.tensor_tensor(hs[:, :, :, :], hs[:, :, :, :], og[:, :, :, :], ALU.mult))
            dve.wait_ge(gain_in, 16)
            head_norm(nc, dve, (mean_ready, root_ready), link, hs[:, :, :, :], sq[:, :, :, :], stat,
                      gain[:, :].unsqueeze(1).to_broadcast([P, NT, GW]), T.mix[:, :, GW:2 * GW])

        @block.scalar
        def _(act):
            nc.scalar.activation(og[:, :, :, :], T.ml_gates[:, :, 2 * NH:2 * NH + GW]
                                 .rearrange("p t (h d) -> p t h d", h=NH), ACT.Sigmoid).then_inc(og_done, 1)
            for h in range(NH):
                act.wait_ge(bcast, h + 1)
                nc.scalar.activation(arow[:, h, :], ps_a[:, h % 2, :], ACT.Copy).then_inc(bcast_out, 1)
            for j in range(n_jobs + 2):
                if j < n_jobs:
                    qi, h = jobs[j]
                    n = P * (qi + 1)
                    act.wait_ge(masked, j + 1)
                    if j >= 2:
                        act.wait_ge(weighed, j - 1)
                    nc.scalar.activation(decay[:, j % 2, 0:n], ktok[:, j % 2, 0:n], ACT.Exp,
                                         bias=T.cols[:, C_NEGM, qi, h:h + 1]).then_inc(decayed, 1)
                if j >= 2:
                    i = j - 2
                    act.wait_ge(turned, i + 1)
                    if i >= 2:
                        act.wait_ge(product, i - 1)
                    n = P * (jobs[i][0] + 1)
                    nc.scalar.activation(probsT[:, i % 2, 0:n], ps_t[:, i % 2, 0:n], ACT.Copy).then_inc(turned_out, 1)
            act.wait_ge(mean_ready, 1)
            nc.scalar.activation(stat[:, 2, :, :], stat[:, 1, :, :], ACT.Sqrt).then_inc(root_ready, 1)


def conv_phase(nc, T, sem, layer, conv_w):
    with ExitStack() as ctx:
        def sb(name, shape):
            return ctx.enter_context(nc.sbuf_tensor(name, shape, F32))
        taps = sb("conv_taps", [P, 6, CONV_W])
        acc = sb("conv_acc", [P, 2, 6, SEQ])
        square = sb("conv_square", [P, 4, SEQ])
        root = sb("conv_root", [P, 2, 4, SEQ])
        ps = ctx.enter_context(nc.psum_tensor("ps_conv", [P, 8, BANK], F32))
        taps_in, chain, convolved, silu_done = sem("conv_taps_in"), sem("conv_chain"), sem("conv_done"), sem("conv_silu")
        squared, summed, eps_added, rooted = sem("conv_squared"), sem("conv_summed"), sem("conv_eps"), sem("conv_rooted")
        unit, turned = sem("conv_unit"), sem("conv_turned")
        block = ctx.enter_context(nc.Block())

        @block.sync
        def _(sp):
            for w in range(CONV_W):
                sp.dma_start(taps[:, :, w], conv_w[bass.ds(layer, 1), w, :]
                             .rearrange("a (c p) -> p (a c)", p=P)).then_inc(taps_in, 16)

        @block.vector
        def _(dve):
            link = linker(dve, chain)
            dve.wait_ge(taps_in, 64)
            for c in range(6):
                a, b = acc[:, 0, c, :], acc[:, 1, c, :]
                link(nc.vector.tensor_scalar(a, T.gdn_in[:, c, 0:SEQ], taps[:, c, 0:1], None, ALU.mult))
                link(nc.vector.scalar_tensor_tensor(b, T.gdn_in[:, c, 1:1 + SEQ], taps[:, c, 1:2], a, ALU.mult, ALU.add))
                link(nc.vector.scalar_tensor_tensor(a, T.gdn_in[:, c, 2:2 + SEQ], taps[:, c, 2:3], b, ALU.mult, ALU.add))
                nc.vector.scalar_tensor_tensor(b, T.gdn_in[:, c, 3:3 + SEQ], taps[:, c, 3:4], a, ALU.mult,
                                               ALU.add).then_inc(convolved, 1)
            for c in range(4):
                dve.wait_ge(silu_done, c + 1)
                nc.vector.tensor_tensor(square[:, c, :], T.gdn_fm[:, c, :], T.gdn_fm[:, c, :],
                                        ALU.mult).then_inc(squared, 1)
            for c in range(4):
                dve.wait_ge(summed, c + 1)
                nc.vector.tensor_scalar_add(root[:, 0, c, :], ps[:, c, :], EPS).then_inc(eps_added, 1)
            for c in range(4):
                dve.wait_ge(rooted, c + 1)
                link(nc.vector.reciprocal(root[:, 0, c, :], root[:, 1, c, :]))
                scale = HD ** -0.5 if c < 2 else 1.0
                nc.vector.scalar_tensor_tensor(T.gdn_fm[:, c, :], T.gdn_fm[:, c, :], scale, root[:, 0, c, :],
                                               ALU.mult, ALU.mult).then_inc(unit, 1)
            dve.wait_ge(unit, 4)
            nc.vector.tensor_copy(T.gdn_fm_odd[:, :, :], T.gdn_fm[HD:P, 0:4, :])
            for c in range(2):
                dve.wait_ge(turned, 2 + c + 1)
                nc.vector.tensor_copy(T.gdn_ktok[:, :, c * P:(c + 1) * P],
                                      ps[:, 6 + c, :].rearrange("p (t d) -> p t d", t=NT))

        @block.scalar
        def _(act):
            for c in range(6):
                act.wait_ge(convolved, c + 1)
                nc.scalar.activation(T.gdn_fm[:, c, :], acc[:, 1, c, :], ACT.Silu).then_inc(silu_done, 1)
            for c in range(4):
                act.wait_ge(eps_added, c + 1)
                nc.scalar.activation(root[:, 1, c, :], root[:, 0, c, :], ACT.Sqrt).then_inc(rooted, 1)
            for c in range(2):
                act.wait_ge(turned, c + 1)
                nc.scalar.activation(T.gdn_vtok[:, :, c * P:(c + 1) * P],
                                     ps[:, 4 + c, :].rearrange("p (t d) -> p t d", t=NT), ACT.Copy)

        @block.tensor
        def _(pe):
            for c in range(4):
                pe.wait_ge(squared, c + 1)
                nc.tensor.matmul(ps[:, c, :], T.const("headones"), square[:, c, :], start=True, stop=True).then_inc(summed, 1)
            pe.wait_ge(silu_done, 6)
            for c in range(2):
                for ti in range(NT):
                    last = nc.tensor.transpose(ps[:, 4 + c, tok(ti)], T.gdn_fm[:, 4 + c, tok(ti)], T.const("ident"))
                last.then_inc(turned, 1)
            pe.wait_ge(unit, 4)
            for c in range(2):
                for ti in range(NT):
                    last = nc.tensor.transpose(ps[:, 6 + c, tok(ti)], T.gdn_fm[:, 2 + c, tok(ti)], T.const("ident"))
                last.then_inc(turned, 1)


def gdn_phase(nc, T, sem, layer, norm_g):
    with ExitStack() as ctx:
        def sb(name, shape):
            return ctx.enter_context(nc.sbuf_tensor(name, shape, F32))

        HT = NT // 2

        def mats(name, tiles=HT):
            return sb(name, [P, tiles, NH, P])
        AT, LT, attnT = mats("gdn_AT"), mats("gdn_LT"), mats("gdn_attnT", NT)
        D, DT = [mats("gdn_D0"), mats("gdn_D1")], [mats("gdn_DT0"), mats("gdn_DT1")]
        X, XT = [mats("gdn_X0"), mats("gdn_X1")], [mats("gdn_XT0"), mats("gdn_XT1")]
        grow = sb("gdn_grow", [P, 2, NH, SEQ])
        work = sb("gdn_work", [P, 3, NH, P])
        expo = sb("gdn_expo_buf", [P, 3, NH, P])
        vb, kb, kd = (sb(f"gdn_{n}", [P, NT, NH, HD]) for n in ("vb", "kb", "kd"))
        U = sb("gdn_U", [P, NT, NH, HD])
        WT = sb("gdn_WT", [HD, NT, NH, P])
        os_ = T.mix[:, :, 2 * GW:3 * GW].rearrange("p t (h d) -> p t h d", h=NH)
        qdec = sb("gdn_qdec", [HD, NH, SEQ])
        state = sb("gdn_state", [HD, 2, NH, HD])
        vnew = sb("gdn_vnew", [P, 2, NH, HD])
        end = sb("gdn_end", [HD, NH, NT])
        gain = sb("gdn_gain", [P, HD])
        stat = sb("gdn_stat", [P, 4, NT, NH])
        ps = ctx.enter_context(nc.psum_tensor("ps_gdn", [P, 8, BANK], F32))
        gain_in, bcast, bcast_out = sem("gdn_gain_in"), sem("gdn_bcast"), sem("gdn_bcast_out")
        grams, args_ready, expo_ready, amats = sem("gdn_grams"), sem("gdn_args"), sem("gdn_expo"), sem("gdn_amats")
        chain, product, taken, lt_ready = sem("gdn_chain"), sem("gdn_product"), sem("gdn_taken"), sem("gdn_lt_ready")
        exp_rows, scaled, qdec_ready = sem("gdn_exp_rows"), sem("gdn_scaled"), sem("gdn_qdec_ready")
        uw_mm, uw_out, silu_done = sem("gdn_uw_mm"), sem("gdn_uw_out"), sem("gdn_silu")
        old_mm, vnew_ready, out_mm, out_taken = sem("gdn_old_mm"), sem("gdn_vnew_ready"), sem("gdn_out_mm"), sem("gdn_out_taken")
        mean_ready, root_ready = sem("gdn_mean"), sem("gdn_root")
        block = ctx.enter_context(nc.Block())

        def fm(kind, h, cols):
            c = 2 * kind + h // 2
            return T.gdn_fm[0:HD, c, cols] if h % 2 == 0 else T.gdn_fm_odd[:, c, cols]

        steps = []
        a, xi = 0, 0
        for _ in range(3):
            b = 1 - a
            steps += [(DT[a], D[a], D[b], None, 1.0), (D[a], DT[a], DT[b], None, 1.0),
                      (DT[b], X[xi], X[1 - xi], X[xi], 1.0), (X[xi], DT[b], XT[1 - xi], XT[xi], 1.0)]
            a, xi = b, 1 - xi
        Y = D[1 - a]
        level_steps = []
        for width in (16, 32, 64):
            level_steps.append(len(steps))
            steps.append((LT, X[xi], Y, None, 1.0))
            if width < 64:
                steps.append((XT[xi], Y, X[1 - xi], X[xi], -1.0))
            steps.append((Y, XT[xi], XT[1 - xi], XT[xi], -1.0))
            xi = 1 - xi
        inv_t = XT[xi]
        n_steps = len(steps)

        @block.sync
        def _(sp):
            sp.dma_start(gain[:, :], norm_g[bass.ds(layer, 1), :].to_broadcast([P, HD])).then_inc(gain_in, 16)

        @block.tensor
        def _(pe):
            for n in range(2 * NH):
                nc.tensor.matmul(ps[:, n, :], T.head_row(n % NH), T.rows[:, 1 + n // NH, :],
                                 start=True, stop=True).then_inc(bcast, 1)
            pe.wait_ge(bcast_out, 2 * NH)
            for half in range(2):
                if half:
                    pe.wait_ge(uw_out, 2 * HT)
                for tj in range(HT):
                    ti = HT * half + tj
                    for h in range(NH):
                        k = fm(1, h, tok(ti))
                        nc.tensor.matmul(ps[:, 4 + 2 * tj, h * P:(h + 1) * P], k, k, start=True, stop=True)
                    for h in range(NH):
                        last = nc.tensor.matmul(ps[:, 5 + 2 * tj, h * P:(h + 1) * P], fm(1, h, tok(ti)),
                                                fm(0, h, tok(ti)), start=True, stop=True)
                    last.then_inc(grams, 1)
                pe.wait_ge(amats, HT * (half + 1))
                for m, (left_t, right, _, _, _) in enumerate(steps):
                    n = n_steps * half + m
                    for tj in range(HT):
                        if m >= 1:
                            pe.wait_ge(taken, HT * (n - 1) + tj + 1)
                        if m in level_steps:
                            pe.wait_ge(lt_ready, HT * (len(level_steps) * half + level_steps.index(m)) + tj + 1)
                        for h in range(NH):
                            last = nc.tensor.matmul(ps[:, 2 * (m % 2) + tj, h * P:(h + 1) * P], left_t[:, tj, h, :],
                                                    right[:, tj, h, :], start=True, stop=True)
                        last.then_inc(product, 1)
                pe.wait_ge(taken, HT * n_steps * (half + 1))
                pe.wait_ge(scaled, 3)
                for tj in range(HT):
                    ti = HT * half + tj
                    for h in range(NH):
                        nc.tensor.matmul(ps[:, 4 + 2 * tj, h * HD:(h + 1) * HD], inv_t[:, tj, h, :], vb[:, ti, h, :],
                                         start=True, stop=True)
                        last = nc.tensor.matmul(ps[0:HD, 5 + 2 * tj, h * P:(h + 1) * P], kb[:, ti, h, :],
                                                inv_t[:, tj, h, :], start=True, stop=True)
                    last.then_inc(uw_mm, 1)
            pe.wait_ge(qdec_ready, 1)
            pe.wait_ge(uw_out, 2 * NT)
            for ti in range(NT):
                old = state[:, (ti + 1) % 2, :, :]
                if ti > 0:
                    pe.wait_ge(out_taken, 2 * ti)
                    for h in range(NH):
                        last = nc.tensor.matmul(ps[:, 0, h * HD:(h + 1) * HD], WT[:, ti, h, :], old[:, h, :],
                                                start=True, stop=True)
                    last.then_inc(old_mm, 1)
                pe.wait_ge(vnew_ready, ti + 1)
                for h in range(NH):
                    if ti > 0:
                        nc.tensor.matmul(ps[:, 1, h * HD:(h + 1) * HD], qdec[:, h, tok(ti)], old[:, h, :],
                                         start=True, stop=False)
                    last = nc.tensor.matmul(ps[:, 1, h * HD:(h + 1) * HD], attnT[:, ti, h, :], vnew[:, ti % 2, h, :],
                                            start=(ti == 0), stop=True)
                last.then_inc(out_mm, 1)
                for h in range(NH):
                    last = nc.tensor.matmul(ps[0:HD, 2, h * HD:(h + 1) * HD], kd[:, ti, h, :], vnew[:, ti % 2, h, :],
                                            start=True, stop=True)
                last.then_inc(out_mm, 1)

        @block.scalar
        def _(act):
            def take_uw(half):
                for tj in range(HT):
                    ti = HT * half + tj
                    act.wait_ge(uw_mm, ti + 1)
                    nc.scalar.activation(U[:, ti, :, :], ps[:, 4 + 2 * tj, 0:GW].rearrange("p (h d) -> p h d", h=NH),
                                         ACT.Copy).then_inc(uw_out, 1)
                    nc.scalar.activation(WT[:, ti, :, :], ps[0:HD, 5 + 2 * tj, :]
                                         .rearrange("p (h t) -> p h t", h=NH), ACT.Copy).then_inc(uw_out, 1)
            for n in range(2 * NH):
                act.wait_ge(bcast, n + 1)
                nc.scalar.activation(grow[:, n // NH, n % NH, :], ps[:, n, :], ACT.Copy).then_inc(bcast_out, 1)
            act.wait_ge(bcast_out, 2 * NH)
            nc.scalar.activation(qdec[:, :, :], grow[0:HD, 0, :, :], ACT.Exp).then_inc(exp_rows, 1)
            nc.scalar.activation(end[:, :, :], grow[0:HD, 0, :, P - 1::P], ACT.Exp).then_inc(exp_rows, 1)
            for ti in range(NT):
                if ti == HT:
                    take_uw(0)
                act.wait_ge(args_ready, ti + 1)
                if ti >= 1:
                    act.wait_ge(amats, ti)
                for h in range(NH):
                    nc.scalar.activation(expo[:, 0, h, :], work[:, 0, h, :], ACT.Exp, bias=T.cols[:, C_R, ti, h:h + 1])
                    nc.scalar.activation(expo[:, 1, h, :], work[:, 1, h, :], ACT.Exp, bias=T.neg_gc[:, ti, h:h + 1])
                    last = nc.scalar.activation(expo[:, 2, h, :], work[:, 2, h, :], ACT.Exp,
                                                bias=T.neg_gc[:, ti, h:h + 1])
                last.then_inc(expo_ready, 1)
            take_uw(1)
            act.wait_ge(mean_ready, 1)
            nc.scalar.activation(stat[:, 2, :, :], stat[:, 1, :, :], ACT.Sqrt).then_inc(root_ready, 1)
            act.wait_ge(root_ready, 1)
            nc.scalar.activation(vb[:, :, :, :], T.gdn_gates[:, :, 2 * NH:2 * NH + GW]
                                 .rearrange("p t (h d) -> p t h d", h=NH), ACT.Silu).then_inc(silu_done, 1)

        @block.vector
        def _(dve):
            link = linker(dve, chain)

            def heads(t, n=P):
                return t.unsqueeze(1).to_broadcast([P, NH, n])
            ktok = T.gdn_ktok[:, :, :].rearrange("p t (h d) -> p t h d", h=NH)
            vtok = T.gdn_vtok[:, :, :].rearrange("p t (h d) -> p t h d", h=NH)
            for out, src, col in ((vb, vtok, C_LB), (kb, ktok, C_R), (kd, ktok, C_KD)):
                for ti in range(NT):
                    last = nc.vector.tensor_tensor(out[:, ti, :, :], src[:, ti, :, :], T.exp_cols[:, col, ti, :]
                                                   .unsqueeze(2).to_broadcast([P, NH, HD]), ALU.mult)
                last.then_inc(scaled, 1)
            dve.wait_ge(exp_rows, 2)
            for h in range(NH):
                last = nc.vector.tensor_tensor(qdec[:, h, :], qdec[:, h, :], fm(0, h, slice(0, SEQ)), ALU.mult)
            last.then_inc(qdec_ready, 1)
            dve.wait_ge(bcast_out, 2 * NH)
            for half in range(2):
                if half:
                    dve.wait_ge(uw_mm, HT)
                for tj in range(HT):
                    ti = HT * half + tj
                    if ti >= 1:
                        dve.wait_ge(expo_ready, ti)
                    gc, r = grow[:, 0, :, tok(ti)], grow[:, 1, :, tok(ti)]
                    link(nc.vector.tensor_scalar_mul(work[:, 0, :, :], gc, -1.0))
                    nc.vector.tensor_tensor(work[:, 1, :, :], r, heads(T.const("mask_strict_t")), ALU.add)
                    nc.vector.tensor_tensor(work[:, 2, :, :], gc, heads(T.const("mask_t")), ALU.add)
                    link(nc.vector.tensor_tensor(work[:, 0, :, :], work[:, 0, :, :], heads(T.const("mask_strict")), ALU.add))
                    nc.vector.engine_nop().then_inc(args_ready, 1)
                    dve.wait_ge(grams, ti + 1)
                    dve.wait_ge(expo_ready, ti + 1)
                    gram = ps[:, 4 + 2 * tj, :].rearrange("p (h c) -> p h c", h=NH)
                    qk = ps[:, 5 + 2 * tj, :].rearrange("p (h c) -> p h c", h=NH)
                    diag, ident = heads(T.const("diag16")), heads(T.const("ident"))
                    nc.vector.tensor_tensor(AT[:, tj, :, :], gram, expo[:, 1, :, :], ALU.mult)
                    nc.vector.tensor_tensor(attnT[:, ti, :, :], qk, expo[:, 2, :, :], ALU.mult)
                    link(nc.vector.tensor_tensor(D[0][:, tj, :, :], gram, expo[:, 0, :, :], ALU.mult))
                    nc.vector.tensor_tensor(DT[0][:, tj, :, :], AT[:, tj, :, :], diag, ALU.mult)
                    link(nc.vector.tensor_tensor(D[0][:, tj, :, :], D[0][:, tj, :, :], diag, ALU.mult))
                    nc.vector.tensor_tensor(X[0][:, tj, :, :], ident, D[0][:, tj, :, :], ALU.subtract)
                    nc.vector.tensor_tensor(XT[0][:, tj, :, :], ident, DT[0][:, tj, :, :], ALU.subtract)
                    nc.vector.tensor_tensor(LT[:, tj, :, :], AT[:, tj, :, :], heads(T.const("below16_t")),
                                            ALU.mult).then_inc(lt_ready, 1)
                    dve.wait_ge(lt_ready, HT * len(level_steps) * half + tj + 1)
                    nc.vector.engine_nop().then_inc(amats, 1)
                for m, (_, _, out, old, sign) in enumerate(steps):
                    n = n_steps * half + m
                    for tj in range(HT):
                        dve.wait_ge(product, HT * n + tj + 1)
                        src = ps[:, 2 * (m % 2) + tj, :].rearrange("p (h c) -> p h c", h=NH)
                        if old is None:
                            nc.vector.tensor_copy(out[:, tj, :, :], src).then_inc(taken, 1)
                        else:
                            nc.vector.tensor_tensor(out[:, tj, :, :], old[:, tj, :, :], src,
                                                    ALU.add if sign > 0 else ALU.subtract).then_inc(taken, 1)
                    if m in level_steps[:-1]:
                        width = 32 << level_steps.index(m)
                        for tj in range(HT):
                            nc.vector.tensor_tensor(LT[:, tj, :, :], AT[:, tj, :, :], heads(T.const(f"below{width}_t")),
                                                    ALU.mult).then_inc(lt_ready, 1)
            dve.wait_ge(uw_out, 2 * NT)
            for ti in range(NT):
                new, old = state[:, ti % 2, :, :], state[:, (ti + 1) % 2, :, :]
                if ti == 0:
                    nc.vector.tensor_copy(vnew[:, 0, :, :], U[:, 0, :, :]).then_inc(vnew_ready, 1)
                else:
                    dve.wait_ge(old_mm, ti)
                    nc.vector.tensor_tensor(vnew[:, ti % 2, :, :], U[:, ti, :, :],
                                            ps[:, 0, 0:GW].rearrange("p (h d) -> p h d", h=NH),
                                            ALU.subtract).then_inc(vnew_ready, 1)
                dve.wait_ge(out_mm, 2 * ti + 1)
                nc.vector.tensor_copy(os_[:, ti, :, :],
                                      ps[:, 1, 0:GW].rearrange("p (h d) -> p h d", h=NH)).then_inc(out_taken, 1)
                dve.wait_ge(out_mm, 2 * ti + 2)
                added = ps[0:HD, 2, 0:GW].rearrange("p (h d) -> p h d", h=NH)
                if ti == 0:
                    nc.vector.tensor_copy(new, added).then_inc(out_taken, 1)
                else:
                    for h in range(NH):
                        last = nc.vector.scalar_tensor_tensor(new[:, h, :], old[:, h, :], end[:, h, ti:ti + 1],
                                                              added[:, h, :], ALU.mult, ALU.add)
                    last.then_inc(out_taken, 1)
                dve.wait_ge(out_taken, 2 * ti + 2)
            dve.wait_ge(gain_in, 16)
            square, normed = kb[:, :, :, :], kd[:, :, :, :]
            merged = "p t h d -> p (t h) d"
            head_norm(nc, dve, (mean_ready, root_ready), link, os_[:, :, :, :], square, stat,
                      gain[:, :].unsqueeze(1).to_broadcast([P, NT * NH, HD]), normed.rearrange(merged))
            dve.wait_ge(silu_done, 1)
            nc.vector.tensor_tensor(T.mix[:, :, 2 * GW:3 * GW].rearrange("p t (h d) -> p t h d", h=NH), normed,
                                    vb[:, :, :, :], ALU.mult)


def output_phase(nc, T, sem, layer, w_out):
    with ExitStack() as ctx:
        w = ctx.enter_context(nc.sbuf_tensor("w_out_buf", [P, KD, D_MODEL], F32))
        mixT = ctx.enter_context(nc.sbuf_tensor("mixT", [P, KD, SEQ], F32))
        ps = ctx.enter_context(nc.psum_tensor("ps_outp", [P, 8, BANK], F32))
        w_in, turned, turned_act, turned_dve = sem("w_out_in"), sem("mix_turned"), sem("mix_act"), sem("mix_dve")
        product = sem("outp_product")
        block = ctx.enter_context(nc.Block())

        @block.sync
        def _(sp):
            sp.dma_start(w[:, :, :], w_out[bass.ds(layer, 1), :, :]
                         .rearrange("a (k p) c -> p (a k) c", p=P)).then_inc(w_in, 16)

        @block.tensor
        def _(pe):
            for k in range(KD):
                for ti in range(NT):
                    last = nc.tensor.transpose(ps[:, k, tok(ti)], T.mix[:, ti, k * P:(k + 1) * P], T.const("ident"))
                last.then_inc(turned, 1)
            pe.wait_ge(turned_act, KD // 2)
            pe.wait_ge(turned_dve, KD // 2)
            pe.wait_ge(w_in, 16)
            for n in range(8):
                ti, half = n // 2, n % 2
                for k in range(KD):
                    last = nc.tensor.matmul(ps[:, n, :], mixT[:, k, tok(ti)], w[:, k, half * BANK:(half + 1) * BANK],
                                            start=(k == 0), stop=(k == KD - 1))
                last.then_inc(product, 1)

        @block.scalar
        def _(act):
            for k in range(0, KD, 2):
                act.wait_ge(turned, k + 1)
                nc.scalar.activation(mixT[:, k, :], ps[:, k, :], ACT.Copy).then_inc(turned_act, 1)

        @block.vector
        def _(dve):
            for k in range(1, KD, 2):
                dve.wait_ge(turned, k + 1)
                nc.vector.tensor_copy(mixT[:, k, :], ps[:, k, :]).then_inc(turned_dve, 1)
            for n in range(8):
                dve.wait_ge(product, n + 1)
                r = T.resid[:, n // 2, (n % 2) * BANK:(n % 2 + 1) * BANK]
                nc.vector.tensor_tensor(r, r, ps[:, n, :], ALU.add)


def query_phase(nc, T, sem, layer, w_q, sub_keys):
    PC = 2 * PH
    with ExitStack() as ctx:
        wbuf = ctx.enter_context(nc.sbuf_tensor("w_q_buf", [P, 2, KD, BANK], F32))
        keys = ctx.enter_context(nc.sbuf_tensor("sub_keys", [P, PC, P], F32))
        ps = ctx.enter_context(nc.psum_tensor("ps_query", [P, 8, BANK], F32))
        keys_in, w_in = sem("sub_keys_in"), [sem(f"w_q_in{g}") for g in range(4)]
        turned, turned_out, product = sem("sub_keys_turned"), sem("sub_keys_out"), sem("query_product")
        out_act, out_dve = sem("query_act"), sem("query_dve")
        block = ctx.enter_context(nc.Block())

        @block.sync
        def _(sp):
            for h in range(0, PH, PH // 2):
                sp.dma_start(keys[:, 2 * h:2 * h + PH, :], sub_keys[bass.ds(layer, 1), h:h + PH // 2, :, :, :]
                             .rearrange("a p c n d -> n (a p c) d")).then_inc(keys_in, 16)
            for g in range(4):
                if g >= 2:
                    sp.wait_ge(product, 4 * (g - 1))
                sp.dma_start(wbuf[:, g % 2, :, :], w_q[bass.ds(layer, 1), :, g * BANK:(g + 1) * BANK]
                             .rearrange("a (k p) c -> p (a k) c", p=P)).then_inc(w_in[g], 16)

        @block.tensor
        def _(pe):
            pe.wait_ge(keys_in, 32)
            for b in range(4):
                for i in range(4):
                    last = nc.tensor.transpose(ps[:, b, tok(i)], keys[:, 4 * b + i, :], T.const("ident"))
                last.then_inc(turned, 1)
            for n in range(PC):
                if n % 4 == 0:
                    pe.wait_ge(w_in[n // 4], 16)
                if n < 4:
                    pe.wait_ge(turned_out, n + 1)
                if n >= 8:
                    pe.wait_ge(out_act if n % 2 == 0 else out_dve, (n - 8) // 2 + 1)
                for k in range(KD):
                    last = nc.tensor.matmul(ps[:, n % 8, :], wbuf[:, (n // 4) % 2, k, tok(n % 4)], T.xnT[:, k, :],
                                            start=(k == 0), stop=(k == KD - 1))
                last.then_inc(product, 1)

        @block.scalar
        def _(act):
            for n in range(0, PC, 2):
                act.wait_ge(product, n + 1)
                nc.scalar.activation(T.peer_q[:, n, :], ps[:, n % 8, :], ACT.Copy).then_inc(out_act, 1)

        @block.vector
        def _(dve):
            for b in range(4):
                dve.wait_ge(turned, b + 1)
                nc.vector.tensor_copy(T.peer_k[:, 4 * b:4 * b + 4, :],
                                      ps[:, b, :].rearrange("p (i n) -> p i n", i=4)).then_inc(turned_out, 1)
            for n in range(1, PC, 2):
                dve.wait_ge(product, n + 1)
                nc.vector.tensor_copy(T.peer_q[:, n, :], ps[:, n % 8, :]).then_inc(out_dve, 1)


def select_phase(nc, T, sem):
    PC = 2 * PH
    LOW = -3.0e38
    with ExitStack() as ctx:
        def sb(name, shape, dtype=F32):
            return ctx.enter_context(nc.sbuf_tensor(name, shape, dtype))
        rest = sb("sel_rest", [P, PC, NK])
        best = sb("sel_best", [P, PC, TOPK])
        where = sb("sel_where", [P, PC, TOPK], U32)
        where_f = sb("sel_where_f", [P, PC, TOPK])
        cand = sb("sel_cand", [P, PH, TOPK * TOPK])
        cand_rest = sb("sel_cand_rest", [P, PH, TOPK * TOPK])
        top = sb("sel_top", [P, PH, TOPK])
        at = sb("sel_at", [P, PH, TOPK], U32)
        at_half = sb("sel_at_half", [P, 2, PH, TOPK], U32)
        at_f = sb("sel_at_f", [P, 2, PH, TOPK])
        same = sb("sel_same", [P, PH * TOPK, TOPK])
        chosen = sb("sel_chosen", [P, 3, PH, TOPK])
        shifted = sb("sel_shifted", [P, PH, TOPK])
        expd = sb("sel_exp", [P, PH, TOPK])
        total = sb("sel_total", [P, 2, PH])
        ps = ctx.enter_context(nc.psum_tensor("ps_select", [P, 4, BANK], F32))
        ps_t = ctx.enter_context(nc.psum_tensor("ps_pick", [P, 2, BANK], F32))
        scored, read, chain, shifted_ready = sem("sel_scored"), sem("sel_read"), sem("sel_chain"), sem("sel_shifted")
        exp_done, chosen_ready, turned, turned_out = (sem("sel_exp_done"), sem("sel_chosen"), sem("sel_turned"),
                                                      sem("sel_turned_out"))
        block = ctx.enter_context(nc.Block())

        @block.tensor
        def _(pe):
            for ti in range(NT + 1):
                if ti < NT:
                    if ti >= 1:
                        pe.wait_ge(read, ti)
                    for pc in range(PC):
                        last = nc.tensor.matmul(ps[:, pc // 4, tok(pc % 4)], T.peer_q[:, pc, tok(ti)],
                                                T.peer_k[:, pc, :], start=True, stop=True)
                    last.then_inc(scored, 1)
                if ti >= 1:
                    pe.wait_ge(chosen_ready, ti)
                    for c in range(3):
                        last = nc.tensor.transpose(ps_t[:, (ti - 1) % 2, tok(c)],
                                                   chosen[:, c, :, :].rearrange("p h k -> p (h k)"), T.const("ident"))
                    last.then_inc(turned, 1)

        @block.scalar
        def _(act):
            for ti in range(NT):
                act.wait_ge(shifted_ready, ti + 1)
                nc.scalar.activation(expd[:, :, :], shifted[:, :, :], ACT.Exp).then_inc(exp_done, 1)
                act.wait_ge(turned, ti + 1)
                nc.scalar.activation(T.pick[:, :, tok(ti)],
                                     ps_t[:, ti % 2, 0:3 * P].rearrange("p (c t) -> p c t", c=3),
                                     ACT.Copy).then_inc(turned_out, 1)

        @block.vector
        def _(dve):
            link = linker(dve, chain)
            for ti in range(NT):
                dve.wait_ge(scored, ti + 1)

                def score(pc):
                    return ps[:, pc // 4, tok(pc % 4)]
                for pc in range(PC):
                    last = nc.vector.max(best[:, pc, 0:8], score(pc))
                link(last)
                for pc in range(PC):
                    nc.vector.max_index(where[:, pc, 0:8], best[:, pc, 0:8], score(pc))
                    last = nc.vector.match_replace(rest[:, pc, :], best[:, pc, 0:8], score(pc), LOW)
                last.then_inc(read, 1)
                dve.wait_ge(read, ti + 1)
                for pc in range(PC):
                    last = nc.vector.max(best[:, pc, 8:16], rest[:, pc, :])
                link(last)
                for pc in range(PC):
                    last = nc.vector.max_index(where[:, pc, 8:16], best[:, pc, 8:16], rest[:, pc, :])
                link(last)
                link(nc.vector.tensor_copy(where_f[:, :, :], where[:, :, :]))
                pair = best[:, :, :].rearrange("p (h c) k -> p c h k", c=2)
                link(nc.vector.tensor_tensor(cand[:, :, :].rearrange("p h (a b) -> p h a b", a=TOPK),
                                             pair[:, 0].unsqueeze(3).to_broadcast([P, PH, TOPK, TOPK]),
                                             pair[:, 1].unsqueeze(2).to_broadcast([P, PH, TOPK, TOPK]), ALU.add))
                for h in range(PH):
                    last = nc.vector.max(top[:, h, 0:8], cand[:, h, :])
                link(last)
                for h in range(PH):
                    nc.vector.max_index(at[:, h, 0:8], top[:, h, 0:8], cand[:, h, :])
                    last = nc.vector.match_replace(cand_rest[:, h, :], top[:, h, 0:8], cand[:, h, :], LOW)
                link(last)
                for h in range(PH):
                    last = nc.vector.max(top[:, h, 8:16], cand_rest[:, h, :])
                link(last)
                if ti >= 1:
                    dve.wait_ge(exp_done, ti)
                nc.vector.tensor_tensor(shifted[:, :, :], top[:, :, :],
                                        top[:, :, 0:1].to_broadcast([P, PH, TOPK]), ALU.subtract).then_inc(shifted_ready, 1)
                for h in range(PH):
                    last = nc.vector.max_index(at[:, h, 8:16], top[:, h, 8:16], cand_rest[:, h, :])
                link(last)
                nc.vector.tensor_single_scalar(at_half[:, 0, :, :], at[:, :, :], 4, ALU.logical_shift_right)
                link(nc.vector.tensor_single_scalar(at_half[:, 1, :, :], at[:, :, :], TOPK - 1, ALU.bitwise_and))
                link(nc.vector.tensor_copy(at_f[:, :, :, :], at_half[:, :, :, :]))
                if ti >= 1:
                    dve.wait_ge(turned, ti)
                ranks = T.const("iota")[:, 0:TOPK].unsqueeze(1).to_broadcast([P, PH * TOPK, TOPK])
                numbers = where_f[:, :, :].rearrange("p (h c) k -> p c h k", c=2)
                for c in range(2):
                    link(nc.vector.tensor_tensor(same[:, :, :], at_f[:, c, :, :].rearrange("p h k -> p (h k)")
                                                 .unsqueeze(2).to_broadcast([P, PH * TOPK, TOPK]), ranks, ALU.is_equal))
                    by_head = same[:, :, :].rearrange("p (h k) r -> p h k r", h=PH)
                    link(nc.vector.tensor_tensor(by_head, by_head, numbers[:, c].unsqueeze(2)
                                                 .to_broadcast([P, PH, TOPK, TOPK]), ALU.mult))
                    link(nc.vector.tensor_reduce(chosen[:, c, :, :].rearrange("p h k -> p (h k)"), same[:, :, :],
                                                 AX.X, ALU.add))
                dve.wait_ge(exp_done, ti + 1)
                link(nc.vector.tensor_reduce(total[:, 0, :], expd[:, :, :], AX.X, ALU.add))
                link(nc.vector.reciprocal(total[:, 1, :], total[:, 0, :]))
                nc.vector.tensor_tensor(chosen[:, 2, :, :], expd[:, :, :],
                                        total[:, 1, :].unsqueeze(2).to_broadcast([P, PH, TOPK]),
                                        ALU.mult).then_inc(chosen_ready, 1)


def gate_map_phase(nc, T, sem, gates_dram):
    TG = 4
    GROUPS_IN = P // TG
    with ExitStack() as ctx:
        first = ctx.enter_context(nc.sbuf_tensor("map_first", [P, 2, TG, NK], F32))
        second = ctx.enter_context(nc.sbuf_tensor("map_second", [P, 2, TG, NK], F32))
        tile = ctx.enter_context(nc.sbuf_tensor("map_tile", [P, 2, NK, P], F32))
        ps = ctx.enter_context(nc.psum_tensor("ps_map", [P, 2, BANK], F32))
        hot_free, bank_free = sem("map_hot_free"), sem("map_bank_free")
        hot_ready = sem("map_hot_ready")
        stored = [sem("map_stored0"), sem("map_stored1")]
        block = ctx.enter_context(nc.Block())

        def columns(ti, it, u):
            return bass.ds(it * (2 * TG) + (P * ti + TG * u), TG)

        @block.vector
        def _(dve):
            dve.sem_inc(hot_free, 2)
            for ti in range(NT):
                with dve.Fori(0, GROUPS_IN // 2) as it:
                    for u in range(2):
                        n = it * 2 + (GROUPS_IN * ti + u)
                        dve.wait_ge(hot_free, n + 1)
                        for i in range(TG):
                            t = it * (2 * TG) + (P * ti + TG * u + i)
                            nc.vector.tensor_scalar(first[:, u, i, :], T.const("iota"),
                                                    T.pick[:, 0, bass.ds(t, 1)], None, ALU.is_equal)
                            last = nc.vector.tensor_scalar(second[:, u, i, :], T.const("iota"),
                                                           T.pick[:, 1, bass.ds(t, 1)], T.pick[:, 2, bass.ds(t, 1)],
                                                           ALU.is_equal, ALU.mult)
                        last.then_inc(hot_ready, 1)

        @block.tensor
        def _(pe):
            for ti in range(NT):
                with pe.Fori(0, GROUPS_IN // 2) as it:
                    for u in range(2):
                        n = it * 2 + (GROUPS_IN * ti + u)
                        pe.wait_ge(hot_ready, n + 1)
                        pe.wait_ge(bank_free, n + 1)
                        for i in range(TG):
                            last = nc.tensor.matmul(ps[:, u, tok(i)], first[:, u, i, :], second[:, u, i, :],
                                                    start=True, stop=True)
                        last.then_inc(hot_free, 1)

        @block.scalar
        def _(act):
            act.sem_inc(bank_free, 2)
            for ti in range(NT):
                if ti >= 2:
                    act.wait_ge(stored[ti % 2], 16)
                with act.Fori(0, GROUPS_IN // 2) as it:
                    for u in range(2):
                        n = it * 2 + (GROUPS_IN * ti + u)
                        act.wait_ge(hot_free, n + 3)
                        nc.scalar.activation(tile[:, ti % 2, :, bass.ds(it * (2 * TG) + TG * u, TG)],
                                             ps[:, u, :].rearrange("p (t j) -> p j t", t=TG),
                                             ACT.Copy).then_inc(bank_free, 1)

        @block.sync
        def _(sp):
            for ti in range(NT):
                sp.wait_ge(bank_free, 2 + GROUPS_IN * (ti + 1))
                sp.dma_start(gates_dram[:, :, tok(ti)], tile[:, ti % 2, :, :]).then_inc(stored[ti % 2], 16)
            for s in stored:
                sp.wait_ge(s, 32)


def expert_phase(nc, T, sem, layer, u_tab, v_tab, gates_dram):
    GE = 4
    N_GROUPS = NK // GE
    with ExitStack() as ctx:
        def sb(name, shape):
            return ctx.enter_context(nc.sbuf_tensor(name, shape, F32))
        u_buf = sb("u_buf", [P, 2, GE, D_MODEL])
        v_buf = sb("v_buf", [P, 2, GE, D_MODEL])
        g_buf = sb("g_buf", [P, 2, GE, SEQ])
        uT = sb("uT", [P, 2, KD, P])
        hidden = sb("hidden", [P, 2, SEQ])
        weight = sb("weight", [P, 2, GE, SEQ])
        ps_u = ctx.enter_context(nc.psum_tensor("ps_uT", [P, 2, 2, BANK], F32))
        ps_h = ctx.enter_context(nc.psum_tensor("ps_hidden", [P, 2, BANK], F32))
        ps_y = ctx.enter_context(nc.psum_tensor("ps_y", [P, 2, BANK], F32))
        u_in, v_in, g_in = ([sem(f"{x}_in{i}") for i in range(2)] for x in "uvg")
        turned_out_act, turned_out_dve = sem("uT_out_act"), sem("uT_out_dve")
        turned, hidden_mm, hidden_done = sem("uT_turned"), sem("hidden_mm"), sem("hidden_done")
        weight_ready, y_mm, y_added = sem("weight_ready"), sem("y_mm"), sem("y_added")
        block = ctx.enter_context(nc.Block())

        def tiles(it, u, e):
            return it * (2 * GE) + (GE * u + e), it * 2 + u
        u_by_key = u_tab.rearrange("l (i j) d -> l i j d", j=NK)
        v_by_key = v_tab.rearrange("l (i j) d -> l i j d", j=NK)

        @block.sync
        def _(sp):
            sp.sem_inc(y_mm, 2 * 2 * NT)
            with sp.Fori(0, N_GROUPS // 2) as it:
                for u in range(2):
                    _, g = tiles(it, u, 0)
                    sp.wait_ge(y_mm, g * (2 * NT) + 2 * NT)
                    cols = bass.ds(it * (2 * GE) + GE * u, GE)
                    for buf, src, loaded in ((u_buf, u_by_key, u_in), (v_buf, v_by_key, v_in)):
                        sp.dma_start(buf[:, u, :, :], src[bass.ds(layer, 1), :, cols, :]
                                     .rearrange("a i j d -> i (a j) d")).then_inc(loaded[u], 16)
                    sp.dma_start(g_buf[:, u, :, :], gates_dram[:, cols, :]).then_inc(g_in[u], 16)

        @block.tensor
        def _(pe):
            pe.sem_inc(hidden_mm, 2)
            with pe.Fori(0, N_GROUPS // 2) as it:
                for u in range(2):
                    def turn(e):
                        n, _ = tiles(it, u, e)
                        pe.wait_ge(turned_out_act, n + 1)
                        pe.wait_ge(turned_out_dve, n + 1)
                        for k in range(KD):
                            last = nc.tensor.transpose(ps_u[:, e % 2, k // 4, tok(k % 4)],
                                                       u_buf[:, u, e, k * P:(k + 1) * P], T.const("ident"))
                        last.then_inc(turned, 1)

                    def hide(e):
                        n, _ = tiles(it, u, e)
                        pe.wait_ge(turned_out_act, n + 3)
                        pe.wait_ge(turned_out_dve, n + 3)
                        pe.wait_ge(hidden_done, n + 1)
                        for k in range(KD):
                            last = nc.tensor.matmul(ps_h[:, e % 2, :], uT[:, e % 2, k, :], T.xnT[:, k, :],
                                                    start=(k == 0), stop=(k == KD - 1))
                        last.then_inc(hidden_mm, 1)
                    pe.wait_ge(u_in[u], it * 16 + 16)
                    turn(0)
                    for e in range(GE):
                        if e + 1 < GE:
                            turn(e + 1)
                        hide(e)
                    pe.wait_ge(v_in[u], it * 16 + 16)
                    for b in range(2 * NT):
                        y = it * (4 * NT) + (2 * NT * u + b)
                        pe.wait_ge(y_added, y + 1)
                        for e in range(GE):
                            n, _ = tiles(it, u, e)
                            if b == 0:
                                pe.wait_ge(weight_ready, n + 3)
                            last = nc.tensor.matmul(ps_y[:, b % 2, :], weight[:, u, e, tok(b // 2)],
                                                    v_buf[:, u, e, (b % 2) * BANK:(b % 2 + 1) * BANK],
                                                    start=(e == 0), stop=(e == GE - 1))
                        last.then_inc(y_mm, 1)

        @block.scalar
        def _(act):
            act.sem_inc(turned_out_act, 2)
            act.sem_inc(hidden_done, 2)
            with act.Fori(0, N_GROUPS // 2) as it:
                for u in range(2):
                    def take(e):
                        n, _ = tiles(it, u, e)
                        act.wait_ge(turned, n + 1)
                        act.wait_ge(hidden_mm, n + 1)
                        nc.scalar.activation(uT[:, e % 2, 0:4, :].rearrange("p k n -> p (k n)"),
                                             ps_u[:, e % 2, 0, :], ACT.Copy).then_inc(turned_out_act, 1)
                    take(0)
                    for e in range(GE):
                        if e + 1 < GE:
                            take(e + 1)
                        n, _ = tiles(it, u, e)
                        act.wait_ge(hidden_mm, n + 3)
                        act.wait_ge(weight_ready, n + 1)
                        nc.scalar.activation(hidden[:, e % 2, :], ps_h[:, e % 2, :], ACT.Gelu).then_inc(hidden_done, 1)

        @block.vector
        def _(dve):
            dve.sem_inc(turned_out_dve, 2)
            dve.sem_inc(weight_ready, 2)
            dve.sem_inc(y_added, 2)
            with dve.Fori(0, N_GROUPS // 2) as it:
                for u in range(2):
                    def take(e):
                        n, _ = tiles(it, u, e)
                        dve.wait_ge(turned, n + 1)
                        dve.wait_ge(hidden_mm, n + 1)
                        nc.vector.tensor_copy(uT[:, e % 2, 4:8, :].rearrange("p k n -> p (k n)"),
                                              ps_u[:, e % 2, 1, :]).then_inc(turned_out_dve, 1)
                    take(0)
                    for e in range(GE):
                        if e + 1 < GE:
                            take(e + 1)
                        n, g = tiles(it, u, e)
                        if e == 0:
                            dve.wait_ge(g_in[u], it * 16 + 16)
                            dve.wait_ge(y_mm, g * (2 * NT) + 2 * NT)
                        dve.wait_ge(hidden_done, n + 3)
                        nc.vector.tensor_tensor(weight[:, u, e, :], hidden[:, e % 2, :], g_buf[:, u, e, :],
                                                ALU.mult).then_inc(weight_ready, 1)
                    for b in range(2 * NT):
                        y = it * (4 * NT) + (2 * NT * u + b)
                        dve.wait_ge(y_mm, y + 4 * NT + 1)
                        if b == 0:
                            dve.wait_ge(y_added, y + 2)
                        r = T.resid[:, b // 2, (b % 2) * BANK:(b % 2 + 1) * BANK]
                        nc.vector.tensor_tensor(r, r, ps_y[:, b % 2, :], ALU.add).then_inc(y_added, 1)


_INS = ["x", "positions", "t5_table", "norm1_g", "norm2_g", "final_norm_g", "w_in", "w_out", "nsa_w_cmp_k",
        "nsa_w_cmp_v", "nsa_cmp_pos", "mlstm_i_bias", "mlstm_f_bias", "mlstm_norm_g", "gdn_conv_w", "gdn_a_log",
        "gdn_dt_bias", "gdn_norm_g", "mla_q_norm_g", "mla_kv_norm_g", "mla_w_uq", "mla_w_ukv", "peer_w_q",
        "peer_sub_keys", "peer_u", "peer_v"]


def program(nc, ins, consts, out):
    T = Tensors()
    bias_dram = nc.dram_tensor("bias_by_distance", [NH, 640 + SEQ], F32, kind="Internal").ap()
    gates_dram = nc.dram_tensor("gates", [NK, NK, SEQ], F32, kind="Internal").ap()
    with ExitStack() as ctx:
        ctx.enter_context(nc.allow_non_contiguous_dma(reason="a few KB of gains, positions and taps"))
        def once(name):
            return ctx.enter_context(nc.semaphore(name))

        def semaphores(stack, kept):
            def sem(name):
                kept.append(stack.enter_context(nc.semaphore(name)))
                return kept[-1]
            return sem

        def zero(kept):
            with nc.Block() as block:
                @block.gpsimd
                def _(pool):
                    for s in kept:
                        pool.sem_clear(s)

        def sb(name, shape, where=None):
            return (where or ctx).enter_context(nc.sbuf_tensor(name, shape, F32))
        T.consts = sb("consts", [P, CONSTS_SHAPE[1] - SEQ])
        T.resid = sb("resid", [P, NT, D_MODEL])
        T.biasq = sb("biasq", [P, NH, SEQ])
        T.biasc = sb("biasc", [P, NH, NT, N_CMP])
        T.cossin = sb("cossin", [P, NT, 2, 16])

        def const(name, row=0, rows=P, width=None):
            at, full = CONST_COLS[name]
            return T.consts[row:row + rows, at:at + (width or full)]
        T.const = const
        T.head_row = lambda h: T.consts[0:NH, CONST_COLS["headrow"][0] + h * P:CONST_COLS["headrow"][0] + (h + 1) * P]
        setup_phase(nc, T, once, ins["x"], ins["positions"], ins["t5_table"], consts, bias_dram)

        def gain_columns(g, layer):
            return g[bass.ds(layer, 1), :].rearrange("a (k p) -> p (a k)", p=P)
        with nc.Fori(0, DEPTH) as layer:
            with ExitStack() as mixer:
                used = []
                sem = semaphores(mixer, used)
                T.mix = sb("mix", [P, NT, D_MODEL], mixer)
                T.gdn_gates = sb("gdn_gates", [P, NT, GW + 2 * NH], mixer)
                T.gdn_fm = sb("gdn_fm", [P, 6, SEQ], mixer)
                T.gdn_fm_odd = sb("gdn_fm_odd", [HD, 4, SEQ], mixer)
                T.gdn_ktok = sb("gdn_ktok", [P, NT, GW], mixer)
                T.gdn_vtok = sb("gdn_vtok", [P, NT, GW], mixer)
                T.cols = sb("cols", [P, 6, NT, NH], mixer)
                T.exp_cols = sb("exp_cols", [P, 6, NT, NH], mixer)
                T.neg_gc = sb("neg_gc", [P, NT, NH], mixer)
                T.rows = sb("rows", [NH, 3, SEQ], mixer)
                with ExitStack() as early:
                    T.nsa_q = sb("nsa_q", [HD, NH, SEQ], early)
                    T.cmp_kv = sb("cmp_kv", [HD, 2, SEQ], early)
                    T.nsa_k = sb("nsa_k", [HD, 2, SEQ], early)
                    T.nsa_tm = sb("nsa_tm", [P, NT, NSA_IN - 448], early)
                    T.ml_q = sb("ml_q", [HD, NH, SEQ], early)
                    T.ml_k = sb("ml_k", [HD, NH, SEQ], early)
                    T.ml_v = sb("ml_v", [P, NT, GW], early)
                    T.ml_gates = sb("ml_gates", [P, NT, GW + 2 * NH], early)
                    T.mla_tm = sb("mla_tm", [P, NT, MLA_IN], early)
                    with ExitStack() as s:
                        T.gdn_in = sb("gdn_in", [P, 6, SEQ + CONV_W - 1], s)
                        with ExitStack() as s2:
                            T.xnT = sb("xnT", [P, KD, SEQ], s2)
                            norm_phase(nc, T, sem, "norm1", gain_columns(ins["norm1_g"], layer))
                            projection_phase(nc, T, sem, layer, ins["w_in"])
                        conv_phase(nc, T, sem, layer, ins["gdn_conv_w"])
                    gate_phase(nc, T, sem, layer, ins["mlstm_i_bias"], ins["mlstm_f_bias"], ins["gdn_dt_bias"],
                               ins["gdn_a_log"])
                    with ExitStack() as s:
                        T.k_cmp = sb("k_cmp", [HD, N_CMP], s)
                        T.v_cmp = sb("v_cmp", [N_CMP, HD], s)
                        T.nsa_gate = sb("nsa_gate", [P, NT, 3 * NH], s)
                        T.mla_qk = sb("mla_qk", [QD, 2 * NH, SEQ], s)
                        T.mla_v = sb("mla_v", [P, NT, NH, HD], s)
                        compress_phase(nc, T, sem, layer, ins["nsa_w_cmp_k"], ins["nsa_w_cmp_v"], ins["nsa_cmp_pos"])
                        mla_phase(nc, T, sem, layer, ins["mla_q_norm_g"], ins["mla_kv_norm_g"], ins["mla_w_uq"],
                                  ins["mla_w_ukv"])
                        attention_phase(nc, T, sem)
                    mlstm_phase(nc, T, sem, layer, ins["mlstm_norm_g"])
                gdn_phase(nc, T, sem, layer, ins["gdn_norm_g"])
                output_phase(nc, T, sem, layer, ins["w_out"])
                zero(used)
            with ExitStack() as peer:
                used = []
                sem = semaphores(peer, used)
                T.xnT = sb("xn2T", [P, KD, SEQ], peer)
                norm_phase(nc, T, sem, "norm2", gain_columns(ins["norm2_g"], layer))
                with ExitStack() as maps:
                    T.pick = sb("pick", [P, 3, SEQ], maps)
                    with ExitStack() as s:
                        T.peer_q = sb("peer_q", [P, 2 * PH, SEQ], s)
                        T.peer_k = sb("peer_k", [P, 2 * PH, NK], s)
                        query_phase(nc, T, sem, layer, ins["peer_w_q"], ins["peer_sub_keys"])
                        select_phase(nc, T, sem)
                    gate_map_phase(nc, T, sem, gates_dram)
                expert_phase(nc, T, sem, layer, ins["peer_u"], ins["peer_v"], gates_dram)
                zero(used)
        final_phase(nc, T, once, ins["final_norm_g"], out)


def final_phase(nc, T, sem, gain_src, out):
    with ExitStack() as ctx:
        gain = ctx.enter_context(nc.sbuf_tensor("final_gain", [P, D_MODEL], F32))
        y = ctx.enter_context(nc.sbuf_tensor("final_y", [P, NT, D_MODEL], F32))
        stat = ctx.enter_context(nc.sbuf_tensor("final_stat", [P, 4, NT], F32))
        gain_in, squares, mean_ready, root_ready = sem("f_gain_in"), sem("f_squares"), sem("f_mean"), sem("f_root")
        chain, ready, stored = sem("f_chain"), sem("f_ready"), sem("f_stored")
        block = ctx.enter_context(nc.Block())

        @block.sync
        def _(sp):
            sp.dma_start(gain[:, :], gain_src.rearrange("(a d) -> a d", a=1).to_broadcast([P, D_MODEL])).then_inc(gain_in, 16)
            for ti in range(NT):
                sp.wait_ge(ready, ti + 1)
                sp.dma_start(out[0, tok(ti), :], y[:, ti, :]).then_inc(stored, 16)
            sp.wait_ge(stored, 16 * NT)

        @block.scalar
        def _(act):
            for ti in range(NT):
                nc.scalar.activation(y[:, ti, :], T.resid[:, ti, :], ACT.Square,
                                     accum_out=stat[:, 0, ti:ti + 1]).then_inc(squares, 1)
            act.wait_ge(mean_ready, 1)
            nc.scalar.activation(stat[:, 2, :], stat[:, 1, :], ACT.Sqrt).then_inc(root_ready, 1)

        @block.vector
        def _(dve):
            link = linker(dve, chain)
            dve.wait_ge(squares, NT)
            nc.vector.tensor_scalar(stat[:, 1, :], stat[:, 0, :], 1.0 / D_MODEL, EPS,
                                    ALU.mult, ALU.add).then_inc(mean_ready, 1)
            dve.wait_ge(root_ready, 1)
            link(nc.vector.reciprocal(stat[:, 3, :], stat[:, 2, :]))
            dve.wait_ge(gain_in, 16)
            for ti in range(NT):
                nc.vector.scalar_tensor_tensor(y[:, ti, :], T.resid[:, ti, :], stat[:, 3, ti:ti + 1], gain[:, :],
                                               ALU.mult, ALU.mult).then_inc(ready, 1)


def kernel(**inputs):
    import numpy as _np
    import concourse.bacc as _bacc
    from concourse import mybir as _mybir
    from concourse.bass_utils import run_bass_kernel_spmd as _run

    nc = _bacc.Bacc("TRN2", target_bir_lowering=False, num_devices=1)
    arrays, ins = {}, {}
    for name in _INS:
        a = _np.ascontiguousarray(inputs[name])
        arrays[f"in_{name}"] = a
        ins[name] = nc.dram_tensor(f"in_{name}", a.shape, _mybir.dt.from_np(a.dtype), kind="ExternalInput").ap()
    c = shape_constants()
    arrays["shape_constants"] = c
    consts = nc.dram_tensor("shape_constants", c.shape, _mybir.dt.float32, kind="ExternalInput").ap()
    out = nc.dram_tensor("out", (1, SEQ, D_MODEL), _mybir.dt.float32, kind="ExternalOutput").ap()
    program(nc, ins, consts, out)
    r = _run(nc, [arrays], core_ids=[0])
    return r.results[0]["out"]
```

```python
import math
from contextlib import ExitStack

import concourse.bass as bass
import numpy as np
from concourse import mybir

F32 = mybir.dt.float32
F32R = mybir.dt.float32r
I32 = mybir.dt.int32
U32 = mybir.dt.uint32
ALU = mybir.AluOpType
ACT = mybir.ActivationFunctionType
AX = mybir.AxisListType

P = 128
D_MODEL, SEQ, DEPTH = 1024, 512, 2
NT = SEQ // P
KD = D_MODEL // P
HD, NH, GW = 64, 4, 256
EPS = 1e-6
NEG = -1e30
CMP_LEN, CMP_STRIDE = 32, 16
N_CMP = (SEQ - CMP_LEN) // CMP_STRIDE + 1
N_BUCKETS, MAX_DISTANCE = 32, 128
Q_LORA, KV_LORA, NOPE, ROPE = 256, 128, 64, 32
QD = NOPE + ROPE
CONV_W = 4
PH, PDK, NK, TOPK = 8, 256, 128, 16
N_EXPERTS = NK * NK
GB = 64

NSA_IN = GW + 6 * HD + 3 * NH
ML_IN = 4 * GW + 2 * NH
MLA_IN = Q_LORA + KV_LORA + ROPE
ML_BASE = NSA_IN
GDN_BASE = ML_BASE + ML_IN
MLA_BASE = GDN_BASE + ML_IN
BANK = 512

CONST_COLS = {}


def shape_constants():
    p = np.arange(P)[:, None]
    c = np.arange(P)[None, :]
    y = np.arange(SEQ)[None, :]
    parts = [
        ("ident", p == c),
        ("iota", np.broadcast_to(c, (P, P))),
        ("headones", p // HD == c // HD),
        ("maskq", np.where(p + SEQ - P - y >= 0, 0.0, NEG)),
        ("mask_strict", np.where(p > c, 0.0, NEG)),
        ("mask_t", np.where(c >= p, 0.0, NEG)),
        ("mask_strict_t", np.where(c > p, 0.0, NEG)),
        ("diag16", p // 16 == c // 16),
    ]
    for n in (16, 32, 64):
        below = (p // n == c // n + 1) & (p // (2 * n) == c // (2 * n))
        parts.append((f"below{n}_t", below.T))
    freq = (10000.0 ** (-np.arange(0, ROPE, 2, dtype=np.float32) / ROPE)).astype(np.float32)
    parts.append(("freq", np.broadcast_to(freq[None, :], (P, ROPE // 2))))
    parts.append(("past_first_block", p >= CMP_LEN - 1))
    d = np.maximum(np.arange(SEQ), 1).astype(np.float32)
    exact = N_BUCKETS // 2
    large = exact + (np.log(d / exact) / math.log(MAX_DISTANCE / exact) * (N_BUCKETS - exact)).astype(np.int32)
    bucket = np.where(np.arange(SEQ) < exact, np.arange(SEQ), np.minimum(large, N_BUCKETS - 1))
    parts.append(("bucket", p == bucket[None, :]))
    at = 0
    for name, a in parts:
        CONST_COLS[name] = (at, a.shape[1])
        at += a.shape[1]
    return np.ascontiguousarray(np.concatenate([np.asarray(a, np.float32) for _, a in parts], axis=1))


CONSTS_SHAPE = shape_constants().shape


class Tensors:
    pass


def linker(engine, sem):
    count = [0]

    def link(ins):
        count[0] += 1
        ins.then_inc(sem, 1)
        engine.wait_ge(sem, count[0])
    return link


def tok(ti):
    return slice(ti * P, (ti + 1) * P)


def setup_phase(nc, T, sem, x, positions, t5_table, consts, bias_dram):
    with ExitStack() as ctx:
        W = 896
        BL = 640 + SEQ
        hank = ctx.enter_context(nc.sbuf_tensor("hank", [P, NH, W], F32))
        table = ctx.enter_context(nc.sbuf_tensor("table", [N_BUCKETS, NH], F32))
        bucket = ctx.enter_context(nc.sbuf_tensor("bucket", [N_BUCKETS, SEQ], F32))
        brow = ctx.enter_context(nc.sbuf_tensor("brow", [NH, BL], F32))
        pos_i = ctx.enter_context(nc.sbuf_tensor("pos_i", [P, NT], I32))
        pos_f = ctx.enter_context(nc.sbuf_tensor("pos_f", [P, NT], F32))
        ang = ctx.enter_context(nc.sbuf_tensor("ang", [P, NT, 2, 16], F32))
        turns = ctx.enter_context(nc.sbuf_tensor("turns", [P, NT, 2, 16], F32))
        turns_i = ctx.enter_context(nc.sbuf_tensor("turns_i", [P, NT, 2, 16], I32))
        ps = ctx.enter_context(nc.psum_tensor("ps_setup", [P, 1, BANK], F32))
        consts_in, small_in, resid_in = sem("consts_in"), sem("small_in"), sem("resid_in")
        row_mm, row_ready, row_out, hank_in = sem("row_mm"), sem("row_ready"), sem("row_out"), sem("hank_in")
        chain, angle_ready, rope_done = sem("setup_chain"), sem("angle_ready"), sem("rope_done")
        block = ctx.enter_context(nc.Block())

        @block.sync
        def _(sp):
            sp.dma_start(T.consts[:, :], consts[:, 0:CONSTS_SHAPE[1] - SEQ]).then_inc(consts_in, 16)
            sp.dma_start(bucket[:, :], consts[0:N_BUCKETS, CONSTS_SHAPE[1] - SEQ:]).then_inc(small_in, 16)
            sp.dma_start(table[:, :], t5_table).then_inc(small_in, 16)
            sp.dma_start(pos_i[:, :], positions[0, :].rearrange("(t p) -> p t", p=P)).then_inc(small_in, 16)
            sp.dma_start(T.resid[:, :, :], x[0, :, :].rearrange("(t p) d -> p t d", p=P)).then_inc(resid_in, 16)
            sp.wait_ge(row_ready, 1)
            sp.dma_start(bias_dram[:, :], brow[:, :]).then_inc(row_out, 16)
            sp.wait_ge(row_out, 16)
            sp.dma_start(hank[:, :, :], bass.AP(tensor=bias_dram.tensor, offset=129,
                                                ap=[[1, P], [BL, NH], [1, W]])).then_inc(hank_in, 16)
            sp.wait_ge(resid_in, 16)

        @block.tensor
        def _(pe):
            pe.wait_ge(consts_in, 16)
            pe.wait_ge(small_in, 48)
            nc.tensor.matmul(ps[0:NH, 0, :], table[:, :], bucket[:, :],
                             start=True, stop=True).then_inc(row_mm, 1)

        @block.vector
        def _(dve):
            link = linker(dve, chain)
            link(nc.vector.memset(brow[:, 0:640], NEG))
            dve.wait_ge(row_mm, 1)
            nc.vector.tensor_copy(brow[:, 640:BL], ps[0:NH, 0, :]).then_inc(row_ready, 1)
            dve.wait_ge(small_in, 48)
            link(nc.vector.tensor_copy(pos_f[:, :], pos_i[:, :]))
            for half in range(2):
                link(nc.vector.tensor_tensor(ang[:, :, half, :],
                                             pos_f[:, :].unsqueeze(2).to_broadcast([P, NT, 16]),
                                             T.const("freq").unsqueeze(1).to_broadcast([P, NT, 16]), ALU.mult))
            for half, ahead in ((0, 0.25), (1, 0.0)):
                link(nc.vector.tensor_scalar(turns[:, :, half, :], ang[:, :, half, :], 1.0 / (2 * math.pi),
                                             ahead, ALU.mult, ALU.add))
            link(nc.vector.tensor_copy(turns_i[:, :, :, :], turns[:, :, :, :]))
            link(nc.vector.tensor_copy(turns[:, :, :, :], turns_i[:, :, :, :]))
            c1 = 6.28125
            c2 = float(np.float32(np.round((2 * math.pi - c1) * 2 ** 20) / 2 ** 20))
            c3 = 2 * math.pi - c1 - c2
            for part in (c1, c2, c3):
                link(nc.vector.scalar_tensor_tensor(ang[:, :, :, :].rearrange("p t c f -> p (t c f)"),
                                                    turns[:, :, :, :].rearrange("p t c f -> p (t c f)"), -part,
                                                    ang[:, :, :, :].rearrange("p t c f -> p (t c f)"),
                                                    ALU.mult, ALU.add))
            link(nc.vector.tensor_scalar_add(ang[:, :, 0, :], ang[:, :, 0, :], math.pi / 2))
            flat = ang[:, :, :, :].rearrange("p t c f -> p (t c f)")
            nc.vector.tensor_scalar(flat, flat, 3.1415925, -3.1415925, ALU.min, ALU.max).then_inc(angle_ready, 1)
            dve.wait_ge(hank_in, 16)
            nc.vector.tensor_copy(T.biasq[:, :, :], hank[:, :, W - 1:W - 1 - SEQ:-1])
            for h in range(NH):
                for ti in range(NT):
                    first = 480 + P * ti
                    nc.vector.tensor_copy(T.biasc[:, h, ti, :],
                                          hank[:, h, first - 16 * (N_CMP - 1):first + 1][:, ::-CMP_STRIDE])

        @block.scalar
        def _(act):
            act.wait_ge(angle_ready, 1)
            nc.scalar.activation(T.cossin[:, :, :, :].rearrange("p t c f -> p (t c f)"),
                                 ang[:, :, :, :].rearrange("p t c f -> p (t c f)"), ACT.Sin)


def norm_phase(nc, T, sem, name, gain_src, split):
    with ExitStack() as ctx:
        gain = ctx.enter_context(nc.sbuf_tensor(f"{name}_gain", [P, KD], F32))
        xn = ctx.enter_context(nc.sbuf_tensor(f"{name}_xn", [P, NT, D_MODEL], F32))
        stat = ctx.enter_context(nc.sbuf_tensor(f"{name}_stat", [P, 4, NT], F32))
        ps = ctx.enter_context(nc.psum_tensor(f"{name}_ps", [P, KD, BANK], F32))
        gain_in, squares, mean_ready, root_ready = (sem(f"{name}_{s}") for s in ("gain_in", "squares", "mean", "root"))
        normed, turned, hi_ready, chain = (sem(f"{name}_{s}") for s in ("normed", "turned", "hi", "chain"))
        block = ctx.enter_context(nc.Block())

        @block.sync
        def _(sp):
            sp.dma_start(gain[:, :], gain_src).then_inc(gain_in, 16)

        @block.scalar
        def _(act):
            for ti in range(NT):
                nc.scalar.activation(xn[:, ti, :], T.resid[:, ti, :], ACT.Square,
                                     accum_out=stat[:, 0, ti:ti + 1]).then_inc(squares, 1)
            act.wait_ge(mean_ready, 1)
            nc.scalar.activation(stat[:, 2, :], stat[:, 1, :], ACT.Sqrt).then_inc(root_ready, 1)
            act.wait_ge(gain_in, 16)
            for k in range(KD):
                act.wait_ge(turned, k + 1)
                if split or k % 2 == 0:
                    out = T.xn_r[:, 0, k, :] if split else T.xnT[:, k, :]
                    nc.scalar.activation(out, ps[:, k, :], ACT.Copy, scale=gain[:, k:k + 1]).then_inc(hi_ready, 1)

        @block.vector
        def _(dve):
            link = linker(dve, chain)
            dve.wait_ge(squares, NT)
            nc.vector.tensor_scalar(stat[:, 1, :], stat[:, 0, :], 1.0 / D_MODEL, EPS,
                                    ALU.mult, ALU.add).then_inc(mean_ready, 1)
            dve.wait_ge(root_ready, 1)
            link(nc.vector.reciprocal(stat[:, 3, :], stat[:, 2, :]))
            for ti in range(NT):
                nc.vector.tensor_scalar(xn[:, ti, :], T.resid[:, ti, :], stat[:, 3, ti:ti + 1], None,
                                        ALU.mult).then_inc(normed, 1)
            dve.wait_ge(gain_in, 16)
            for k in range(KD):
                if split:
                    dve.wait_ge(hi_ready, k + 1)
                    nc.vector.scalar_tensor_tensor(T.xn_r[:, 1, k, :], ps[:, k, :], gain[:, k:k + 1],
                                                   T.xn_r[:, 0, k, :].bitcast(F32), ALU.mult, ALU.subtract)
                elif k % 2 == 1:
                    dve.wait_ge(turned, k + 1)
                    nc.vector.tensor_scalar(T.xnT[:, k, :], ps[:, k, :], gain[:, k:k + 1], None, ALU.mult)

        @block.tensor
        def _(pe):
            pe.wait_ge(normed, NT)
            for k in range(KD):
                for ti in range(NT):
                    last = nc.tensor.transpose(ps[:, k, tok(ti)], xn[:, ti, k * P:(k + 1) * P], T.const("ident"))
                last.then_inc(turned, 1)


GROUPS = [(0, 384), (384, NSA_IN - 384),
          (ML_BASE, 384), (ML_BASE + 384, 384), (ML_BASE + 768, GW + 2 * NH),
          (GDN_BASE, 384), (GDN_BASE + 384, 384), (GDN_BASE + 768, GW + 2 * NH),
          (MLA_BASE, MLA_IN)]
MAX_GROUP = max(width for _, width in GROUPS)


def projection_tiles():
    tiles = []

    def fm(g, col, width, copies):
        tiles.append((g, True, col, width, 0, copies))

    def tm(g, col, width, name):
        for ti in range(NT):
            tiles.append((g, False, col, width, ti, [(name, ti, 0, 1.0)]))
    scale = HD ** -0.5
    for i in range(2):
        fm(0, i * P, P, [("nsa_q", 2 * i + j, 64 * j, scale) for j in range(2)])
    fm(0, 256, P, [("cmp_kv", j, 64 * j, 1.0) for j in range(2)])
    fm(1, 0, HD, [("nsa_k", 0, 0, 1.0)])
    fm(1, 128, HD, [("nsa_k", 1, 0, 1.0)])
    tm(1, 64, NSA_IN - 448, "nsa_tm")
    for i in range(2):
        fm(2, i * P, P, [("ml_q", 2 * i + j, 64 * j, 1.0) for j in range(2)])
    fm(2, 256, P, [("ml_k", j, 64 * j, scale) for j in range(2)])
    fm(3, 0, P, [("ml_k", 2 + j, 64 * j, scale) for j in range(2)])
    tm(3, P, GW, "ml_v")
    tm(4, 0, GW + 2 * NH, "ml_gates")
    for i in range(6):
        fm(5 + i // 3, i % 3 * P, P, [("gdn_in", i, 0, 1.0)])
    tm(7, 0, GW + 2 * NH, "gdn_gates")
    tm(8, 0, MLA_IN, "mla_tm")
    return tiles


def projection_phase(nc, T, sem, layer, w_in):
    tiles = projection_tiles()
    with ExitStack() as ctx:
        wbuf = ctx.enter_context(nc.sbuf_tensor("w_in_buf", [P, 2, KD, MAX_GROUP], F32))
        ps = ctx.enter_context(nc.psum_tensor("ps_proj", [P, 8, BANK], F32))
        group_in = [sem(f"w_in_{g}") for g in range(len(GROUPS))]
        product, out_act, out_dve = sem("proj_product"), sem("proj_act"), sem("proj_dve")
        block = ctx.enter_context(nc.Block())

        def target(copy, width, is_fm):
            name, at, row, _ = copy
            if name == "gdn_in":
                return T.gdn_in[:, at, CONV_W - 1:CONV_W - 1 + SEQ]
            if is_fm:
                return {"nsa_q": T.nsa_q, "cmp_kv": T.cmp_kv, "nsa_k": T.nsa_k,
                        "ml_q": T.ml_q, "ml_k": T.ml_k}[name][:, at, :]
            return {"nsa_tm": T.nsa_tm, "ml_v": T.ml_v, "ml_gates": T.ml_gates,
                    "gdn_gates": T.gdn_gates, "mla_tm": T.mla_tm}[name][:, at, :]

        def source(n, copy):
            _, is_fm, _, width, _, copies = tiles[n]
            if not is_fm:
                return ps[:, n % 8, 0:width]
            rows = HD if copy[0] != "gdn_in" else P
            return ps[copy[2]:copy[2] + rows, n % 8, :]

        @block.sync
        def _(sp):
            for g, (base, width) in enumerate(GROUPS):
                if g >= 2:
                    sp.wait_ge(product, [t[0] for t in tiles].index(g - 1))
                sp.dma_start(wbuf[:, g % 2, :, 0:width],
                             w_in[bass.ds(layer, 1), :, base:base + width]
                             .rearrange("a (k p) c -> p (a k) c", p=P)).then_inc(group_in[g], 16)

        @block.tensor
        def _(pe):
            for n, (g, is_fm, col, width, ti, _) in enumerate(tiles):
                if n == 0 or tiles[n - 1][0] != g:
                    pe.wait_ge(group_in[g], 16)
                if n >= 8:
                    pe.wait_ge(out_act if n % 2 == 0 else out_dve, (n - 8) // 2 + 1)
                for k in range(KD):
                    w = wbuf[:, g % 2, k, col:col + width]
                    if is_fm:
                        last = nc.tensor.matmul(ps[0:width, n % 8, :], w, T.xnT[:, k, :],
                                                start=(k == 0), stop=(k == KD - 1))
                    else:
                        last = nc.tensor.matmul(ps[:, n % 8, 0:width], T.xnT[:, k, tok(ti)], w,
                                                start=(k == 0), stop=(k == KD - 1))
                last.then_inc(product, 1)

        @block.scalar
        def _(act):
            for n in range(0, len(tiles), 2):
                act.wait_ge(product, n + 1)
                for copy in tiles[n][5]:
                    last = nc.scalar.activation(target(copy, tiles[n][3], tiles[n][1]), source(n, copy),
                                                ACT.Copy, scale=copy[3])
                last.then_inc(out_act, 1)

        @block.vector
        def _(dve):
            nc.vector.memset(T.gdn_in[:, :, 0:CONV_W - 1], 0.0)
            for n in range(1, len(tiles), 2):
                dve.wait_ge(product, n + 1)
                for copy in tiles[n][5]:
                    last = nc.vector.tensor_scalar(target(copy, tiles[n][3], tiles[n][1]), source(n, copy),
                                                   copy[3], None, ALU.mult)
                last.then_inc(out_dve, 1)


C_NEGM, C_NEGMT, C_GC, C_R, C_KD, C_LB = range(6)


def gate_phase(nc, T, sem, layer, ml_i_bias, ml_f_bias, gdn_dt_bias, gdn_a_log):
    with ExitStack() as ctx:
        def sb(name, shape):
            return ctx.enter_context(nc.sbuf_tensor(name, shape, F32))
        bias = sb("gate_bias", [P, 4, NH])
        lx = sb("gate_lx", [P, NT, 3, NH])
        tmp = sb("gate_tmp", [P, 3, NT, 3, NH])
        ea = sb("gate_ea", [P, NH])
        tokg = sb("gate_tok", [P, 4, NT, NH])
        rows = sb("gate_rows", [NH, 4, SEQ])
        work = sb("gate_work", [NH, 6, SEQ])
        cum = sb("gate_cum", [NH, 2, SEQ])
        ones = sb("gate_ones", [NH, SEQ])
        ps = ctx.enter_context(nc.psum_tensor("ps_gate", [P, 8, BANK], F32))
        bias_in, chain, shrunk, exp_done = sem("gate_bias_in"), sem("gate_chain"), sem("gate_shrunk"), sem("gate_exp")
        shifted, ln_done, tok_ready, row_mm = sem("gate_shifted"), sem("gate_ln"), sem("gate_tok_ready"), sem("gate_row_mm")
        rows_ready, col_mm, cols_ready = sem("gate_rows_ready"), sem("gate_col_mm"), sem("gate_cols_ready")
        block = ctx.enter_context(nc.Block())

        @block.sync
        def _(sp):
            for n, src in enumerate((ml_i_bias, ml_f_bias, gdn_dt_bias, gdn_a_log)):
                sp.dma_start(bias[:, n, :], src[bass.ds(layer, 1), :].to_broadcast([P, NH])).then_inc(bias_in, 16)

        @block.scalar
        def _(act):
            act.wait_ge(shrunk, 1)
            nc.scalar.activation(tmp[:, 1, :, :, :].rearrange("p t c h -> p (t c h)"),
                                 tmp[:, 0, :, :, :].rearrange("p t c h -> p (t c h)"), ACT.Exp).then_inc(exp_done, 1)
            nc.scalar.activation(ea[:, :], bias[:, 3, :], ACT.Exp).then_inc(exp_done, 1)
            act.wait_ge(shifted, 1)
            nc.scalar.activation(tmp[:, 2, :, :, :].rearrange("p t c h -> p (t c h)"),
                                 tmp[:, 1, :, :, :].rearrange("p t c h -> p (t c h)"), ACT.Ln).then_inc(ln_done, 1)
            act.wait_ge(cols_ready, 1)
            nc.scalar.activation(T.exp_cols[:, :, :, :].rearrange("p c t h -> p (c t h)"),
                                 T.cols[:, :, :, :].rearrange("p c t h -> p (c t h)"), ACT.Exp)

        @block.vector
        def _(dve):
            link = linker(dve, chain)
            nc.vector.tensor_copy(T.headrow[:, :, :], T.const("ident", 0, NH, NH).unsqueeze(2).to_broadcast([NH, NH, P]))
            dve.wait_ge(bias_in, 64)

            def over_tiles(n):
                return bias[:, n, :].unsqueeze(1).to_broadcast([P, NT, NH])
            nc.vector.tensor_tensor(tokg[:, 0, :, :], T.ml_gates[:, :, 0:NH], over_tiles(0), ALU.add)
            link(nc.vector.tensor_tensor(lx[:, :, 0, :], T.ml_gates[:, :, NH:2 * NH], over_tiles(1), ALU.add))
            link(nc.vector.tensor_copy(lx[:, :, 1, :], T.gdn_gates[:, :, 0:NH]))
            link(nc.vector.tensor_tensor(lx[:, :, 2, :], T.gdn_gates[:, :, NH:2 * NH], over_tiles(2), ALU.add))
            link(nc.vector.tensor_scalar_mul(lx[:, :, 2, :], lx[:, :, 2, :], -1.0))
            flat = lx[:, :, :, :].rearrange("p t c h -> p (t c h)")

            def part(n):
                return tmp[:, n, :, :, :].rearrange("p t c h -> p (t c h)")
            link(nc.vector.tensor_scalar_mul(part(0), flat, -1.0))
            nc.vector.tensor_tensor(part(0), part(0), flat, ALU.min).then_inc(shrunk, 1)
            dve.wait_ge(exp_done, 2)
            nc.vector.tensor_scalar_add(part(1), part(1), 1.0).then_inc(shifted, 1)
            link(nc.vector.tensor_scalar_min(part(0), flat, 0.0))
            dve.wait_ge(ln_done, 1)
            for c in range(3):
                link(nc.vector.tensor_tensor(tokg[:, 1 + c, :, :], tmp[:, 0, :, c, :], tmp[:, 2, :, c, :],
                                             ALU.subtract))
            nc.vector.tensor_tensor(tokg[:, 3, :, :], tokg[:, 3, :, :],
                                    ea[:, :].unsqueeze(1).to_broadcast([P, NT, NH]), ALU.mult).then_inc(tok_ready, 1)
            dve.wait_ge(row_mm, 1)
            link(nc.vector.tensor_copy(rows[:, :, :], ps[0:NH, 0:4, :]))
            link(nc.vector.memset(ones[:, :], 1.0))
            link(nc.vector.tensor_tensor_scan(cum[:, 0, :], ones[:, :], rows[:, 1, :], 0.0, ALU.mult, ALU.add))
            link(nc.vector.tensor_tensor(T.rows[:, 0, :], rows[:, 0, :], cum[:, 0, :], ALU.subtract))
            link(nc.vector.tensor_tensor_scan(cum[:, 1, :], T.rows[:, 0, :], T.rows[:, 0, :], 0.0, ALU.max, ALU.max))
            link(nc.vector.tensor_scalar_mul(work[:, C_NEGM, :], cum[:, 1, :], -1.0))
            link(nc.vector.tensor_tensor(work[:, C_NEGMT, :], work[:, C_NEGM, :], cum[:, 0, :], ALU.subtract))
            for ti in range(NT):
                link(nc.vector.tensor_tensor_scan(work[:, C_GC, tok(ti)], ones[:, tok(0)], rows[:, 3, tok(ti)],
                                                  0.0, ALU.mult, ALU.add))
                end = (ti + 1) * P
                link(nc.vector.tensor_scalar(work[:, C_KD, tok(ti)], work[:, C_GC, tok(ti)], -1.0,
                                             work[:, C_GC, end - 1:end], ALU.mult, ALU.add))
            link(nc.vector.tensor_copy(T.rows[:, 1, :], work[:, C_GC, :]))
            link(nc.vector.tensor_tensor(work[:, C_R, :], work[:, C_GC, :], rows[:, 2, :], ALU.add))
            link(nc.vector.tensor_copy(T.rows[:, 2, :], work[:, C_R, :]))
            nc.vector.tensor_copy(work[:, C_LB, :], rows[:, 2, :]).then_inc(rows_ready, 1)
            dve.wait_ge(col_mm, 1)
            nc.vector.tensor_copy(T.cols[:, :, :, :].rearrange("p c t h -> p (c t h)"),
                                  ps[:, 4, 0:6 * NT * NH]).then_inc(cols_ready, 1)
            dve.wait_ge(cols_ready, 1)
            nc.vector.tensor_scalar_mul(T.neg_gc[:, :, :].rearrange("p t h -> p (t h)"),
                                        T.cols[:, C_GC, :, :].rearrange("p t h -> p (t h)"), -1.0)

        @block.tensor
        def _(pe):
            pe.wait_ge(tok_ready, 1)
            for c in range(4):
                for ti in range(NT):
                    last = nc.tensor.transpose(ps[0:NH, c, tok(ti)], tokg[:, c, ti, :], T.const("ident"))
            last.then_inc(row_mm, 1)
            pe.wait_ge(rows_ready, 1)
            for c in range(6):
                for ti in range(NT):
                    at = (c * NT + ti) * NH
                    last = nc.tensor.transpose(ps[:, 4, at:at + NH], work[:, c, tok(ti)],
                                               T.const("ident", 0, NH, NH))
            last.then_inc(col_mm, 1)


def compress_phase(nc, T, sem, layer, w_cmp_k, w_cmp_v, cmp_pos):
    with ExitStack() as ctx:
        wk = ctx.enter_context(nc.sbuf_tensor("cmp_wk", [HD, CMP_LEN, HD], F32))
        wv = ctx.enter_context(nc.sbuf_tensor("cmp_wv", [HD, CMP_LEN, HD], F32))
        pos = ctx.enter_context(nc.sbuf_tensor("cmp_pos", [CMP_LEN, HD], F32))
        posT = ctx.enter_context(nc.sbuf_tensor("cmp_posT", [HD, CMP_LEN], F32))
        blocks = ctx.enter_context(nc.sbuf_tensor("cmp_blocks", [HD, 2, N_CMP, CMP_LEN], F32))
        ps = ctx.enter_context(nc.psum_tensor("ps_cmp", [P, 3, BANK], F32))
        loaded, pos_mm, pos_ready = sem("cmp_loaded"), sem("cmp_pos_mm"), sem("cmp_pos_ready")
        blocks_ready, product = sem("cmp_blocks_ready"), sem("cmp_product")
        block = ctx.enter_context(nc.Block())

        @block.sync
        def _(sp):
            sp.dma_start(pos[:, :], cmp_pos[bass.ds(layer, 1), :, :].rearrange("a l d -> (a l) d")).then_inc(loaded, 16)
            for w, src in ((wk, w_cmp_k), (wv, w_cmp_v)):
                sp.dma_start(w[:, :, :], src[bass.ds(layer, 1), :, :]
                             .rearrange("a (l d) e -> d (a l) e", d=HD)).then_inc(loaded, 16)

        @block.tensor
        def _(pe):
            pe.wait_ge(loaded, 48)
            nc.tensor.transpose(ps[0:HD, 2, 0:CMP_LEN], pos[:, :], T.const("ident", 0, CMP_LEN, CMP_LEN)).then_inc(pos_mm, 1)
            pe.wait_ge(blocks_ready, 2)
            for i in range(CMP_LEN):
                last = nc.tensor.matmul(ps[0:HD, 0, 0:N_CMP], wk[:, i, :], blocks[:, 0, :, i],
                                        start=(i == 0), stop=(i == CMP_LEN - 1))
            last.then_inc(product, 1)
            for i in range(CMP_LEN):
                last = nc.tensor.matmul(ps[0:N_CMP, 1, 0:HD], blocks[:, 1, :, i], wv[:, i, :],
                                        start=(i == 0), stop=(i == CMP_LEN - 1))
            last.then_inc(product, 1)

        @block.vector
        def _(dve):
            dve.wait_ge(pos_mm, 1)
            nc.vector.tensor_copy(posT[:, :], ps[0:HD, 2, 0:CMP_LEN]).then_inc(pos_ready, 1)
            dve.wait_ge(pos_ready, 1)
            for c in range(2):
                src = T.cmp_kv[:, c, :]
                src = bass.AP(tensor=src.tensor, offset=src.offset,
                              ap=[list(src.ap[0]), [CMP_STRIDE, N_CMP], [1, CMP_LEN]])
                nc.vector.tensor_tensor(blocks[:, c, :, :], src,
                                        posT[:, :].unsqueeze(1).to_broadcast([HD, N_CMP, CMP_LEN]),
                                        ALU.add).then_inc(blocks_ready, 1)
            dve.wait_ge(product, 1)
            nc.vector.tensor_copy(T.k_cmp[:, :], ps[0:HD, 0, 0:N_CMP])
            dve.wait_ge(product, 2)
            nc.vector.tensor_copy(T.v_cmp[:, :], ps[0:N_CMP, 1, 0:HD])

        @block.scalar
        def _(act):
            nc.scalar.activation(T.nsa_gate[:, :, :], T.nsa_tm[:, :, 192:192 + 3 * NH], ACT.Sigmoid)


def mla_phase(nc, T, sem, layer, q_norm_g, kv_norm_g, w_uq, w_ukv):
    with ExitStack() as ctx:
        def sb(name, shape):
            return ctx.enter_context(nc.sbuf_tensor(name, shape, F32))
        wq = sb("mla_wq", [P, 2, NH * QD])
        wkv = sb("mla_wkv", [P, NH * 2 * HD])
        gain = sb("mla_gain", [P, 3])
        stat = sb("mla_stat", [P, 4, NT, 2])
        cn = sb("mla_cn", [P, NT, Q_LORA + KV_LORA])
        cT = sb("mla_cT", [P, 3, SEQ])
        qcat = sb("mla_qcat", [P, NT, NH, QD])
        kcat = sb("mla_kcat", [P, NT, NH, QD])
        kr = sb("mla_kr", [P, NT, ROPE])
        ra = sb("mla_ra", [P, 4, NT, NH, 16])
        rk = sb("mla_rk", [P, 4, NT, 16])
        ps = ctx.enter_context(nc.psum_tensor("ps_mla", [P, 8, BANK], F32))
        loaded, squares, mean_ready, root = sem("mla_loaded"), sem("mla_squares"), sem("mla_mean"), sem("mla_root")
        normed, turned, turned_out, product = sem("mla_normed"), sem("mla_turned"), sem("mla_turned_out"), sem("mla_product")
        raw_out, chain, cats_ready, cat_turned, chain_act = (sem("mla_raw_out"), sem("mla_chain"), sem("mla_cats"),
                                                             sem("mla_cat_turned"), sem("mla_cat_out"))
        block = ctx.enter_context(nc.Block())
        widths = ((0, Q_LORA), (Q_LORA, Q_LORA + KV_LORA))

        @block.sync
        def _(sp):
            sp.dma_start(wq[:, :, :], w_uq[bass.ds(layer, 1), :, :]
                         .rearrange("a (k p) c -> p (a k) c", p=P)).then_inc(loaded, 16)
            sp.dma_start(wkv[:, :], w_ukv[bass.ds(layer, 1), :, :].rearrange("a p c -> (a p) c")).then_inc(loaded, 16)
            sp.dma_start(gain[:, 0:2], q_norm_g[bass.ds(layer, 1), :].rearrange("a (k p) -> p (a k)", p=P),
                         ).then_inc(loaded, 16)
            sp.dma_start(gain[:, 2:3], kv_norm_g[bass.ds(layer, 1), :].rearrange("a p -> p a")).then_inc(loaded, 16)

        @block.scalar
        def _(act):
            for ti in range(NT):
                for c, (a, b) in enumerate(widths):
                    nc.scalar.activation(cn[:, ti, a:b], T.mla_tm[:, ti, a:b], ACT.Square,
                                         accum_out=stat[:, 0, ti, c:c + 1]).then_inc(squares, 1)
            act.wait_ge(mean_ready, 2)
            nc.scalar.activation(stat[:, 2, :, :], stat[:, 1, :, :], ACT.Sqrt).then_inc(root, 1)
            act.wait_ge(loaded, 64)
            for c in range(3):
                act.wait_ge(turned, c + 1)
                nc.scalar.activation(cT[:, c, :], ps[:, c, :], ACT.Copy, scale=gain[:, c:c + 1]).then_inc(turned_out, 1)
            for ti in range(NT):
                act.wait_ge(product, NT + ti + 1)
                bank = ps[:, 4 + ti, :].rearrange("p (h c) -> p h c", h=NH)
                nc.scalar.activation(T.mla_v[:, ti, :, :], bank[:, :, HD:2 * HD], ACT.Copy)
                nc.scalar.activation(kcat[:, ti, :, 0:HD], bank[:, :, 0:HD], ACT.Copy).then_inc(raw_out, 1)
            for n in range(0, 8, 2):
                act.wait_ge(cat_turned, n + 1)
                nc.scalar.activation(T.mla_qk[:, n, :], ps[0:QD, n, :], ACT.Copy)

        @block.vector
        def _(dve):
            link = linker(dve, chain)
            dve.wait_ge(squares, 2 * NT)
            for c, (a, b) in enumerate(widths):
                nc.vector.tensor_scalar(stat[:, 1, :, c], stat[:, 0, :, c], 1.0 / (b - a), EPS,
                                        ALU.mult, ALU.add).then_inc(mean_ready, 1)
            dve.wait_ge(root, 1)
            link(nc.vector.reciprocal(stat[:, 3, :, :], stat[:, 2, :, :]))
            for ti in range(NT):
                for c, (a, b) in enumerate(widths):
                    nc.vector.tensor_scalar(cn[:, ti, a:b], T.mla_tm[:, ti, a:b], stat[:, 3, ti, c:c + 1], None,
                                            ALU.mult).then_inc(normed, 1)
            for ti in range(NT):
                dve.wait_ge(product, ti + 1)
                bank = ps[:, ti, 0:NH * QD].rearrange("p (h c) -> p h c", h=NH)
                link(nc.vector.tensor_scalar(qcat[:, ti, :, :], bank, QD ** -0.5, None, ALU.mult))
            cos, sin = T.cossin[:, :, 0, :], T.cossin[:, :, 1, :]
            cosq, sinq = (v.unsqueeze(2).to_broadcast([P, NT, NH, 16]) for v in (cos, sin))
            t1, t2 = qcat[:, :, :, HD:HD + 16], qcat[:, :, :, HD + 16:QD]
            k1, k2 = (T.mla_tm[:, :, Q_LORA + KV_LORA + 16 * i:Q_LORA + KV_LORA + 16 * i + 16] for i in range(2))
            for ti in range(NT):
                cq = cos[:, ti, :].unsqueeze(1).to_broadcast([P, NH, 16])
                sq = sin[:, ti, :].unsqueeze(1).to_broadcast([P, NH, 16])
                nc.vector.tensor_tensor(ra[:, 0, ti, :, :], t1[:, ti], cq, ALU.mult)
                nc.vector.tensor_tensor(ra[:, 1, ti, :, :], t2[:, ti], sq, ALU.mult)
                nc.vector.tensor_tensor(ra[:, 2, ti, :, :], t2[:, ti], cq, ALU.mult)
                link(nc.vector.tensor_tensor(ra[:, 3, ti, :, :], t1[:, ti], sq, ALU.mult))
            nc.vector.tensor_tensor(t1, ra[:, 0, :, :, :], ra[:, 1, :, :, :], ALU.subtract).then_inc(cats_ready, 1)
            nc.vector.tensor_tensor(t2, ra[:, 2, :, :, :], ra[:, 3, :, :, :], ALU.add).then_inc(cats_ready, 1)
            nc.vector.tensor_tensor(rk[:, 0, :, :], k1, cos, ALU.mult)
            nc.vector.tensor_tensor(rk[:, 1, :, :], k2, sin, ALU.mult)
            nc.vector.tensor_tensor(rk[:, 2, :, :], k2, cos, ALU.mult)
            link(nc.vector.tensor_tensor(rk[:, 3, :, :], k1, sin, ALU.mult))
            nc.vector.tensor_tensor(kr[:, :, 0:16], rk[:, 0, :, :], rk[:, 1, :, :], ALU.subtract)
            link(nc.vector.tensor_tensor(kr[:, :, 16:32], rk[:, 2, :, :], rk[:, 3, :, :], ALU.add))
            nc.vector.tensor_copy(kcat[:, :, :, HD:QD],
                                  kr[:, :, :].unsqueeze(2).to_broadcast([P, NT, NH, ROPE])).then_inc(cats_ready, 1)
            for n in range(1, 8, 2):
                dve.wait_ge(cat_turned, n + 1)
                nc.vector.tensor_copy(T.mla_qk[:, n, :], ps[0:QD, n, :])

        @block.tensor
        def _(pe):
            pe.wait_ge(normed, 2 * NT)
            for c in range(3):
                for ti in range(NT):
                    last = nc.tensor.transpose(ps[:, c, tok(ti)], cn[:, ti, c * P:(c + 1) * P], T.const("ident"))
                last.then_inc(turned, 1)
            pe.wait_ge(turned_out, 3)
            for ti in range(NT):
                for c in range(2):
                    last = nc.tensor.matmul(ps[:, ti, 0:NH * QD], cT[:, c, tok(ti)], wq[:, c, :],
                                            start=(c == 0), stop=(c == 1))
                last.then_inc(product, 1)
            for ti in range(NT):
                nc.tensor.matmul(ps[:, 4 + ti, :], cT[:, 2, tok(ti)], wkv[:, :], start=True, stop=True).then_inc(product, 1)
            pe.wait_ge(cats_ready, 3)
            pe.wait_ge(raw_out, NT)
            for n in range(8):
                cat = (qcat, kcat)[n // NH]
                for ti in range(NT):
                    last = nc.tensor.transpose(ps[0:QD, n, tok(ti)], cat[:, ti, n % NH, :], T.const("ident"))
                last.then_inc(cat_turned, 1)


def attention_phase(nc, T, sem):
    assert min(16, SEQ // 64) == SEQ // 64
    jobs = [(kind, qi, h) for qi in range(NT) for h in range(NH) for kind in ("cmp", "sel", "win", "mla")]
    n_jobs = len(jobs)
    with ExitStack() as ctx:
        def sb(name, shape):
            return ctx.enter_context(nc.sbuf_tensor(name, shape, F32))
        scores = sb("att_scores", [P, 2, SEQ])
        probs = sb("att_probs", [P, 2, SEQ])
        probsT = sb("att_probsT", [P, 2, SEQ])
        top = sb("att_top", [P, n_jobs])
        negtop = sb("att_negtop", [P, n_jobs])
        total = sb("att_total", [P, n_jobs])
        inv = sb("att_inv", [P, n_jobs])
        fac = sb("att_fac", [P, n_jobs])
        ps_s = ctx.enter_context(nc.psum_tensor("ps_scores", [P, 2, BANK], F32))
        ps_t = ctx.enter_context(nc.psum_tensor("ps_probsT", [P, 2, BANK], F32))
        ps_o = ctx.enter_context(nc.psum_tensor("ps_out", [P, 2, BANK], F32))
        scored, masked, top_ready, exp_done = sem("att_scored"), sem("att_masked"), sem("att_top_ready"), sem("att_exp")
        turned, turned_out, product, chain = sem("att_turned"), sem("att_turned_out"), sem("att_product"), sem("att_chain")
        finished = sem("att_finished")
        block = ctx.enter_context(nc.Block())

        def keys(job):
            kind, qi, h = job
            return N_CMP if kind == "cmp" else P * (qi + 1)

        def parts(job):
            n = keys(job)
            return [(b, min(P, n - P * b)) for b in range((n + P - 1) // P)]

        @block.tensor
        def _(pe):
            for j in range(n_jobs + 2):
                if j < n_jobs:
                    kind, qi, h = jobs[j]
                    if j >= 2:
                        pe.wait_ge(masked, j - 1)
                    if kind == "mla":
                        q, k = T.mla_qk[:, h, tok(qi)], T.mla_qk[:, NH + h, 0:keys(jobs[j])]
                    else:
                        q = T.nsa_q[:, h, tok(qi)]
                        k = {"cmp": T.k_cmp[:, :], "sel": T.nsa_k[:, 0, 0:keys(jobs[j])],
                             "win": T.nsa_k[:, 1, 0:keys(jobs[j])]}[kind]
                    nc.tensor.matmul(ps_s[:, j % 2, 0:keys(jobs[j])], q, k, start=True, stop=True).then_inc(scored, 1)
                if 1 <= j <= n_jobs:
                    i = j - 1
                    pe.wait_ge(exp_done, i + 1)
                    if i >= 2:
                        pe.wait_ge(turned_out, i - 1)
                    for b, n in parts(jobs[i]):
                        last = nc.tensor.transpose(ps_t[0:n, i % 2, tok(b)], probs[:, i % 2, P * b:P * b + n],
                                                   T.const("ident"))
                    last.then_inc(turned, 1)
                if j >= 2:
                    i = j - 2
                    kind, qi, h = jobs[i]
                    pe.wait_ge(turned_out, i + 1)
                    if i >= 2:
                        pe.wait_ge(finished, i - 1)
                    for b, n in parts(jobs[i]):
                        v = {"cmp": T.v_cmp[:, :], "sel": T.nsa_tm[:, b, 0:HD], "win": T.nsa_tm[:, b, 2 * HD:3 * HD],
                             "mla": T.mla_v[:, b, h, :]}[kind]
                        last = nc.tensor.matmul(ps_o[:, i % 2, 0:HD], probsT[0:n, i % 2, tok(b)], v,
                                                start=(b == 0), stop=(b == len(parts(jobs[i])) - 1))
                    last.then_inc(product, 1)

        @block.vector
        def _(dve):
            link = linker(dve, chain)
            for j in range(n_jobs + 2):
                if j < n_jobs:
                    kind, qi, h = jobs[j]
                    n = keys(jobs[j])
                    dve.wait_ge(scored, j + 1)
                    if j >= 2:
                        dve.wait_ge(exp_done, j - 1)
                    bias = {"cmp": T.biasc[:, h, qi, :], "mla": T.const("maskq")[:, SEQ - n:SEQ]}.get(
                        kind, T.biasq[:, h, SEQ - n:SEQ])
                    nc.vector.tensor_tensor_reduce(out=scores[:, j % 2, 0:n], in0=ps_s[:, j % 2, 0:n], in1=bias,
                                                   scale=1.0, scalar=-3e38, op0=ALU.add, op1=ALU.max,
                                                   accum_out=top[:, j:j + 1]).then_inc(masked, 1)
                    dve.wait_ge(masked, j + 1)
                    nc.vector.tensor_scalar_mul(negtop[:, j:j + 1], top[:, j:j + 1], -1.0).then_inc(top_ready, 1)
                if j >= 2:
                    i = j - 2
                    kind, qi, h = jobs[i]
                    dve.wait_ge(exp_done, i + 1)
                    link(nc.vector.reciprocal(inv[:, i:i + 1], total[:, i:i + 1]))
                    f = inv[:, i:i + 1]
                    if kind != "mla":
                        branch = {"cmp": 0, "sel": 1, "win": 2}[kind]
                        gate = T.nsa_gate[:, qi, branch * NH + h:branch * NH + h + 1]
                        link(nc.vector.tensor_tensor(fac[:, i:i + 1], f, gate, ALU.mult))
                        f = fac[:, i:i + 1]
                        if kind == "cmp" and qi == 0:
                            link(nc.vector.tensor_tensor(f, f, T.const("past_first_block"), ALU.mult))
                    dve.wait_ge(product, i + 1)
                    o = ps_o[:, i % 2, 0:HD]
                    if kind in ("cmp", "mla"):
                        at = h * HD + (3 * GW if kind == "mla" else 0)
                        nc.vector.tensor_scalar(T.mix[:, qi, at:at + HD], o, f, None, ALU.mult).then_inc(finished, 1)
                    else:
                        dve.wait_ge(finished, i)
                        nc.vector.scalar_tensor_tensor(T.mix[:, qi, h * HD:h * HD + HD], o, f,
                                                       T.mix[:, qi, h * HD:h * HD + HD], ALU.mult,
                                                       ALU.add).then_inc(finished, 1)

        @block.scalar
        def _(act):
            for j in range(n_jobs + 1):
                if j < n_jobs:
                    n = keys(jobs[j])
                    act.wait_ge(top_ready, j + 1)
                    if j >= 2:
                        act.wait_ge(turned, j - 1)
                    nc.scalar.activation(probs[:, j % 2, 0:n], scores[:, j % 2, 0:n], ACT.Exp,
                                         bias=negtop[:, j:j + 1], accum_out=total[:, j:j + 1]).then_inc(exp_done, 1)
                if j >= 1:
                    i = j - 1
                    act.wait_ge(turned, i + 1)
                    if i >= 2:
                        act.wait_ge(product, i - 1)
                    rows = min(P, keys(jobs[i]))
                    nc.scalar.activation(probsT[0:rows, i % 2, 0:P * len(parts(jobs[i]))],
                                         ps_t[0:rows, i % 2, 0:P * len(parts(jobs[i]))],
                                         ACT.Copy).then_inc(turned_out, 1)


def head_norm(nc, dve, act_sems, link, values, square, stat, gain, out):
    mean_ready, root_ready = act_sems
    link(nc.vector.tensor_tensor(square, values, values, ALU.mult))
    link(nc.vector.tensor_reduce(stat[:, 0, :, :], square, AX.X, ALU.add))
    nc.vector.tensor_scalar(stat[:, 1, :, :], stat[:, 0, :, :], 1.0 / HD, EPS, ALU.mult, ALU.add).then_inc(mean_ready, 1)
    dve.wait_ge(root_ready, 1)
    link(nc.vector.reciprocal(stat[:, 3, :, :], stat[:, 2, :, :]))
    link(nc.vector.tensor_tensor(square, values, stat[:, 3, :, :].unsqueeze(3).to_broadcast([P, NT, NH, HD]), ALU.mult))
    if out.shape[1] == NT:
        square = square.rearrange("p t h d -> p t (h d)")
    else:
        square = square.rearrange("p t h d -> p (t h) d")
    link(nc.vector.tensor_tensor(out, square, gain, ALU.mult))


def mlstm_phase(nc, T, sem, layer, norm_g):
    jobs = [(qi, h) for qi in range(NT) for h in range(NH)]
    n_jobs = len(jobs)
    with ExitStack() as ctx:
        def sb(name, shape):
            return ctx.enter_context(nc.sbuf_tensor(name, shape, F32))
        arow = sb("ml_arow", [P, NH, SEQ])
        ktok = sb("ml_masked", [P, 2, SEQ])
        decay = sb("ml_decay", [P, 2, SEQ])
        probs = sb("ml_probs", [P, 2, SEQ])
        probsT = sb("ml_probsT", [P, 2, SEQ])
        den = sb("ml_den", [P, 4, n_jobs])
        hs = sb("ml_hs", [P, NT, NH, HD])
        sq = sb("ml_square", [P, NT, NH, HD])
        og = sb("ml_og", [P, NT, NH, HD])
        gain = sb("ml_gain", [P, GW])
        stat = sb("ml_stat", [P, 4, NT, NH])
        ps_s = ctx.enter_context(nc.psum_tensor("ps_ml_scores", [P, 2, BANK], F32))
        ps_t = ctx.enter_context(nc.psum_tensor("ps_ml_probsT", [P, 2, BANK], F32))
        ps_o = ctx.enter_context(nc.psum_tensor("ps_ml_out", [P, 2, BANK], F32))
        ps_a = ctx.enter_context(nc.psum_tensor("ps_ml_arow", [P, 2, BANK], F32))
        gain_in, bcast, bcast_out, masked = sem("ml_gain_in"), sem("ml_bcast"), sem("ml_bcast_out"), sem("ml_masked")
        decayed, scored, weighed, turned = sem("ml_decayed"), sem("ml_scored"), sem("ml_weighed"), sem("ml_turned")
        turned_out, product, finished, chain = (sem("ml_turned_out"), sem("ml_product"), sem("ml_finished"),
                                                sem("ml_chain"))
        og_done, mean_ready, root_ready = sem("ml_og_done"), sem("ml_mean"), sem("ml_root")
        block = ctx.enter_context(nc.Block())

        @block.sync
        def _(sp):
            sp.dma_start(gain[:, :], norm_g[bass.ds(layer, 1), :].to_broadcast([P, GW])).then_inc(gain_in, 16)

        @block.tensor
        def _(pe):
            for h in range(NH):
                if h >= 2:
                    pe.wait_ge(bcast_out, h - 1)
                nc.tensor.matmul(ps_a[:, h % 2, :], T.headrow[:, h, :], T.rows[:, 0, :],
                                 start=True, stop=True).then_inc(bcast, 1)
            for j in range(n_jobs + 2):
                if j < n_jobs:
                    qi, h = jobs[j]
                    if j >= 2:
                        pe.wait_ge(weighed, j - 1)
                    nc.tensor.matmul(ps_s[:, j % 2, 0:P * (qi + 1)], T.ml_q[:, h, tok(qi)],
                                     T.ml_k[:, h, 0:P * (qi + 1)], start=True, stop=True).then_inc(scored, 1)
                if 1 <= j <= n_jobs:
                    i = j - 1
                    pe.wait_ge(weighed, i + 1)
                    if i >= 2:
                        pe.wait_ge(turned_out, i - 1)
                    for b in range(jobs[i][0] + 1):
                        last = nc.tensor.transpose(ps_t[:, i % 2, tok(b)], probs[:, i % 2, tok(b)], T.const("ident"))
                    last.then_inc(turned, 1)
                if j >= 2:
                    i = j - 2
                    qi, h = jobs[i]
                    pe.wait_ge(turned_out, i + 1)
                    if i >= 2:
                        pe.wait_ge(finished, i - 1)
                    for b in range(qi + 1):
                        last = nc.tensor.matmul(ps_o[:, i % 2, 0:HD], probsT[:, i % 2, tok(b)],
                                                T.ml_v[:, b, h * HD:(h + 1) * HD], start=(b == 0), stop=(b == qi))
                    last.then_inc(product, 1)

        @block.vector
        def _(dve):
            link = linker(dve, chain)
            for j in range(n_jobs + 3):
                if j < n_jobs:
                    qi, h = jobs[j]
                    n = P * (qi + 1)
                    if j < NH:
                        dve.wait_ge(bcast_out, j + 1)
                    if j >= 2:
                        dve.wait_ge(decayed, j - 1)
                    nc.vector.tensor_tensor(ktok[:, j % 2, 0:n], arow[:, h, 0:n], T.const("maskq")[:, SEQ - n:SEQ],
                                            ALU.add).then_inc(masked, 1)
                if 1 <= j <= n_jobs:
                    i = j - 1
                    qi, h = jobs[i]
                    n = P * (qi + 1)
                    dve.wait_ge(scored, i + 1)
                    dve.wait_ge(decayed, i + 1)
                    if i >= 2:
                        dve.wait_ge(turned, i - 1)
                    nc.vector.tensor_tensor_reduce(out=probs[:, i % 2, 0:n], in0=ps_s[:, i % 2, 0:n],
                                                   in1=decay[:, i % 2, 0:n], scale=1.0, scalar=0.0, op0=ALU.mult,
                                                   op1=ALU.add, accum_out=den[:, 0, i:i + 1]).then_inc(weighed, 1)
                if j >= 3:
                    i = j - 3
                    qi, h = jobs[i]
                    dve.wait_ge(weighed, i + 1)
                    link(nc.vector.scalar_tensor_tensor(den[:, 1, i:i + 1], den[:, 0, i:i + 1], -1.0,
                                                        den[:, 0, i:i + 1], ALU.mult, ALU.max))
                    link(nc.vector.tensor_tensor(den[:, 2, i:i + 1], den[:, 1, i:i + 1],
                                                 T.exp_cols[:, C_NEGMT, qi, h:h + 1], ALU.max))
                    link(nc.vector.reciprocal(den[:, 3, i:i + 1], den[:, 2, i:i + 1]))
                    dve.wait_ge(product, i + 1)
                    nc.vector.tensor_scalar(hs[:, qi, h, :], ps_o[:, i % 2, 0:HD], den[:, 3, i:i + 1], None,
                                            ALU.mult).then_inc(finished, 1)
            dve.wait_ge(finished, n_jobs)
            dve.wait_ge(og_done, 1)
            link(nc.vector.tensor_tensor(hs[:, :, :, :], hs[:, :, :, :], og[:, :, :, :], ALU.mult))
            dve.wait_ge(gain_in, 16)
            head_norm(nc, dve, (mean_ready, root_ready), link, hs[:, :, :, :], sq[:, :, :, :], stat,
                      gain[:, :].unsqueeze(1).to_broadcast([P, NT, GW]), T.mix[:, :, GW:2 * GW])

        @block.scalar
        def _(act):
            nc.scalar.activation(og[:, :, :, :], T.ml_gates[:, :, 2 * NH:2 * NH + GW]
                                 .rearrange("p t (h d) -> p t h d", h=NH), ACT.Sigmoid).then_inc(og_done, 1)
            for h in range(NH):
                act.wait_ge(bcast, h + 1)
                nc.scalar.activation(arow[:, h, :], ps_a[:, h % 2, :], ACT.Copy).then_inc(bcast_out, 1)
            for j in range(n_jobs + 2):
                if j < n_jobs:
                    qi, h = jobs[j]
                    n = P * (qi + 1)
                    act.wait_ge(masked, j + 1)
                    if j >= 2:
                        act.wait_ge(weighed, j - 1)
                    nc.scalar.activation(decay[:, j % 2, 0:n], ktok[:, j % 2, 0:n], ACT.Exp,
                                         bias=T.cols[:, C_NEGM, qi, h:h + 1]).then_inc(decayed, 1)
                if j >= 2:
                    i = j - 2
                    act.wait_ge(turned, i + 1)
                    if i >= 2:
                        act.wait_ge(product, i - 1)
                    n = P * (jobs[i][0] + 1)
                    nc.scalar.activation(probsT[:, i % 2, 0:n], ps_t[:, i % 2, 0:n], ACT.Copy).then_inc(turned_out, 1)
            act.wait_ge(mean_ready, 1)
            nc.scalar.activation(stat[:, 2, :, :], stat[:, 1, :, :], ACT.Sqrt).then_inc(root_ready, 1)


def conv_phase(nc, T, sem, layer, conv_w):
    with ExitStack() as ctx:
        def sb(name, shape):
            return ctx.enter_context(nc.sbuf_tensor(name, shape, F32))
        taps = sb("conv_taps", [P, 6, CONV_W])
        acc = sb("conv_acc", [P, 2, 6, SEQ])
        square = sb("conv_square", [P, 4, SEQ])
        root = sb("conv_root", [P, 2, 4, SEQ])
        ps = ctx.enter_context(nc.psum_tensor("ps_conv", [P, 8, BANK], F32))
        taps_in, chain, convolved, silu_done = sem("conv_taps_in"), sem("conv_chain"), sem("conv_done"), sem("conv_silu")
        squared, summed, eps_added, rooted = sem("conv_squared"), sem("conv_summed"), sem("conv_eps"), sem("conv_rooted")
        unit, turned = sem("conv_unit"), sem("conv_turned")
        block = ctx.enter_context(nc.Block())

        @block.sync
        def _(sp):
            for w in range(CONV_W):
                sp.dma_start(taps[:, :, w], conv_w[bass.ds(layer, 1), w, :]
                             .rearrange("a (c p) -> p (a c)", p=P)).then_inc(taps_in, 16)

        @block.vector
        def _(dve):
            link = linker(dve, chain)
            dve.wait_ge(taps_in, 64)
            for c in range(6):
                a, b = acc[:, 0, c, :], acc[:, 1, c, :]
                link(nc.vector.tensor_scalar(a, T.gdn_in[:, c, 0:SEQ], taps[:, c, 0:1], None, ALU.mult))
                link(nc.vector.scalar_tensor_tensor(b, T.gdn_in[:, c, 1:1 + SEQ], taps[:, c, 1:2], a, ALU.mult, ALU.add))
                link(nc.vector.scalar_tensor_tensor(a, T.gdn_in[:, c, 2:2 + SEQ], taps[:, c, 2:3], b, ALU.mult, ALU.add))
                nc.vector.scalar_tensor_tensor(b, T.gdn_in[:, c, 3:3 + SEQ], taps[:, c, 3:4], a, ALU.mult,
                                               ALU.add).then_inc(convolved, 1)
            for c in range(4):
                dve.wait_ge(silu_done, c + 1)
                nc.vector.tensor_tensor(square[:, c, :], T.gdn_fm[:, c, :], T.gdn_fm[:, c, :],
                                        ALU.mult).then_inc(squared, 1)
            for c in range(4):
                dve.wait_ge(summed, c + 1)
                nc.vector.tensor_scalar_add(root[:, 0, c, :], ps[:, c, :], EPS).then_inc(eps_added, 1)
            for c in range(4):
                dve.wait_ge(rooted, c + 1)
                link(nc.vector.reciprocal(root[:, 0, c, :], root[:, 1, c, :]))
                scale = HD ** -0.5 if c < 2 else 1.0
                nc.vector.scalar_tensor_tensor(T.gdn_fm[:, c, :], T.gdn_fm[:, c, :], scale, root[:, 0, c, :],
                                               ALU.mult, ALU.mult).then_inc(unit, 1)
            dve.wait_ge(unit, 4)
            nc.vector.tensor_copy(T.gdn_fm_odd[:, :, :], T.gdn_fm[HD:P, 0:4, :])
            for c in range(2):
                dve.wait_ge(turned, 2 + c + 1)
                nc.vector.tensor_copy(T.gdn_ktok[:, :, c * P:(c + 1) * P],
                                      ps[:, 6 + c, :].rearrange("p (t d) -> p t d", t=NT))

        @block.scalar
        def _(act):
            for c in range(6):
                act.wait_ge(convolved, c + 1)
                nc.scalar.activation(T.gdn_fm[:, c, :], acc[:, 1, c, :], ACT.Silu).then_inc(silu_done, 1)
            for c in range(4):
                act.wait_ge(eps_added, c + 1)
                nc.scalar.activation(root[:, 1, c, :], root[:, 0, c, :], ACT.Sqrt).then_inc(rooted, 1)
            for c in range(2):
                act.wait_ge(turned, c + 1)
                nc.scalar.activation(T.gdn_vtok[:, :, c * P:(c + 1) * P],
                                     ps[:, 4 + c, :].rearrange("p (t d) -> p t d", t=NT), ACT.Copy)

        @block.tensor
        def _(pe):
            for c in range(4):
                pe.wait_ge(squared, c + 1)
                nc.tensor.matmul(ps[:, c, :], T.const("headones"), square[:, c, :], start=True, stop=True).then_inc(summed, 1)
            pe.wait_ge(silu_done, 6)
            for c in range(2):
                for ti in range(NT):
                    last = nc.tensor.transpose(ps[:, 4 + c, tok(ti)], T.gdn_fm[:, 4 + c, tok(ti)], T.const("ident"))
                last.then_inc(turned, 1)
            pe.wait_ge(unit, 4)
            for c in range(2):
                for ti in range(NT):
                    last = nc.tensor.transpose(ps[:, 6 + c, tok(ti)], T.gdn_fm[:, 2 + c, tok(ti)], T.const("ident"))
                last.then_inc(turned, 1)


def gdn_phase(nc, T, sem, layer, norm_g):
    with ExitStack() as ctx:
        def sb(name, shape):
            return ctx.enter_context(nc.sbuf_tensor(name, shape, F32))

        HT = NT // 2

        def mats(name, tiles=HT):
            return sb(name, [P, tiles, NH, P])
        AT, LT, attnT = mats("gdn_AT"), mats("gdn_LT"), mats("gdn_attnT", NT)
        D, DT = [mats("gdn_D0"), mats("gdn_D1")], [mats("gdn_DT0"), mats("gdn_DT1")]
        X, XT = [mats("gdn_X0"), mats("gdn_X1")], [mats("gdn_XT0"), mats("gdn_XT1")]
        grow = sb("gdn_grow", [P, 2, NH, SEQ])
        work = sb("gdn_work", [P, 3, NH, P])
        expo = sb("gdn_expo_buf", [P, 3, NH, P])
        vb, kb, kd = (sb(f"gdn_{n}", [P, NT, NH, HD]) for n in ("vb", "kb", "kd"))
        U = sb("gdn_U", [P, NT, NH, HD])
        WT = sb("gdn_WT", [HD, NT, NH, P])
        os_ = T.mix[:, :, 2 * GW:3 * GW].rearrange("p t (h d) -> p t h d", h=NH)
        qdec = sb("gdn_qdec", [HD, NH, SEQ])
        state = sb("gdn_state", [HD, 2, NH, HD])
        vnew = sb("gdn_vnew", [P, 2, NH, HD])
        end = sb("gdn_end", [HD, NH, NT])
        gain = sb("gdn_gain", [P, HD])
        stat = sb("gdn_stat", [P, 4, NT, NH])
        ps = ctx.enter_context(nc.psum_tensor("ps_gdn", [P, 8, BANK], F32))
        gain_in, bcast, bcast_out = sem("gdn_gain_in"), sem("gdn_bcast"), sem("gdn_bcast_out")
        grams, args_ready, expo_ready, amats = sem("gdn_grams"), sem("gdn_args"), sem("gdn_expo"), sem("gdn_amats")
        chain, product, taken, lt_ready = sem("gdn_chain"), sem("gdn_product"), sem("gdn_taken"), sem("gdn_lt_ready")
        exp_rows, scaled, qdec_ready = sem("gdn_exp_rows"), sem("gdn_scaled"), sem("gdn_qdec_ready")
        uw_mm, uw_out, silu_done = sem("gdn_uw_mm"), sem("gdn_uw_out"), sem("gdn_silu")
        old_mm, vnew_ready, out_mm, out_taken = sem("gdn_old_mm"), sem("gdn_vnew_ready"), sem("gdn_out_mm"), sem("gdn_out_taken")
        mean_ready, root_ready = sem("gdn_mean"), sem("gdn_root")
        block = ctx.enter_context(nc.Block())

        def fm(kind, h, cols):
            c = 2 * kind + h // 2
            return T.gdn_fm[0:HD, c, cols] if h % 2 == 0 else T.gdn_fm_odd[:, c, cols]

        steps = []
        a, xi = 0, 0
        for _ in range(3):
            b = 1 - a
            steps += [(DT[a], D[a], D[b], None, 1.0), (D[a], DT[a], DT[b], None, 1.0),
                      (DT[b], X[xi], X[1 - xi], X[xi], 1.0), (X[xi], DT[b], XT[1 - xi], XT[xi], 1.0)]
            a, xi = b, 1 - xi
        Y = D[1 - a]
        level_steps = []
        for width in (16, 32, 64):
            level_steps.append(len(steps))
            steps.append((LT, X[xi], Y, None, 1.0))
            if width < 64:
                steps.append((XT[xi], Y, X[1 - xi], X[xi], -1.0))
            steps.append((Y, XT[xi], XT[1 - xi], XT[xi], -1.0))
            xi = 1 - xi
        inv_t = XT[xi]
        n_steps = len(steps)

        @block.sync
        def _(sp):
            sp.dma_start(gain[:, :], norm_g[bass.ds(layer, 1), :].to_broadcast([P, HD])).then_inc(gain_in, 16)

        @block.tensor
        def _(pe):
            for n in range(2 * NH):
                nc.tensor.matmul(ps[:, n, :], T.headrow[:, n % NH, :], T.rows[:, 1 + n // NH, :],
                                 start=True, stop=True).then_inc(bcast, 1)
            pe.wait_ge(bcast_out, 2 * NH)
            for half in range(2):
                if half:
                    pe.wait_ge(uw_out, 2 * HT)
                for tj in range(HT):
                    ti = HT * half + tj
                    for h in range(NH):
                        k = fm(1, h, tok(ti))
                        nc.tensor.matmul(ps[:, 4 + 2 * tj, h * P:(h + 1) * P], k, k, start=True, stop=True)
                    for h in range(NH):
                        last = nc.tensor.matmul(ps[:, 5 + 2 * tj, h * P:(h + 1) * P], fm(1, h, tok(ti)),
                                                fm(0, h, tok(ti)), start=True, stop=True)
                    last.then_inc(grams, 1)
                pe.wait_ge(amats, HT * (half + 1))
                for m, (left_t, right, _, _, _) in enumerate(steps):
                    n = n_steps * half + m
                    for tj in range(HT):
                        if m >= 1:
                            pe.wait_ge(taken, HT * (n - 1) + tj + 1)
                        if m in level_steps:
                            pe.wait_ge(lt_ready, HT * (len(level_steps) * half + level_steps.index(m)) + tj + 1)
                        for h in range(NH):
                            last = nc.tensor.matmul(ps[:, 2 * (m % 2) + tj, h * P:(h + 1) * P], left_t[:, tj, h, :],
                                                    right[:, tj, h, :], start=True, stop=True)
                        last.then_inc(product, 1)
                pe.wait_ge(taken, HT * n_steps * (half + 1))
                pe.wait_ge(scaled, 3)
                for tj in range(HT):
                    ti = HT * half + tj
                    for h in range(NH):
                        nc.tensor.matmul(ps[:, 4 + 2 * tj, h * HD:(h + 1) * HD], inv_t[:, tj, h, :], vb[:, ti, h, :],
                                         start=True, stop=True)
                        last = nc.tensor.matmul(ps[0:HD, 5 + 2 * tj, h * P:(h + 1) * P], kb[:, ti, h, :],
                                                inv_t[:, tj, h, :], start=True, stop=True)
                    last.then_inc(uw_mm, 1)
            pe.wait_ge(qdec_ready, 1)
            pe.wait_ge(uw_out, 2 * NT)
            for ti in range(NT):
                old = state[:, (ti + 1) % 2, :, :]
                if ti > 0:
                    pe.wait_ge(out_taken, 2 * ti)
                    for h in range(NH):
                        last = nc.tensor.matmul(ps[:, 0, h * HD:(h + 1) * HD], WT[:, ti, h, :], old[:, h, :],
                                                start=True, stop=True)
                    last.then_inc(old_mm, 1)
                pe.wait_ge(vnew_ready, ti + 1)
                for h in range(NH):
                    if ti > 0:
                        nc.tensor.matmul(ps[:, 1, h * HD:(h + 1) * HD], qdec[:, h, tok(ti)], old[:, h, :],
                                         start=True, stop=False)
                    last = nc.tensor.matmul(ps[:, 1, h * HD:(h + 1) * HD], attnT[:, ti, h, :], vnew[:, ti % 2, h, :],
                                            start=(ti == 0), stop=True)
                last.then_inc(out_mm, 1)
                for h in range(NH):
                    last = nc.tensor.matmul(ps[0:HD, 2, h * HD:(h + 1) * HD], kd[:, ti, h, :], vnew[:, ti % 2, h, :],
                                            start=True, stop=True)
                last.then_inc(out_mm, 1)

        @block.scalar
        def _(act):
            def take_uw(half):
                for tj in range(HT):
                    ti = HT * half + tj
                    act.wait_ge(uw_mm, ti + 1)
                    nc.scalar.activation(U[:, ti, :, :], ps[:, 4 + 2 * tj, 0:GW].rearrange("p (h d) -> p h d", h=NH),
                                         ACT.Copy).then_inc(uw_out, 1)
                    nc.scalar.activation(WT[:, ti, :, :], ps[0:HD, 5 + 2 * tj, :]
                                         .rearrange("p (h t) -> p h t", h=NH), ACT.Copy).then_inc(uw_out, 1)
            for n in range(2 * NH):
                act.wait_ge(bcast, n + 1)
                nc.scalar.activation(grow[:, n // NH, n % NH, :], ps[:, n, :], ACT.Copy).then_inc(bcast_out, 1)
            act.wait_ge(bcast_out, 2 * NH)
            nc.scalar.activation(qdec[:, :, :], grow[0:HD, 0, :, :], ACT.Exp).then_inc(exp_rows, 1)
            nc.scalar.activation(end[:, :, :], grow[0:HD, 0, :, P - 1::P], ACT.Exp).then_inc(exp_rows, 1)
            for ti in range(NT):
                if ti == HT:
                    take_uw(0)
                act.wait_ge(args_ready, ti + 1)
                if ti >= 1:
                    act.wait_ge(amats, ti)
                for h in range(NH):
                    nc.scalar.activation(expo[:, 0, h, :], work[:, 0, h, :], ACT.Exp, bias=T.cols[:, C_R, ti, h:h + 1])
                    nc.scalar.activation(expo[:, 1, h, :], work[:, 1, h, :], ACT.Exp, bias=T.neg_gc[:, ti, h:h + 1])
                    last = nc.scalar.activation(expo[:, 2, h, :], work[:, 2, h, :], ACT.Exp,
                                                bias=T.neg_gc[:, ti, h:h + 1])
                last.then_inc(expo_ready, 1)
            take_uw(1)
            act.wait_ge(mean_ready, 1)
            nc.scalar.activation(stat[:, 2, :, :], stat[:, 1, :, :], ACT.Sqrt).then_inc(root_ready, 1)
            act.wait_ge(root_ready, 1)
            nc.scalar.activation(vb[:, :, :, :], T.gdn_gates[:, :, 2 * NH:2 * NH + GW]
                                 .rearrange("p t (h d) -> p t h d", h=NH), ACT.Silu).then_inc(silu_done, 1)

        @block.vector
        def _(dve):
            link = linker(dve, chain)

            def heads(t, n=P):
                return t.unsqueeze(1).to_broadcast([P, NH, n])
            ktok = T.gdn_ktok[:, :, :].rearrange("p t (h d) -> p t h d", h=NH)
            vtok = T.gdn_vtok[:, :, :].rearrange("p t (h d) -> p t h d", h=NH)
            for out, src, col in ((vb, vtok, C_LB), (kb, ktok, C_R), (kd, ktok, C_KD)):
                for ti in range(NT):
                    last = nc.vector.tensor_tensor(out[:, ti, :, :], src[:, ti, :, :], T.exp_cols[:, col, ti, :]
                                                   .unsqueeze(2).to_broadcast([P, NH, HD]), ALU.mult)
                last.then_inc(scaled, 1)
            dve.wait_ge(exp_rows, 2)
            for h in range(NH):
                last = nc.vector.tensor_tensor(qdec[:, h, :], qdec[:, h, :], fm(0, h, slice(0, SEQ)), ALU.mult)
            last.then_inc(qdec_ready, 1)
            dve.wait_ge(bcast_out, 2 * NH)
            for half in range(2):
                if half:
                    dve.wait_ge(uw_mm, HT)
                for tj in range(HT):
                    ti = HT * half + tj
                    if ti >= 1:
                        dve.wait_ge(expo_ready, ti)
                    gc, r = grow[:, 0, :, tok(ti)], grow[:, 1, :, tok(ti)]
                    link(nc.vector.tensor_scalar_mul(work[:, 0, :, :], gc, -1.0))
                    nc.vector.tensor_tensor(work[:, 1, :, :], r, heads(T.const("mask_strict_t")), ALU.add)
                    nc.vector.tensor_tensor(work[:, 2, :, :], gc, heads(T.const("mask_t")), ALU.add)
                    link(nc.vector.tensor_tensor(work[:, 0, :, :], work[:, 0, :, :], heads(T.const("mask_strict")), ALU.add))
                    nc.vector.engine_nop().then_inc(args_ready, 1)
                    dve.wait_ge(grams, ti + 1)
                    dve.wait_ge(expo_ready, ti + 1)
                    gram = ps[:, 4 + 2 * tj, :].rearrange("p (h c) -> p h c", h=NH)
                    qk = ps[:, 5 + 2 * tj, :].rearrange("p (h c) -> p h c", h=NH)
                    diag, ident = heads(T.const("diag16")), heads(T.const("ident"))
                    nc.vector.tensor_tensor(AT[:, tj, :, :], gram, expo[:, 1, :, :], ALU.mult)
                    nc.vector.tensor_tensor(attnT[:, ti, :, :], qk, expo[:, 2, :, :], ALU.mult)
                    link(nc.vector.tensor_tensor(D[0][:, tj, :, :], gram, expo[:, 0, :, :], ALU.mult))
                    nc.vector.tensor_tensor(DT[0][:, tj, :, :], AT[:, tj, :, :], diag, ALU.mult)
                    link(nc.vector.tensor_tensor(D[0][:, tj, :, :], D[0][:, tj, :, :], diag, ALU.mult))
                    nc.vector.tensor_tensor(X[0][:, tj, :, :], ident, D[0][:, tj, :, :], ALU.subtract)
                    nc.vector.tensor_tensor(XT[0][:, tj, :, :], ident, DT[0][:, tj, :, :], ALU.subtract)
                    nc.vector.tensor_tensor(LT[:, tj, :, :], AT[:, tj, :, :], heads(T.const("below16_t")),
                                            ALU.mult).then_inc(lt_ready, 1)
                    dve.wait_ge(lt_ready, HT * len(level_steps) * half + tj + 1)
                    nc.vector.engine_nop().then_inc(amats, 1)
                for m, (_, _, out, old, sign) in enumerate(steps):
                    n = n_steps * half + m
                    for tj in range(HT):
                        dve.wait_ge(product, HT * n + tj + 1)
                        src = ps[:, 2 * (m % 2) + tj, :].rearrange("p (h c) -> p h c", h=NH)
                        if old is None:
                            nc.vector.tensor_copy(out[:, tj, :, :], src).then_inc(taken, 1)
                        else:
                            nc.vector.tensor_tensor(out[:, tj, :, :], old[:, tj, :, :], src,
                                                    ALU.add if sign > 0 else ALU.subtract).then_inc(taken, 1)
                    if m in level_steps[:-1]:
                        width = 32 << level_steps.index(m)
                        for tj in range(HT):
                            nc.vector.tensor_tensor(LT[:, tj, :, :], AT[:, tj, :, :], heads(T.const(f"below{width}_t")),
                                                    ALU.mult).then_inc(lt_ready, 1)
            dve.wait_ge(uw_out, 2 * NT)
            for ti in range(NT):
                new, old = state[:, ti % 2, :, :], state[:, (ti + 1) % 2, :, :]
                if ti == 0:
                    nc.vector.tensor_copy(vnew[:, 0, :, :], U[:, 0, :, :]).then_inc(vnew_ready, 1)
                else:
                    dve.wait_ge(old_mm, ti)
                    nc.vector.tensor_tensor(vnew[:, ti % 2, :, :], U[:, ti, :, :],
                                            ps[:, 0, 0:GW].rearrange("p (h d) -> p h d", h=NH),
                                            ALU.subtract).then_inc(vnew_ready, 1)
                dve.wait_ge(out_mm, 2 * ti + 1)
                nc.vector.tensor_copy(os_[:, ti, :, :],
                                      ps[:, 1, 0:GW].rearrange("p (h d) -> p h d", h=NH)).then_inc(out_taken, 1)
                dve.wait_ge(out_mm, 2 * ti + 2)
                added = ps[0:HD, 2, 0:GW].rearrange("p (h d) -> p h d", h=NH)
                if ti == 0:
                    nc.vector.tensor_copy(new, added).then_inc(out_taken, 1)
                else:
                    for h in range(NH):
                        last = nc.vector.scalar_tensor_tensor(new[:, h, :], old[:, h, :], end[:, h, ti:ti + 1],
                                                              added[:, h, :], ALU.mult, ALU.add)
                    last.then_inc(out_taken, 1)
                dve.wait_ge(out_taken, 2 * ti + 2)
            dve.wait_ge(gain_in, 16)
            square, normed = kb[:, :, :, :], kd[:, :, :, :]
            merged = "p t h d -> p (t h) d"
            head_norm(nc, dve, (mean_ready, root_ready), link, os_[:, :, :, :], square, stat,
                      gain[:, :].unsqueeze(1).to_broadcast([P, NT * NH, HD]), normed.rearrange(merged))
            dve.wait_ge(silu_done, 1)
            nc.vector.tensor_tensor(T.mix[:, :, 2 * GW:3 * GW].rearrange("p t (h d) -> p t h d", h=NH), normed,
                                    vb[:, :, :, :], ALU.mult)


def output_phase(nc, T, sem, layer, w_out):
    with ExitStack() as ctx:
        w = ctx.enter_context(nc.sbuf_tensor("w_out_buf", [P, KD, D_MODEL], F32))
        mixT = ctx.enter_context(nc.sbuf_tensor("mixT", [P, KD, SEQ], F32))
        ps = ctx.enter_context(nc.psum_tensor("ps_outp", [P, 8, BANK], F32))
        w_in, turned, turned_act, turned_dve = sem("w_out_in"), sem("mix_turned"), sem("mix_act"), sem("mix_dve")
        product = sem("outp_product")
        block = ctx.enter_context(nc.Block())

        @block.sync
        def _(sp):
            sp.dma_start(w[:, :, :], w_out[bass.ds(layer, 1), :, :]
                         .rearrange("a (k p) c -> p (a k) c", p=P)).then_inc(w_in, 16)

        @block.tensor
        def _(pe):
            for k in range(KD):
                for ti in range(NT):
                    last = nc.tensor.transpose(ps[:, k, tok(ti)], T.mix[:, ti, k * P:(k + 1) * P], T.const("ident"))
                last.then_inc(turned, 1)
            pe.wait_ge(turned_act, KD // 2)
            pe.wait_ge(turned_dve, KD // 2)
            pe.wait_ge(w_in, 16)
            for n in range(8):
                ti, half = n // 2, n % 2
                for k in range(KD):
                    last = nc.tensor.matmul(ps[:, n, :], mixT[:, k, tok(ti)], w[:, k, half * BANK:(half + 1) * BANK],
                                            start=(k == 0), stop=(k == KD - 1))
                last.then_inc(product, 1)

        @block.scalar
        def _(act):
            for k in range(0, KD, 2):
                act.wait_ge(turned, k + 1)
                nc.scalar.activation(mixT[:, k, :], ps[:, k, :], ACT.Copy).then_inc(turned_act, 1)

        @block.vector
        def _(dve):
            for k in range(1, KD, 2):
                dve.wait_ge(turned, k + 1)
                nc.vector.tensor_copy(mixT[:, k, :], ps[:, k, :]).then_inc(turned_dve, 1)
            for n in range(8):
                dve.wait_ge(product, n + 1)
                r = T.resid[:, n // 2, (n % 2) * BANK:(n % 2 + 1) * BANK]
                nc.vector.tensor_tensor(r, r, ps[:, n, :], ALU.add)


def query_phase(nc, T, sem, H, layer, w_q, sub_keys):
    PC = 2 * PH
    GC = 2
    GROUPS_Q = PC // GC
    with ExitStack() as ctx:
        wbuf = ctx.enter_context(nc.sbuf_tensor("w_q_buf", [P, 2, KD, GC * P], F32))
        w_r = ctx.enter_context(nc.sbuf_tensor("w_q_r", [P, 2, 2, KD, GC * P], F32R))
        keys = H.hidden[:, :, :, :].rearrange("p a b (c d) -> p (a b c) d", d=P)
        ps = ctx.enter_context(nc.psum_tensor("ps_query", [P, 8, BANK], F32))
        keys_in, w_in = sem("sub_keys_in"), [sem("w_q_in0"), sem("w_q_in1")]
        turned, turned_out, product = sem("sub_keys_turned"), sem("sub_keys_out"), sem("query_product")
        w_hi, w_lo, out_done = sem("w_q_hi"), sem("w_q_lo"), sem("query_out")
        block = ctx.enter_context(nc.Block())

        @block.sync
        def _(sp):
            for g in range(GROUPS_Q):
                if g >= 2:
                    sp.wait_ge(w_lo, g - 1)
                sp.dma_start(wbuf[:, g % 2, :, :], w_q[bass.ds(layer, 1), :, g * GC * P:(g + 1) * GC * P]
                             .rearrange("a (k p) c -> p (a k) c", p=P)).then_inc(w_in[g % 2], 16)
                if g == 0:
                    for h in range(0, PH, PH // 2):
                        sp.dma_start(keys[:, 2 * h:2 * h + PH, :], sub_keys[bass.ds(layer, 1), h:h + PH // 2, :, :, :]
                                     .rearrange("a p c n d -> n (a p c) d")).then_inc(keys_in, 16)

        @block.tensor
        def _(pe):
            pe.wait_ge(keys_in, 32)
            for b in range(4):
                for i in range(4):
                    last = nc.tensor.transpose(ps[:, b, tok(i)], keys[:, 4 * b + i, :], T.const("ident"))
                last.then_inc(turned, 1)
            for n in range(PC):
                if n % GC == 0:
                    pe.wait_ge(w_lo, n // GC + 1)
                if n < 4:
                    pe.wait_ge(turned_out, n + 1)
                if n >= 8:
                    pe.wait_ge(out_done, n - 7)
                for m, (x, y) in enumerate(((0, 0), (0, 1), (1, 0))):
                    for k in range(KD):
                        last = nc.tensor.matmul(ps[:, n % 8, :], w_r[:, (n // GC) % 2, x, k, tok(n % GC)],
                                                T.xn_r[:, y, k, :], start=(m == 0 and k == 0),
                                                stop=(m == 2 and k == KD - 1))
                last.then_inc(product, 1)

        @block.scalar
        def _(act):
            def copy_out(n):
                act.wait_ge(product, n + 1)
                nc.scalar.activation(T.peer_q[:, n, :], ps[:, n % 8, :], ACT.Copy).then_inc(out_done, 1)
            for g in range(GROUPS_Q):
                act.wait_ge(w_in[g % 2], 16 * (g // 2 + 1))
                if g >= 2:
                    act.wait_ge(product, (g - 1) * GC)
                nc.scalar.activation(w_r[:, g % 2, 0, :, :].rearrange("p k c -> p (k c)"),
                                     wbuf[:, g % 2, :, :].rearrange("p k c -> p (k c)"), ACT.Copy).then_inc(w_hi, 1)
                if g >= 2:
                    for n in range((g - 2) * GC, (g - 1) * GC):
                        copy_out(n)
            for n in range((GROUPS_Q - 2) * GC, PC):
                copy_out(n)

        @block.vector
        def _(dve):
            for g in range(GROUPS_Q):
                dve.wait_ge(w_hi, g + 1)
                nc.vector.tensor_tensor(w_r[:, g % 2, 1, :, :], wbuf[:, g % 2, :, :],
                                        w_r[:, g % 2, 0, :, :].bitcast(F32), ALU.subtract).then_inc(w_lo, 1)
                if g == 0:
                    for b in range(4):
                        dve.wait_ge(turned, b + 1)
                        nc.vector.tensor_copy(T.peer_k[:, 4 * b:4 * b + 4, :],
                                              ps[:, b, :].rearrange("p (i n) -> p i n", i=4)).then_inc(turned_out, 1)


class HiddenTiles:

    STORED = NK // 2
    AHEAD_TURNED, AHEAD_LO, AHEAD_MM, AHEAD_DONE = 3, 1, 2, 1

    def __init__(self, nc, T, stack, sem, layer, u_tab, hidden_dram):
        def sb(name, shape, dtype=F32):
            return stack.enter_context(nc.sbuf_tensor(name, shape, dtype))
        self.nc, self.T, self.layer, self.dram = nc, T, layer, hidden_dram
        self.u_by_key = u_tab.rearrange("l (i j) d -> l i j d", j=NK)
        self.u_buf = sb("u_buf", [P, 2, 2, D_MODEL])
        self.u_turned = sb("u_turned", [P, KD * P])
        self.uT = sb("uT", [P, 2, 2, KD * P], F32R)
        self.hidden = sb("hidden", [P, 2, 2, SEQ])
        self.u_in = [sem("u_in0"), sem("u_in1")]
        self.turned, self.u_hi, self.u_lo = sem("u_turned"), sem("u_hi"), sem("u_lo")
        self.hidden_mm, self.hidden_done = sem("hidden_mm"), sem("hidden_done")
        self.stored = [sem("hidden_stored0"), sem("hidden_stored1")]

    def take_banks(self, stack):
        self.ps_u = stack.enter_context(self.nc.psum_tensor("ps_uT", [P, KD * P], F32))
        self.ps_h = stack.enter_context(self.nc.psum_tensor("ps_hidden", [P, BANK], F32))

    def first_counts(self, pool):
        pool.sem_inc(self.turned, self.AHEAD_TURNED)
        pool.sem_inc(self.u_lo, self.AHEAD_LO)
        pool.sem_inc(self.hidden_mm, self.AHEAD_MM)
        pool.sem_inc(self.hidden_done, self.AHEAD_DONE)
        for s in self.stored:
            pool.sem_inc(s, 16)

    def load(self, sp, g, p):
        sp.wait_ge(self.turned, g * 2 + (self.AHEAD_TURNED - 2))
        sp.dma_start(self.u_buf[:, p, :, :], self.u_by_key[bass.ds(self.layer, 1), :, bass.ds(g * 2, 2), :]
                     .rearrange("a i j d -> i (a j) d")).then_inc(self.u_in[p], 16)

    def turn(self, pe, n, p, e):
        if e == 0:
            pe.wait_ge(self.u_in[p], (n - 2 * p) * 4 + 16)
        pe.wait_ge(self.u_lo, n + self.AHEAD_LO)
        for k in range(KD):
            last = self.nc.tensor.transpose(self.ps_u[:, tok(k)], self.u_buf[:, p, e, tok(k)], self.T.const("ident"))
        last.then_inc(self.turned, 1)

    def split_hi(self, act, n, e):
        act.wait_ge(self.turned, n + (1 + self.AHEAD_TURNED))
        act.wait_ge(self.hidden_mm, n + (self.AHEAD_MM - 1))
        self.nc.scalar.activation(self.u_turned[:, :], self.ps_u[:, :], ACT.Copy)
        self.nc.scalar.activation(self.uT[:, e, 0, :], self.ps_u[:, :], ACT.Copy).then_inc(self.u_hi, 1)

    def split_lo(self, pool, n, e):
        pool.wait_ge(self.u_hi, n + 1)
        self.nc.gpsimd.tensor_tensor(self.uT[:, e, 1, :], self.u_turned[:, :], self.uT[:, e, 0, :].bitcast(F32),
                                     ALU.subtract).then_inc(self.u_lo, 1)

    def multiply(self, pe, n, e, parts=range(3)):
        for m in parts:
            a, b = ((0, 0), (0, 1), (1, 0))[m]
            if m == 0:
                pe.wait_ge(self.u_lo, n + (1 + self.AHEAD_LO))
                pe.wait_ge(self.hidden_done, n + self.AHEAD_DONE)
            for k in range(KD):
                last = self.nc.tensor.matmul(self.ps_h[:, :], self.uT[:, e, a, tok(k)], self.T.xn_r[:, b, k, :],
                                             start=(m == 0 and k == 0), stop=(m == 2 and k == KD - 1))
            if m == 2:
                last.then_inc(self.hidden_mm, 1)

    def gelu(self, act, n, p, e, free=None, count=None):
        act.wait_ge(self.hidden_mm, n + (1 + self.AHEAD_MM))
        if free is None:
            if e == 0:
                act.wait_ge(self.stored[p], (n - 2 * p) * 4 + 16)
        else:
            act.wait_ge(free, count)
        self.nc.scalar.activation(self.hidden[:, p, e, :], self.ps_h[:, :], ACT.Gelu).then_inc(self.hidden_done, 1)

    def store(self, sp, g, p):
        sp.wait_ge(self.hidden_done, g * 2 + (2 + self.AHEAD_DONE))
        sp.dma_start(self.dram[:, bass.ds(g * 2, 2), :], self.hidden[:, p, :, :]).then_inc(self.stored[p], 16)

    def wait_stored(self, sp, groups):
        for s in self.stored:
            sp.wait_ge(s, 16 * (groups // 2 + 1))


def select_phase(nc, T, sem, H):
    PC = 2 * PH
    HG = 4
    LOW = -3.0e38
    with ExitStack() as ctx:
        def sb(name, shape, dtype=F32):
            return ctx.enter_context(nc.sbuf_tensor(name, shape, dtype))
        rest = sb("sel_rest", [P, PC, NK])
        best = sb("sel_best", [P, PC, TOPK])
        where = sb("sel_where", [P, PC, TOPK], U32)
        where_f = sb("sel_where_f", [P, PC, TOPK])
        cand = sb("sel_cand", [P, PH, TOPK * TOPK])
        cand_rest = sb("sel_cand_rest", [P, PH, TOPK * TOPK])
        top = sb("sel_top", [P, PH, TOPK])
        at = sb("sel_at", [P, PH, TOPK], U32)
        at_half = sb("sel_at_half", [P, 2, PH, TOPK], U32)
        at_f = sb("sel_at_f", [P, 2, PH, TOPK])
        same = sb("sel_same", [P, PH * TOPK, TOPK])
        chosen = sb("sel_chosen", [P, 2, 3, PH, TOPK])
        shifted = sb("sel_shifted", [P, PH, TOPK])
        expd = sb("sel_exp", [P, PH, TOPK])
        total = sb("sel_total", [P, 2, PH])
        ps = ctx.enter_context(nc.psum_tensor("ps_select", [P, 4, BANK], F32))
        ps_t = ctx.enter_context(nc.psum_tensor("ps_pick", [P, BANK], F32))
        scored, read, chain, shifted_ready = sem("sel_scored"), sem("sel_read"), sem("sel_chain"), sem("sel_shifted")
        exp_done, chosen_ready, turned, turned_out = (sem("sel_exp_done"), sem("sel_chosen"), sem("sel_turned"),
                                                      sem("sel_turned_out"))
        block = ctx.enter_context(nc.Block())

        def hidden_groups(engine, ti, step):
            with engine.Fori(0, HG // 2) as it:
                for p in range(2):
                    step(it * 2 + (HG * ti + p), p)

        @block.sync
        def _(sp):
            def step(g, p):
                H.load(sp, g + 2, p)
                H.store(sp, g, p)
            H.load(sp, 0, 0)
            H.load(sp, 1, 1)
            for ti in range(NT):
                hidden_groups(sp, ti, step)
            H.wait_stored(sp, NT * HG)

        @block.tensor
        def _(pe):
            def step(g, p):
                for e in range(2):
                    H.turn(pe, g * 2 + (e + 1), (p + e) % 2, 1 - e)
                    H.multiply(pe, g * 2 + e, e)

            def score(ti):
                if ti >= 1:
                    pe.wait_ge(read, ti)
                for pc in range(PC):
                    last = nc.tensor.matmul(ps[:, pc // 4, tok(pc % 4)], T.peer_q[:, pc, tok(ti)],
                                            T.peer_k[:, pc, :], start=True, stop=True)
                last.then_inc(scored, 1)

            def turn_choice(ti):
                pe.wait_ge(chosen_ready, ti + 1)
                if ti >= 1:
                    pe.wait_ge(turned_out, ti)
                for c in range(3):
                    last = nc.tensor.transpose(ps_t[:, tok(c)], chosen[:, ti % 2, c, :, :].rearrange("p h k -> p (h k)"),
                                               T.const("ident"))
                last.then_inc(turned, 1)
            score(0)
            H.turn(pe, 0, 0, 0)
            for ti in range(NT):
                hidden_groups(pe, ti, step)
                if ti + 1 < NT:
                    score(ti + 1)
                if ti >= 1:
                    turn_choice(ti - 1)
            turn_choice(NT - 1)

        @block.scalar
        def _(act):
            def step(g, p):
                for e in range(2):
                    H.split_hi(act, g * 2 + (e + 1), 1 - e)
                    H.gelu(act, g * 2 + e, p, e)

            def copy_choice(ti):
                act.wait_ge(turned, ti + 1)
                nc.scalar.activation(T.pick[:, :, tok(ti)], ps_t[:, 0:3 * P].rearrange("p (c t) -> p c t", c=3),
                                     ACT.Copy).then_inc(turned_out, 1)
            H.split_hi(act, 0, 0)
            for ti in range(NT):
                hidden_groups(act, ti, step)
                act.wait_ge(shifted_ready, ti + 1)
                nc.scalar.activation(expd[:, :, :], shifted[:, :, :], ACT.Exp).then_inc(exp_done, 1)
                if ti >= 1:
                    copy_choice(ti - 1)
            copy_choice(NT - 1)

        @block.gpsimd
        def _(pool):
            H.first_counts(pool)
            H.split_lo(pool, 0, 0)
            with pool.Fori(0, NT * HG) as g:
                for e in range(2):
                    H.split_lo(pool, g * 2 + (e + 1), 1 - e)

        @block.vector
        def _(dve):
            link = linker(dve, chain)

            def finish(ti):
                dve.wait_ge(exp_done, ti + 1)
                link(nc.vector.tensor_reduce(total[:, 0, :], expd[:, :, :], AX.X, ALU.add))
                link(nc.vector.reciprocal(total[:, 1, :], total[:, 0, :]))
                nc.vector.tensor_tensor(chosen[:, ti % 2, 2, :, :], expd[:, :, :],
                                        total[:, 1, :].unsqueeze(2).to_broadcast([P, PH, TOPK]),
                                        ALU.mult).then_inc(chosen_ready, 1)
            for ti in range(NT):
                dve.wait_ge(scored, ti + 1)

                def score(pc):
                    return ps[:, pc // 4, tok(pc % 4)]
                for pc in range(PC):
                    last = nc.vector.max(best[:, pc, 0:8], score(pc))
                link(last)
                for pc in range(PC):
                    nc.vector.max_index(where[:, pc, 0:8], best[:, pc, 0:8], score(pc))
                    last = nc.vector.match_replace(rest[:, pc, :], best[:, pc, 0:8], score(pc), LOW)
                last.then_inc(read, 1)
                dve.wait_ge(read, ti + 1)
                for pc in range(PC):
                    last = nc.vector.max(best[:, pc, 8:16], rest[:, pc, :])
                link(last)
                for pc in range(PC):
                    last = nc.vector.max_index(where[:, pc, 8:16], best[:, pc, 8:16], rest[:, pc, :])
                link(last)
                link(nc.vector.tensor_copy(where_f[:, :, :], where[:, :, :]))
                if ti >= 1:
                    finish(ti - 1)
                pair = best[:, :, :].rearrange("p (h c) k -> p c h k", c=2)
                link(nc.vector.tensor_tensor(cand[:, :, :].rearrange("p h (a b) -> p h a b", a=TOPK),
                                             pair[:, 0].unsqueeze(3).to_broadcast([P, PH, TOPK, TOPK]),
                                             pair[:, 1].unsqueeze(2).to_broadcast([P, PH, TOPK, TOPK]), ALU.add))
                for h in range(PH):
                    last = nc.vector.max(top[:, h, 0:8], cand[:, h, :])
                link(last)
                for h in range(PH):
                    nc.vector.max_index(at[:, h, 0:8], top[:, h, 0:8], cand[:, h, :])
                    last = nc.vector.match_replace(cand_rest[:, h, :], top[:, h, 0:8], cand[:, h, :], LOW)
                link(last)
                for h in range(PH):
                    last = nc.vector.max(top[:, h, 8:16], cand_rest[:, h, :])
                link(last)
                nc.vector.tensor_tensor(shifted[:, :, :], top[:, :, :],
                                        top[:, :, 0:1].to_broadcast([P, PH, TOPK]), ALU.subtract).then_inc(shifted_ready, 1)
                for h in range(PH):
                    last = nc.vector.max_index(at[:, h, 8:16], top[:, h, 8:16], cand_rest[:, h, :])
                link(last)
                nc.vector.tensor_single_scalar(at_half[:, 0, :, :], at[:, :, :], 4, ALU.logical_shift_right)
                link(nc.vector.tensor_single_scalar(at_half[:, 1, :, :], at[:, :, :], TOPK - 1, ALU.bitwise_and))
                link(nc.vector.tensor_copy(at_f[:, :, :, :], at_half[:, :, :, :]))
                if ti >= 2:
                    dve.wait_ge(turned, ti - 1)
                ranks = T.const("iota")[:, 0:TOPK].unsqueeze(1).to_broadcast([P, PH * TOPK, TOPK])
                numbers = where_f[:, :, :].rearrange("p (h c) k -> p c h k", c=2)
                for c in range(2):
                    link(nc.vector.tensor_tensor(same[:, :, :], at_f[:, c, :, :].rearrange("p h k -> p (h k)")
                                                 .unsqueeze(2).to_broadcast([P, PH * TOPK, TOPK]), ranks, ALU.is_equal))
                    by_head = same[:, :, :].rearrange("p (h k) r -> p h k r", h=PH)
                    link(nc.vector.tensor_tensor(by_head, by_head, numbers[:, c].unsqueeze(2)
                                                 .to_broadcast([P, PH, TOPK, TOPK]), ALU.mult))
                    link(nc.vector.tensor_reduce(chosen[:, ti % 2, c, :, :].rearrange("p h k -> p (h k)"), same[:, :, :],
                                                 AX.X, ALU.add))
            finish(NT - 1)


def gate_map_phase(nc, T, sem, H, gates_dram):
    TG = 4
    HOT = 4
    PER_BLOCK = GB // TG
    TILES = PER_BLOCK // 4
    FIRST = NK // 4
    with ExitStack() as ctx:
        first = ctx.enter_context(nc.sbuf_tensor("map_first", [P, HOT, TG, NK], F32))
        second = ctx.enter_context(nc.sbuf_tensor("map_second", [P, HOT, TG, NK], F32))
        tile = ctx.enter_context(nc.sbuf_tensor("map_tile", [P, 2, NK, GB], F32))
        ps = ctx.enter_context(nc.psum_tensor("ps_map", [P, HOT, BANK], F32))
        hot_free, bank_free = sem("map_hot_free"), sem("map_bank_free")
        hot_ready = sem("map_hot_ready")
        stored = [sem("map_stored0"), sem("map_stored1")]
        block = ctx.enter_context(nc.Block())

        @block.vector
        def _(dve):
            dve.sem_inc(hot_free, HOT)
            with dve.Fori(0, SEQ // (TG * HOT)) as it:
                for u in range(HOT):
                    dve.wait_ge(hot_free, it * HOT + (u + 1))
                    for i in range(TG):
                        t = it * (HOT * TG) + (TG * u + i)
                        nc.vector.tensor_scalar(first[:, u, i, :], T.const("iota"),
                                                T.pick[:, 0, bass.ds(t, 1)], None, ALU.is_equal)
                        last = nc.vector.tensor_scalar(second[:, u, i, :], T.const("iota"),
                                                       T.pick[:, 1, bass.ds(t, 1)], T.pick[:, 2, bass.ds(t, 1)],
                                                       ALU.is_equal, ALU.mult)
                    last.then_inc(hot_ready, 1)

        @block.tensor
        def _(pe):
            def spread(m, u):
                pe.wait_ge(hot_ready, m + 1)
                pe.wait_ge(bank_free, m + 1)
                for i in range(TG):
                    last = nc.tensor.matmul(ps[:, u, tok(i)], first[:, u, i, :], second[:, u, i, :],
                                            start=True, stop=True)
                last.then_inc(hot_free, 1)
            with pe.Fori(0, SEQ // GB) as it:
                for s in range(TILES):
                    n, m = it * TILES + (FIRST + s), it * PER_BLOCK + 4 * s
                    H.turn(pe, n + 1, (s + 1) // 2 % 2, (s + 1) % 2)
                    spread(m, 0)
                    for part in range(3):
                        H.multiply(pe, n, s % 2, (part,))
                        spread(m + (part + 1), part + 1)

        @block.scalar
        def _(act):
            act.sem_inc(bank_free, HOT)
            with act.Fori(0, SEQ // GB // 2) as it:
                for half in range(2):
                    act.wait_ge(stored[half], it * 16 + 16)
                    for s in range(TILES):
                        n, m = (it * 2 + half) * TILES + (FIRST + s), (it * 2 + half) * PER_BLOCK + 4 * s
                        H.split_hi(act, n + 1, (s + 1) % 2)
                        for u in range(4):
                            if u == 3:
                                H.gelu(act, n, s // 2 % 2, s % 2)
                            act.wait_ge(hot_free, m + (u + 1 + HOT))
                            nc.scalar.activation(tile[:, half, :, (4 * s + u) * TG:(4 * s + u + 1) * TG],
                                                 ps[:, u, :].rearrange("p (t j) -> p j t", t=TG),
                                                 ACT.Copy).then_inc(bank_free, 1)

        @block.gpsimd
        def _(pool):
            for s in stored:
                pool.sem_inc(s, 16)
            with pool.Fori(0, NK // 4 // 2) as g:
                for e in range(2):
                    H.split_lo(pool, g * 2 + (FIRST + e + 1), 1 - e)

        @block.sync
        def _(sp):
            with sp.Fori(0, SEQ // GB // 2) as it:
                for half in range(2):
                    tb = it * 2 + half
                    for p in range(TILES // 2):
                        g = tb * (TILES // 2) + (FIRST // 2 + p)
                        H.load(sp, g + 2, p)
                        H.store(sp, g, p)
                    sp.wait_ge(bank_free, tb * PER_BLOCK + (HOT + PER_BLOCK))
                    sp.dma_start(gates_dram[:, bass.ds(tb, 1), :, :].rearrange("i a j t -> i (a j) t"),
                                 tile[:, half, :, :]).then_inc(stored[half], 16)
            H.wait_stored(sp, NK // 4)
            for s in stored:
                sp.wait_ge(s, 16 * (SEQ // GB // 2 + 1))


def expert_phase(nc, T, sem, H, layer, v_tab, gates_dram, hidden_dram):
    OLD, NEW = 0, 1
    STEPS = H.STORED // 2
    YB = 2 * NT
    BANKS = 4
    with ExitStack() as ctx:
        def sb(name, shape, dtype=F32):
            return ctx.enter_context(nc.sbuf_tensor(name, shape, dtype))
        v_buf = sb("v_buf", [P, 2, 2, D_MODEL])
        g_buf = sb("g_buf", [P, 2, SEQ // GB, 2, GB])
        old_hidden = sb("old_hidden", [P, 2, SEQ])
        weight = sb("weight", [P, 2, 2, SEQ])
        weight_r = sb("weight_r", [P, 2, 2, 2, SEQ], F32R)
        v_r = sb("v_r", [P, 2, 2, 2, D_MODEL], F32R)
        ps_y = ctx.enter_context(nc.psum_tensor("ps_y", [P, BANKS, BANK], F32))
        v_in, g_in, weighted, v_hi, v_lo, w_hi, w_lo = ([sem(f"{x}_{kind}") for kind in ("old", "new")] for x in (
            "v_in", "g_in", "weighted", "v_hi", "v_lo", "w_hi", "w_lo"))
        h_in, y_mm, y_added = sem("h_in"), sem("y_mm"), sem("y_added")
        AHEAD_MM, AHEAD_ADDED, AHEAD_LO, AHEAD_WEIGHTED = 1, BANKS, 2, 2
        block = ctx.enter_context(nc.Block())
        v_by_key = v_tab.rearrange("l (i j) d -> l i j d", j=NK)

        def all_steps(engine, step):
            with engine.Fori(0, (STEPS - 2) // 2) as it:
                for p in range(2):
                    step(it * 2 + p, p, 2)
            step(STEPS - 2, 0, 1)
            step(STEPS - 1, 1, 0)

        @block.sync
        def _(sp):
            def keys(k, kind):
                return bass.ds(k * 2 + (H.STORED if kind == NEW else 0), 2)

            def load_v(k, kind):
                sp.dma_start(v_buf[:, kind, :, :], v_by_key[bass.ds(layer, 1), :, keys(k, kind), :]
                             .rearrange("a i j d -> i (a j) d")).then_inc(v_in[kind], 16)

            def load_gates(k, kind):
                sp.dma_start(g_buf[:, kind, :, :, :], gates_dram[:, :, keys(k, kind), :]).then_inc(g_in[kind], 16)
                if kind == OLD:
                    sp.dma_start(old_hidden[:, :, :], hidden_dram[:, bass.ds(k * 2, 2), :]).then_inc(h_in, 16)

            def step(k, p, after):
                if after == 2:
                    H.load(sp, k + (H.STORED // 2 + 2), p)
                if after >= 1:
                    sp.wait_ge(v_lo[NEW], k * 2 + 2)
                    load_v(k + 1, NEW)
                    sp.wait_ge(weighted[NEW], k * 2 + (2 + AHEAD_WEIGHTED))
                    load_gates(k + 1, NEW)
                if after == 2:
                    sp.wait_ge(weighted[OLD], k * 2 + (4 + AHEAD_WEIGHTED))
                    load_gates(k + 2, OLD)
                    sp.wait_ge(v_lo[OLD], k * 2 + 4)
                    load_v(k + 2, OLD)
            for kind in (OLD, NEW):
                load_v(0, kind)
                load_gates(0, kind)
            sp.wait_ge(weighted[OLD], 2 + AHEAD_WEIGHTED)
            load_gates(1, OLD)
            sp.wait_ge(v_lo[OLD], 2)
            load_v(1, OLD)
            all_steps(sp, step)

        @block.tensor
        def _(pe):
            def output(k, kind, parts):
                for b in parts:
                    if b == 0:
                        pe.wait_ge(w_lo[kind], k * 2 + (2 + AHEAD_LO))
                        pe.wait_ge(v_lo[kind], k * 2 + 2)
                    pe.wait_ge(y_added, k * (2 * YB) + (kind * YB + b + 1))
                    for i in range(2):
                        for n, (x, y) in enumerate(((0, 0), (0, 1), (1, 0))):
                            last = nc.tensor.matmul(ps_y[:, b % BANKS, :], weight_r[:, kind, i, x, tok(b // 2)],
                                                    v_r[:, kind, i, y, (b % 2) * BANK:(b % 2 + 1) * BANK],
                                                    start=(i == 0 and n == 0), stop=(i == 1 and n == 2))
                    last.then_inc(y_mm, 1)

            def step(k, p, after):
                for e in range(2):
                    n = k * 2 + (H.STORED + e)
                    if e == 0 or after >= 1:
                        H.turn(pe, n + 1, (p + e) % 2, 1 - e)
                    H.multiply(pe, n, e)
                    output(k, OLD, range(e * YB // 2, (e + 1) * YB // 2))
                output(k, NEW, range(YB))
            all_steps(pe, step)

        @block.scalar
        def _(act):
            def value_hi(k, kind):
                act.wait_ge(v_in[kind], k * 16 + 16)
                act.wait_ge(y_mm, k * (2 * YB) + (AHEAD_MM if kind == NEW else AHEAD_MM - YB))
                for e in range(2):
                    nc.scalar.activation(v_r[:, kind, e, 0, :], v_buf[:, kind, e, :], ACT.Copy).then_inc(v_hi[kind], 1)

            def weight_hi(k, kind, e):
                act.wait_ge(weighted[kind], k * 2 + (e + 1 + AHEAD_WEIGHTED))
                nc.scalar.activation(weight_r[:, kind, e, 0, :], weight[:, kind, e, :], ACT.Copy).then_inc(w_hi[kind], 1)

            def step(k, p, after):
                n = k * 2 + H.STORED
                H.split_hi(act, n + 1, 1)
                value_hi(k, NEW)
                for e in range(2):
                    H.gelu(act, n + e, 0, e, weighted[NEW], k * 2 + (e - 1 + AHEAD_WEIGHTED))
                    weight_hi(k, NEW, e)
                    if e == 0 and after >= 1:
                        H.split_hi(act, n + 2, 0)
                if after >= 1:
                    value_hi(k + 1, OLD)
                    weight_hi(k + 1, OLD, 0)
                    weight_hi(k + 1, OLD, 1)
            act.wait_ge(v_in[OLD], 16)
            for e in range(2):
                nc.scalar.activation(v_r[:, OLD, e, 0, :], v_buf[:, OLD, e, :], ACT.Copy).then_inc(v_hi[OLD], 1)
                weight_hi(0, OLD, e)
            all_steps(act, step)

        @block.vector
        def _(dve):
            dve.sem_inc(y_added, AHEAD_ADDED)
            dve.sem_inc(y_mm, AHEAD_MM)
            for kind in (OLD, NEW):
                dve.sem_inc(w_lo[kind], AHEAD_LO)
                dve.sem_inc(weighted[kind], AHEAD_WEIGHTED)

            def weigh(k, kind, e):
                if e == 0:
                    dve.wait_ge(g_in[kind], k * 16 + 16)
                if kind == OLD:
                    if e == 0:
                        dve.wait_ge(h_in, k * 16 + 16)
                else:
                    dve.wait_ge(H.hidden_done, k * 2 + (H.STORED + e + 1 + H.AHEAD_DONE))
                dve.wait_ge(w_lo[kind], k * 2 + (e - 1 + AHEAD_LO))
                source = old_hidden[:, e, :] if kind == OLD else H.hidden[:, 0, e, :]
                nc.vector.tensor_tensor(weight[:, kind, e, :].rearrange("p (b t) -> p b t", t=GB),
                                        source.rearrange("p (b t) -> p b t", t=GB), g_buf[:, kind, :, e, :],
                                        ALU.mult).then_inc(weighted[kind], 1)

            def add(k, kind, parts):
                for b in parts:
                    if b == 0:
                        dve.wait_ge(y_added, k * (2 * YB) + (kind * YB + AHEAD_ADDED))
                    dve.wait_ge(y_mm, k * (2 * YB) + (kind * YB + b + 1 + AHEAD_MM))
                    r = T.resid[:, b // 2, (b % 2) * BANK:(b % 2 + 1) * BANK]
                    nc.vector.tensor_tensor(r, r, ps_y[:, b % BANKS, :], ALU.add).then_inc(y_added, 1)

            def step(k, p, after):
                for e in range(2):
                    weigh(k, NEW, e)
                    add(k, OLD, range(e * YB // 2, (e + 1) * YB // 2))
                if after >= 1:
                    weigh(k + 1, OLD, 0)
                    weigh(k + 1, OLD, 1)
                add(k, NEW, range(YB))
            weigh(0, OLD, 0)
            weigh(0, OLD, 1)
            all_steps(dve, step)

        @block.gpsimd
        def _(pool):
            def value_lo(k, kind):
                for e in range(2):
                    pool.wait_ge(v_hi[kind], k * 2 + (e + 1))
                    nc.gpsimd.tensor_tensor(v_r[:, kind, e, 1, :], v_buf[:, kind, e, :],
                                            v_r[:, kind, e, 0, :].bitcast(F32), ALU.subtract).then_inc(v_lo[kind], 1)

            def weight_lo(k, kind, e):
                pool.wait_ge(w_hi[kind], k * 2 + (e + 1))
                nc.gpsimd.tensor_tensor(weight_r[:, kind, e, 1, :], weight[:, kind, e, :],
                                        weight_r[:, kind, e, 0, :].bitcast(F32), ALU.subtract).then_inc(w_lo[kind], 1)

            def step(k, p, after):
                n = k * 2 + H.STORED
                H.split_lo(pool, n + 1, 1)
                value_lo(k, NEW)
                weight_lo(k, NEW, 0)
                if after >= 1:
                    H.split_lo(pool, n + 2, 0)
                weight_lo(k, NEW, 1)
                if after >= 1:
                    value_lo(k + 1, OLD)
                    weight_lo(k + 1, OLD, 0)
                    weight_lo(k + 1, OLD, 1)
            value_lo(0, OLD)
            weight_lo(0, OLD, 0)
            weight_lo(0, OLD, 1)
            all_steps(pool, step)


_INS = ["x", "positions", "t5_table", "norm1_g", "norm2_g", "final_norm_g", "w_in", "w_out", "nsa_w_cmp_k",
        "nsa_w_cmp_v", "nsa_cmp_pos", "mlstm_i_bias", "mlstm_f_bias", "mlstm_norm_g", "gdn_conv_w", "gdn_a_log",
        "gdn_dt_bias", "gdn_norm_g", "mla_q_norm_g", "mla_kv_norm_g", "mla_w_uq", "mla_w_ukv", "peer_w_q",
        "peer_sub_keys", "peer_u", "peer_v"]


def program(nc, ins, consts, out):
    T = Tensors()
    bias_dram = nc.dram_tensor("bias_by_distance", [NH, 640 + SEQ], F32, kind="Internal").ap()
    gates_dram = nc.dram_tensor("gates", [NK, SEQ // GB, NK, GB], F32, kind="Internal").ap()
    hidden_dram = nc.dram_tensor("hidden_tiles", [P, HiddenTiles.STORED, SEQ], F32, kind="Internal").ap()
    with ExitStack() as ctx:
        ctx.enter_context(nc.allow_non_contiguous_dma(reason="a few KB of gains, positions and taps"))
        def once(name):
            return ctx.enter_context(nc.semaphore(name))

        def semaphores(stack, kept):
            def sem(name):
                kept.append(stack.enter_context(nc.semaphore(name)))
                return kept[-1]
            return sem

        def zero(kept):
            with nc.Block() as block:
                @block.gpsimd
                def _(pool):
                    for s in kept:
                        pool.sem_clear(s)

        def sb(name, shape, where=None):
            return (where or ctx).enter_context(nc.sbuf_tensor(name, shape, F32))
        T.consts = sb("consts", [P, CONSTS_SHAPE[1] - SEQ])
        T.resid = sb("resid", [P, NT, D_MODEL])
        T.biasq = sb("biasq", [P, NH, SEQ])
        T.biasc = sb("biasc", [P, NH, NT, N_CMP])
        T.cossin = sb("cossin", [P, NT, 2, 16])

        def const(name, row=0, rows=P, width=None):
            at, full = CONST_COLS[name]
            return T.consts[row:row + rows, at:at + (width or full)]
        T.const = const
        setup_phase(nc, T, once, ins["x"], ins["positions"], ins["t5_table"], consts, bias_dram)

        def gain_columns(g, layer):
            return g[bass.ds(layer, 1), :].rearrange("a (k p) -> p (a k)", p=P)
        with nc.Fori(0, DEPTH) as layer:
            with ExitStack() as mixer:
                used = []
                sem = semaphores(mixer, used)
                T.mix = sb("mix", [P, NT, D_MODEL], mixer)
                T.gdn_gates = sb("gdn_gates", [P, NT, GW + 2 * NH], mixer)
                T.gdn_fm = sb("gdn_fm", [P, 6, SEQ], mixer)
                T.gdn_fm_odd = sb("gdn_fm_odd", [HD, 4, SEQ], mixer)
                T.gdn_ktok = sb("gdn_ktok", [P, NT, GW], mixer)
                T.gdn_vtok = sb("gdn_vtok", [P, NT, GW], mixer)
                T.cols = sb("cols", [P, 6, NT, NH], mixer)
                T.exp_cols = sb("exp_cols", [P, 6, NT, NH], mixer)
                T.neg_gc = sb("neg_gc", [P, NT, NH], mixer)
                T.rows = sb("rows", [NH, 3, SEQ], mixer)
                T.headrow = sb("headrow", [NH, NH, P], mixer)
                with ExitStack() as early:
                    T.nsa_q = sb("nsa_q", [HD, NH, SEQ], early)
                    T.cmp_kv = sb("cmp_kv", [HD, 2, SEQ], early)
                    T.nsa_k = sb("nsa_k", [HD, 2, SEQ], early)
                    T.nsa_tm = sb("nsa_tm", [P, NT, NSA_IN - 448], early)
                    T.ml_q = sb("ml_q", [HD, NH, SEQ], early)
                    T.ml_k = sb("ml_k", [HD, NH, SEQ], early)
                    T.ml_v = sb("ml_v", [P, NT, GW], early)
                    T.ml_gates = sb("ml_gates", [P, NT, GW + 2 * NH], early)
                    T.mla_tm = sb("mla_tm", [P, NT, MLA_IN], early)
                    with ExitStack() as s:
                        T.gdn_in = sb("gdn_in", [P, 6, SEQ + CONV_W - 1], s)
                        with ExitStack() as s2:
                            T.xnT = sb("xnT", [P, KD, SEQ], s2)
                            norm_phase(nc, T, sem, "norm1", gain_columns(ins["norm1_g"], layer), False)
                            projection_phase(nc, T, sem, layer, ins["w_in"])
                        conv_phase(nc, T, sem, layer, ins["gdn_conv_w"])
                    gate_phase(nc, T, sem, layer, ins["mlstm_i_bias"], ins["mlstm_f_bias"], ins["gdn_dt_bias"],
                               ins["gdn_a_log"])
                    with ExitStack() as s:
                        T.k_cmp = sb("k_cmp", [HD, N_CMP], s)
                        T.v_cmp = sb("v_cmp", [N_CMP, HD], s)
                        T.nsa_gate = sb("nsa_gate", [P, NT, 3 * NH], s)
                        T.mla_qk = sb("mla_qk", [QD, 2 * NH, SEQ], s)
                        T.mla_v = sb("mla_v", [P, NT, NH, HD], s)
                        compress_phase(nc, T, sem, layer, ins["nsa_w_cmp_k"], ins["nsa_w_cmp_v"], ins["nsa_cmp_pos"])
                        mla_phase(nc, T, sem, layer, ins["mla_q_norm_g"], ins["mla_kv_norm_g"], ins["mla_w_uq"],
                                  ins["mla_w_ukv"])
                        attention_phase(nc, T, sem)
                    mlstm_phase(nc, T, sem, layer, ins["mlstm_norm_g"])
                gdn_phase(nc, T, sem, layer, ins["gdn_norm_g"])
                output_phase(nc, T, sem, layer, ins["w_out"])
                zero(used)
            with ExitStack() as peer:
                used = []
                sem = semaphores(peer, used)
                T.xn_r = peer.enter_context(nc.sbuf_tensor("xn2_r", [P, 2, KD, SEQ], F32R))
                norm_phase(nc, T, sem, "norm2", gain_columns(ins["norm2_g"], layer), True)
                T.pick = sb("pick", [P, 3, SEQ], peer)
                hidden_tiles = HiddenTiles(nc, T, peer, sem, layer, ins["peer_u"], hidden_dram)
                with ExitStack() as s:
                    T.peer_q = sb("peer_q", [P, 2 * PH, SEQ], s)
                    T.peer_k = sb("peer_k", [P, 2 * PH, NK], s)
                    query_phase(nc, T, sem, hidden_tiles, layer, ins["peer_w_q"], ins["peer_sub_keys"])
                    hidden_tiles.take_banks(peer)
                    select_phase(nc, T, sem, hidden_tiles)
                gate_map_phase(nc, T, sem, hidden_tiles, gates_dram)
                expert_phase(nc, T, sem, hidden_tiles, layer, ins["peer_v"], gates_dram, hidden_dram)
                zero(used)
        final_phase(nc, T, once, ins["final_norm_g"], out)


def final_phase(nc, T, sem, gain_src, out):
    with ExitStack() as ctx:
        gain = ctx.enter_context(nc.sbuf_tensor("final_gain", [P, D_MODEL], F32))
        y = ctx.enter_context(nc.sbuf_tensor("final_y", [P, NT, D_MODEL], F32))
        stat = ctx.enter_context(nc.sbuf_tensor("final_stat", [P, 4, NT], F32))
        gain_in, squares, mean_ready, root_ready = sem("f_gain_in"), sem("f_squares"), sem("f_mean"), sem("f_root")
        chain, ready, stored = sem("f_chain"), sem("f_ready"), sem("f_stored")
        block = ctx.enter_context(nc.Block())

        @block.sync
        def _(sp):
            sp.dma_start(gain[:, :], gain_src.rearrange("(a d) -> a d", a=1).to_broadcast([P, D_MODEL])).then_inc(gain_in, 16)
            for ti in range(NT):
                sp.wait_ge(ready, ti + 1)
                sp.dma_start(out[0, tok(ti), :], y[:, ti, :]).then_inc(stored, 16)
            sp.wait_ge(stored, 16 * NT)

        @block.scalar
        def _(act):
            for ti in range(NT):
                nc.scalar.activation(y[:, ti, :], T.resid[:, ti, :], ACT.Square,
                                     accum_out=stat[:, 0, ti:ti + 1]).then_inc(squares, 1)
            act.wait_ge(mean_ready, 1)
            nc.scalar.activation(stat[:, 2, :], stat[:, 1, :], ACT.Sqrt).then_inc(root_ready, 1)

        @block.vector
        def _(dve):
            link = linker(dve, chain)
            dve.wait_ge(squares, NT)
            nc.vector.tensor_scalar(stat[:, 1, :], stat[:, 0, :], 1.0 / D_MODEL, EPS,
                                    ALU.mult, ALU.add).then_inc(mean_ready, 1)
            dve.wait_ge(root_ready, 1)
            link(nc.vector.reciprocal(stat[:, 3, :], stat[:, 2, :]))
            dve.wait_ge(gain_in, 16)
            for ti in range(NT):
                nc.vector.scalar_tensor_tensor(y[:, ti, :], T.resid[:, ti, :], stat[:, 3, ti:ti + 1], gain[:, :],
                                               ALU.mult, ALU.mult).then_inc(ready, 1)


def kernel(**inputs):
    import numpy as _np
    import concourse.bacc as _bacc
    from concourse import mybir as _mybir
    from concourse.bass_utils import run_bass_kernel_spmd as _run

    nc = _bacc.Bacc("TRN2", target_bir_lowering=False, num_devices=1)
    arrays, ins = {}, {}
    for name in _INS:
        a = _np.ascontiguousarray(inputs[name])
        arrays[f"in_{name}"] = a
        ins[name] = nc.dram_tensor(f"in_{name}", a.shape, _mybir.dt.from_np(a.dtype), kind="ExternalInput").ap()
    c = shape_constants()
    arrays["shape_constants"] = c
    consts = nc.dram_tensor("shape_constants", c.shape, _mybir.dt.float32, kind="ExternalInput").ap()
    out = nc.dram_tensor("out", (1, SEQ, D_MODEL), _mybir.dt.float32, kind="ExternalOutput").ap()
    program(nc, ins, consts, out)
    r = _run(nc, [arrays], core_ids=[0])
    return r.results[0]["out"]
```
